# Optimizing a Trainium2 kernel written in Bass

```python
import math
import jax
import jax.numpy as jnp
from jax import lax
import numpy as np

D_MODEL = 2048
BATCH = 1
SEQ = 256
DEPTH = 1
DEC_BATCH = 8
DEC_SEQ = 4
PAST_LEN = 2048
PAGE_SIZE = 128

HG_HEADS = 16
HG_DK = 128
HG_DV = 128
HG_CHUNK = 32
GDN_QK_HEADS = 16
GDN_V_HEADS = 32
GDN_DK = 128
GDN_DV = 128
GDN_CHUNK = 64
CONV_W = 4
D_FF = 4 * D_MODEL
NORM_EPS = 1e-6

HG_W = HG_HEADS * HG_DK
HG_VW = HG_HEADS * HG_DV
GDN_QK_W = GDN_QK_HEADS * GDN_DK
GDN_V_W = GDN_V_HEADS * GDN_DV
CONV_CH = 2 * GDN_QK_W + GDN_V_W
GDN_SCALE = GDN_DK ** -0.5
IN_SPLITS = (HG_W, HG_W, HG_VW, HG_VW, GDN_QK_W, GDN_QK_W, GDN_V_W, GDN_V_W, GDN_V_HEADS, GDN_V_HEADS, D_MODEL, D_MODEL)
N_IN = 4 * HG_W + 2 * GDN_QK_W + 2 * GDN_V_W + 2 * GDN_V_HEADS + 2 * D_MODEL

kernel_name = "hybrid_hgrn2_gdn_decoder_step"

def rmsnorm(x, g):
    x32 = x.astype(jnp.float32)
    return x32 * lax.rsqrt(jnp.mean(x32 * x32, axis=-1, keepdims=True) + NORM_EPS) * g.astype(jnp.float32)

def l2norm(x):
    return x * lax.rsqrt(jnp.sum(x * x, axis=-1, keepdims=True) + NORM_EPS)

def to_chunks(x, C, n):
    B, T = x.shape[0], x.shape[1]
    x = jnp.pad(x, [(0, 0), (0, n * C - T)] + [(0, 0)] * (x.ndim - 2))
    x = x.reshape((B, n, C) + x.shape[2:])
    return jnp.moveaxis(x, (1, 3), (0, 2))

def from_chunks(x, T):
    n, B, H, C, D = x.shape
    x = jnp.moveaxis(x, (0, 2), (1, 3)).reshape(B, n * C, H, D)
    return x[:, :T]

def hgrn2_scan(q, f, inp, S0):
    T = q.shape[1]
    C = min(HG_CHUNK, T)
    n = -(-T // C)
    log_f = jnp.log(f)
    k = 1.0 - f
    qc, gc, kc, ic = [to_chunks(a, C, n) for a in (q, log_f, k, inp)]
    causal = jnp.tril(jnp.ones((C, C), dtype=bool))
    ref = C // 2

    def step(S, xs):
        q_, g_, k_, i_ = xs
        G = jnp.cumsum(g_, axis=2)
        G_ref = G[:, :, ref:ref + 1]
        G_last = G[:, :, C - 1:C]
        A = jnp.einsum('bhtd,bhsd->bhts', q_ * jnp.exp(G - G_ref), k_ * jnp.exp(G_ref - G))
        A = jnp.where(causal, A, 0.0)
        o = (jnp.einsum('bhts,bhsv->bhtv', A, i_)
             + jnp.einsum('bhtd,bhdv->bhtv', q_ * jnp.exp(G), S))
        S = (jnp.exp(G_last[:, :, 0])[..., None] * S
             + jnp.einsum('bhsd,bhsv->bhdv', k_ * jnp.exp(G_last - G), i_))
        return S, o

    S, o = lax.scan(step, S0, (qc, gc, kc, ic))
    return from_chunks(o, T), S

def gdn_scan(q, k, v, log_a, beta, S0):
    T = q.shape[1]
    C = min(GDN_CHUNK, T)
    n = -(-T // C)
    qc, kc, vc, gc, bc = [to_chunks(a, C, n) for a in (q, k, v, log_a, beta)]
    incl = jnp.tril(jnp.ones((C, C), dtype=bool))
    strict = jnp.tril(jnp.ones((C, C), dtype=bool), -1)
    eye = jnp.eye(C, dtype=jnp.float32)

    def step(S, xs):
        q_, k_, v_, g_, b_ = xs
        gam = jnp.cumsum(g_, axis=-1)
        L = jnp.exp(jnp.where(incl, gam[..., :, None] - gam[..., None, :], -jnp.inf))
        kb = k_ * b_[..., None]
        A = jnp.where(strict, jnp.einsum('bhtd,bhsd->bhts', kb, k_) * L, 0.0)
        rhs = jnp.concatenate([v_ * b_[..., None], kb * jnp.exp(gam)[..., None]], axis=-1)
        X = lax.linalg.triangular_solve(A + eye, rhs, left_side=True, lower=True, unit_diagonal=True)
        u, w = X[..., :GDN_DV], X[..., GDN_DV:]
        v_new = u - jnp.einsum('bhtd,bhdv->bhtv', w, S)
        attn = jnp.einsum('bhtd,bhsd->bhts', q_, k_) * L
        o = (jnp.einsum('bhtd,bhdv->bhtv', q_ * jnp.exp(gam)[..., None], S)
             + jnp.einsum('bhts,bhsv->bhtv', attn, v_new))
        g_last = gam[..., C - 1:C]
        S = (jnp.exp(g_last)[..., None] * S
             + jnp.einsum('bhsd,bhsv->bhdv', k_ * jnp.exp(g_last - gam)[..., None], v_new))
        return S, o

    S, o = lax.scan(step, S0, (qc, kc, vc, gc, bc))
    return from_chunks(o, T), S

def token_mixer(a, conv_buf, s_hg, s_gdn, lb, w_in, conv_w, A_log, dt_bias,
                hg_norm_g, gdn_norm_g, w_out_hg, w_out_gdn, w_o):
    B, T, _ = a.shape
    f32 = jnp.float32
    proj = jnp.matmul(a, w_in).astype(f32)
    offsets = [int(o) for o in np.cumsum(IN_SPLITS)[:-1]]
    hq, hf, hi, hg, gq, gk, gv, gz, gb, ga, gate_a, gate_b = jnp.split(proj, offsets, axis=-1)

    q_h = jax.nn.silu(hq).reshape(B, T, HG_HEADS, HG_DK)
    f_h = (lb + (1.0 - lb) * jax.nn.sigmoid(hf)).reshape(B, T, HG_HEADS, HG_DK)
    i_h = hi.reshape(B, T, HG_HEADS, HG_DV)
    o_hg, s_hg_new = hgrn2_scan(q_h, f_h, i_h, s_hg.astype(f32))
    o_hg = (rmsnorm(o_hg, hg_norm_g) * jax.nn.silu(hg.reshape(B, T, HG_HEADS, HG_DV))).reshape(B, T, HG_VW)

    u = jnp.concatenate([gq, gk, gv], axis=-1)
    ucat = jnp.concatenate([conv_buf.astype(f32), u], axis=1)
    cw = conv_w.astype(f32)
    conv = cw[0] * ucat[:, 0:T]
    for j in range(1, CONV_W):
        conv = conv + cw[j] * ucat[:, j:j + T]
    conv_buf_new = ucat[:, T:]
    conv = jax.nn.silu(conv)
    cq, ck, cv = jnp.split(conv, [GDN_QK_W, 2 * GDN_QK_W], axis=-1)
    rep = GDN_V_HEADS // GDN_QK_HEADS
    q_g = jnp.repeat(l2norm(cq.reshape(B, T, GDN_QK_HEADS, GDN_DK)), rep, axis=2) * GDN_SCALE
    k_g = jnp.repeat(l2norm(ck.reshape(B, T, GDN_QK_HEADS, GDN_DK)), rep, axis=2)
    v_g = cv.reshape(B, T, GDN_V_HEADS, GDN_DV)
    beta = jax.nn.sigmoid(gb)
    log_a = -jnp.exp(A_log.astype(f32)) * jax.nn.softplus(ga + dt_bias.astype(f32))
    o_gdn, s_gdn_new = gdn_scan(q_g, k_g, v_g, log_a, beta, s_gdn.astype(f32))
    o_gdn = (rmsnorm(o_gdn, gdn_norm_g) * jax.nn.silu(gz.reshape(B, T, GDN_V_HEADS, GDN_DV))).reshape(B, T, GDN_V_W)

    merged = (jax.nn.sigmoid(gate_a) * jnp.matmul(o_hg, w_out_hg)
              + jax.nn.sigmoid(gate_b) * jnp.matmul(o_gdn, w_out_gdn))
    return jnp.matmul(merged, w_o), conv_buf_new, s_hg_new, s_gdn_new

def run_trunk(x, c, conv_buf, st_hg, st_gdn, lb_logits, w_ada, b_ada, norm_g, w_in, conv_w,
              A_log, dt_bias, hg_norm_g, gdn_norm_g, w_out_hg, w_out_gdn, w_o, w_up, w_down):
    f32 = jnp.float32
    lbs = jnp.cumsum(jax.nn.softmax(lb_logits.astype(f32), axis=0), axis=0)
    h = x.astype(f32)
    cs = jax.nn.silu(c.astype(f32))
    new_conv, new_hg, new_gdn = [], [], []
    for l in range(DEPTH):
        mod = jnp.matmul(cs, w_ada[l]) + b_ada[l]
        sh1, sc1, g1, sh2, sc2, g2 = [m[:, None, :] for m in jnp.split(mod, 6, axis=-1)]
        a = rmsnorm(h, norm_g[l, 0]) * (1.0 + sc1) + sh1
        mix, cb, shg, sgd = token_mixer(a, conv_buf[l], st_hg[l], st_gdn[l], lbs[l], w_in[l], conv_w[l],
                                        A_log[l], dt_bias[l], hg_norm_g[l], gdn_norm_g[l],
                                        w_out_hg[l], w_out_gdn[l], w_o[l])
        h = h + g1 * rmsnorm(mix, norm_g[l, 1])
        a = rmsnorm(h, norm_g[l, 2]) * (1.0 + sc2) + sh2
        ff = jnp.matmul(jnp.square(jax.nn.relu(jnp.matmul(a, w_up[l]))), w_down[l])
        h = h + g2 * rmsnorm(ff, norm_g[l, 3])
        new_conv.append(cb)
        new_hg.append(shg)
        new_gdn.append(sgd)
    return h.astype(x.dtype), jnp.stack(new_conv), jnp.stack(new_hg), jnp.stack(new_gdn)

def setup_inputs(seed: int = 0) -> dict:
    key = jax.random.key(seed)
    ks = jax.random.split(key, 24)
    f32 = jnp.float32

    def nrm(k, shape, scale):
        return jax.random.normal(k, shape, f32) * scale

    dt = jnp.exp(jax.random.uniform(ks[14], (DEPTH, GDN_V_HEADS), f32, math.log(1e-3), math.log(1e-1)))
    return {
        "x_prompt": nrm(ks[0], (BATCH, SEQ, D_MODEL), 1.0),
        "x_sample": nrm(ks[1], (DEC_BATCH, DEC_SEQ, D_MODEL), 1.0),
        "state_hgrn": nrm(ks[2], (DEPTH, DEC_BATCH, HG_HEADS, HG_DK, HG_DV), 0.5),
        "state_gdn": nrm(ks[3], (DEPTH, DEC_BATCH, GDN_V_HEADS, GDN_DK, GDN_DV), 0.1),
        "cache_conv": nrm(ks[4], (DEPTH, DEC_BATCH, CONV_W - 1, CONV_CH), 1.0),
        "c_prompt": nrm(ks[5], (BATCH, D_MODEL), 1.0),
        "c_sample": nrm(ks[6], (DEC_BATCH, D_MODEL), 1.0),
        "lb_logits": nrm(ks[7], (DEPTH + 1, HG_W), 0.1),
        "w_ada": nrm(ks[8], (DEPTH, D_MODEL, 6 * D_MODEL), 0.5 * D_MODEL ** -0.5),
        "b_ada": nrm(ks[9], (DEPTH, 6 * D_MODEL), 0.02),
        "norm_g": 1.0 + nrm(ks[10], (DEPTH, 4, D_MODEL), 0.02),
        "w_in": nrm(ks[11], (DEPTH, D_MODEL, N_IN), D_MODEL ** -0.5),
        "conv_w": nrm(ks[12], (DEPTH, CONV_W, CONV_CH), CONV_W ** -0.5),
        "A_log": jnp.log(jax.random.uniform(ks[13], (DEPTH, GDN_V_HEADS), f32, 1.0, 16.0)),
        "dt_bias": dt + jnp.log(-jnp.expm1(-dt)),
        "hg_norm_g": 1.0 + nrm(ks[15], (DEPTH, HG_DV), 0.02),
        "gdn_norm_g": 1.0 + nrm(ks[16], (DEPTH, GDN_DV), 0.02),
        "w_out_hg": nrm(ks[17], (DEPTH, HG_VW, D_MODEL), HG_VW ** -0.5),
        "w_out_gdn": nrm(ks[18], (DEPTH, GDN_V_W, D_MODEL), GDN_V_W ** -0.5),
        "w_o": nrm(ks[19], (DEPTH, D_MODEL, D_MODEL), D_MODEL ** -0.5),
        "w_up": nrm(ks[20], (DEPTH, D_MODEL, D_FF), D_MODEL ** -0.5),
        "w_down": nrm(ks[21], (DEPTH, D_FF, D_MODEL), D_FF ** -0.5),
    }

def reference(x_prompt, x_sample, state_hgrn, state_gdn, cache_conv, c_prompt, c_sample,
              lb_logits, w_ada, b_ada, norm_g, w_in, conv_w, A_log, dt_bias, hg_norm_g, gdn_norm_g,
              w_out_hg, w_out_gdn, w_o, w_up, w_down):
    sdt = state_hgrn.dtype
    zero_conv = jnp.zeros((DEPTH, BATCH, CONV_W - 1, CONV_CH), cache_conv.dtype)
    zero_hg = jnp.zeros((DEPTH, BATCH, HG_HEADS, HG_DK, HG_DV), sdt)
    zero_gdn = jnp.zeros((DEPTH, BATCH, GDN_V_HEADS, GDN_DK, GDN_DV), state_gdn.dtype)
    y_prompt, conv_p, hg_p, gdn_p = run_trunk(
        x_prompt, c_prompt, zero_conv, zero_hg, zero_gdn, lb_logits, w_ada, b_ada, norm_g, w_in, conv_w,
        A_log, dt_bias, hg_norm_g, gdn_norm_g, w_out_hg, w_out_gdn, w_o, w_up, w_down)
    y_sample, conv_s, hg_s, gdn_s = run_trunk(
        x_sample, c_sample, cache_conv, state_hgrn, state_gdn, lb_logits, w_ada, b_ada, norm_g, w_in, conv_w,
        A_log, dt_bias, hg_norm_g, gdn_norm_g, w_out_hg, w_out_gdn, w_o, w_up, w_down)
    return (y_prompt, y_sample,
            hg_p.astype(sdt), gdn_p.astype(state_gdn.dtype), conv_p.astype(cache_conv.dtype),
            hg_s.astype(sdt), gdn_s.astype(state_gdn.dtype), conv_s.astype(cache_conv.dtype))


_drawn_inputs = setup_inputs


def setup_inputs(seed=0):
    import zlib

    import numpy as np

    out = dict(_drawn_inputs(seed))
    spreads = {}
    factors = {}
    for name, (base, spread) in spreads.items():
        noise = np.random.default_rng([zlib.crc32(name.encode()), seed]).standard_normal(out[name].shape)
        drawn = base * np.exp(spread * noise) if base else spread * noise
        out[name] = jnp.asarray(drawn.astype(out[name].dtype))
    for name, factor in factors.items():
        out[name] = (out[name] * factor).astype(out[name].dtype)
    return out
```

```python
from contextlib import ExitStack

import concourse.bass as bass
from concourse import mybir

F32 = mybir.dt.float32
F32R = mybir.dt.float32r
ALU = mybir.AluOpType
ACT = mybir.ActivationFunctionType
TABLE_SET = "natural_log_exp_and_others"

P = 128
RAW = 8
SPLIT = 4
PK = 4
AHEAD = 2
EPS = 1e-6

SIGNALS = (
    "rows_zeroed rows_in small_in x_in const_step consts_made vec_turned vec_made c_turned c_exp cs_made "
    "x_rs x_scaled x_turned a_tmp a_hi a_lo ada_used ada_free pro_dve pro_act "
    "lb_diff lb_exp beta_exp soft_exp soft_den soft_ln bg_made bg_turned bg_taken chunk_sums "
    "chunk_exp tab_made "
    "hi_made lo_made piece_used acc_free0 acc_free1 "
    "h_qexp h_qden h_qrec h_sc h_fden h_frec h_f h_k h_ln h_scan h_diff h_e h_decayed h_decayed_p "
    "h_gexp h_gden h_grec h_turned h_at h_tok h_spread h_ds h_step h_s0 h_new h_o h_sq h_ss h_ssln h_rs "
    "h_t1 h_out h_ohi h_olo h_stored "
    "g_zero g_cc g_halo_turned g_halo g_tap g_cexp g_c g_tail g_tail_turned g_tail_out "
    "g_tail_stored g_turned g_qk_turned "
    "g_attn g_lev g_t1 g_pu g_pucp g_ut g_unew g_tnew g_w g_vn g_ds g_st g_ws "
    "g_qw g_sw g_qws g_vtt g_vns g_vx g_dss g_s0 g_sdec g_snew g_o g_osq g_oss g_ossln "
    "g_ors g_ohi g_olo g_zexp g_z g_stored g_stored_s "
    "t_den t_out t_stored0 t_stored1 t_in0 t_in1 t_s2 t_s3 m_hi m_lo w_sum w_ss w_ln w_rs w_h w_hsq "
    "w_xin0 w_xin1 w_clear w_t2 w_xturned b_lo b_hi y_turned y_out y_stored"
).split()
COUNTS_ON = {
    "g_d": "h_turned", "g_kk": "h_ds", "g_l1": "h_ss", "g_uts": "h_o", "g_ss": "h_qexp", "g_ssln": "h_ln",
    "g_rs": "h_gexp", "g_qkt": "h_tok", "g_qpt": "h_sq", "g_ex": "h_ssln", "g_wcp": "h_rs", "g_ocp": "h_e",
    "g_cw": "h_qden", "g_part": "h_qrec", "g_cden": "h_gden", "g_crec": "h_grec", "g_zden": "h_fden",
    "g_zrec": "h_frec", "g_sc": "h_sc", "g_tokv": "h_f", "g_tokqk": "h_k", "g_a": "h_scan", "g_qkm": "h_diff",
    "g_u1": "h_decayed", "g_oadd": "h_at", "g_ot1": "h_t1", "g_out": "h_out", "g_gr": "h_spread",
    "g_tokd": "h_decayed_p", "g_vt": "h_olo", "f_hi": "m_hi", "f_lo": "m_lo", "w_t1": "t_s3", "b_tmp": "t_s2",
    "f_sq": "b_lo",
}
EARLIER = 16



def atleast0(count):
    return max(count, 0) if isinstance(count, int) else count


class At:

    def __init__(self, slab, n=0, slabs=0):
        self.slab0, self.n, self.slabs = slab, n, slabs
        self.piece0, self.pieces = 4 * slab, 4 * slabs

    def pieces_before(self, k):
        return self.piece0 + k + self.n * self.pieces

    def slot(self, k, ring):
        return (self.piece0 + k) % ring

    def loads_done(self, k):
        return 16 * ((self.piece0 + k) // RAW + 1) + self.n * (16 * self.pieces // RAW)

    def bank(self, slab):
        return (self.slab0 + slab) % 2

    def drained(self, slab):
        return (self.slab0 + slab) // 2 + self.n * (self.slabs // 2)


def hybrid_layer(nc, x_prompt, x_sample, state_hgrn, state_gdn, cache_conv, c_prompt, c_sample, lb_logits,
                 w_ada, b_ada, norm_g, w_in, conv_w, A_log, dt_bias, hg_norm_g, gdn_norm_g,
                 w_out_hg, w_out_gdn, w_o, w_up, w_down,
                 y_prompt, y_sample, hg_prompt, gdn_prompt, conv_prompt, hg_sample, gdn_sample, conv_sample):
    TP, D = x_prompt.shape[1:]
    NB, TS = x_sample.shape[:2]
    NS = NB * TS
    T = TP + NS
    KT = D // P
    HH = state_hgrn.shape[2]
    GH = state_gdn.shape[2]
    GJ = GH // 2
    HC, GC = 32, 64
    NHC, NGC = TP // HC, TP // GC
    LEV = 6
    QSCALE = P ** -0.5
    F = w_up.shape[2]
    FG = F // D
    NC = 1 + NB
    assert (TP, NB, TS, KT, HH, GJ) == (256, 8, 4, 16, 16, 16) and 1 << LEV == GC

    OQ, OF, OI, OG = 0, D, 2 * D, 3 * D
    GQ = 4 * D
    GK = GQ + GJ * P
    GV = GK + GJ * P
    GZ = GV + GH * P
    GB = GZ + GH * P
    GATE_A = GB + 2 * GH
    GATE_B = GATE_A + D

    def by_k(w):
        return w[0].rearrange("(k p) n -> p k n", p=P)

    win, wada, whg, wgdn, wo, wup, wdown = (by_k(w) for w in (w_in, w_ada, w_out_hg, w_out_gdn, w_o, w_up, w_down))
    merged_d = nc.dram_tensor("merged_scratch", (KT, P, T), F32, kind="Internal").ap()
    gate_d = nc.dram_tensor("gate_scratch", (KT, P, T), F32, kind="Internal").ap()
    half_d = nc.dram_tensor("half_scratch", (KT, P, T), F32, kind="Internal").ap()

    S_BG = 0
    S_H0 = 1
    S_H1 = S_H0 + 4
    S_GA0 = S_H1 + 4 * (HH - 1)
    S_GA1 = S_GA0 + 4
    S_WA = S_GA1 + KT - 4
    S_G0 = S_WA + KT
    S_G1 = S_G0 + 6
    HALF = GJ // 2
    S_WB1 = S_G1 + 6 * HALF
    S_G2 = S_WB1 + KT
    S_GB0 = S_G2 + 6 * (GJ - 1 - HALF)
    S_GB1 = S_GB0 + 6
    S_WB2 = S_GB1 + KT - 6
    S_WO = S_WB2 + KT
    S_FF = S_WO + KT
    S_END = S_FF + 2 * KT * FG
    ADA_HALVES = 2 * 6 * KT
    ADA_LOADS = 16 * ADA_HALVES // (RAW // 2)

    with ExitStack() as ctx:
        def scoped(stack):
            def sb(name, shape, dt=F32):
                return stack.enter_context(nc.sbuf_tensor(name, shape, dt))
            return sb

        sb = scoped(ctx)
        sg = {n: ctx.enter_context(nc.semaphore(n)) for n in SIGNALS}
        sg.update({later: sg[earlier] for later, earlier in COUNTS_ON.items()})
        assert EARLIER == HH == KT
        raw_in = [ctx.enter_context(nc.semaphore(f"raw_in{i}")) for i in range(RAW // 2)]

        raw = sb("raw", [P, RAW, PK, P])
        whi = sb("whi", [P, SPLIT, PK, P], F32R)
        wlo = sb("wlo", [P, SPLIT, PK, P], F32R)
        ahi = sb("ahi", [P, KT, T], F32R)
        alo = sb("alo", [P, KT, T], F32R)
        ohi = sb("ohi", [P, KT, T], F32R)
        olo = sb("olo", [P, KT, T], F32R)
        vec = sb("vec", [P, 4, P])
        mod = sb("mod", [P, 6 * KT, NC])
        ident = sb("ident", [P, P])
        ones = sb("ones", [P, P])
        smask = sb("smask", [NS, NS])
        cm4 = sb("cm4", [NS, NB])
        cm64 = sb("cm64", [P, 2])
        m_incl = sb("m_incl", [P, P])
        m_str = sb("m_str", [P, P])
        m_str_s = sb("m_str_s", [NS, NS])
        levm = sb("levm", [P, LEV, P])
        eps = sb("eps", [P, 1])
        pa = sb("pa", [P, 2, T])
        pb = sb("pb", [P, 2, T])
        tab = sb("tab", [P, GH, 27])

        with ExitStack() as front:
            sb = scoped(front)
            hmask = sb("hmask", [P, P])
            reset = sb("reset", [P, T])
            cm32 = sb("cm32", [P, P // HC])
            lbt = sb("lbt", [P, HH, 2])
            with ExitStack() as part:
                sb = scoped(part)
                xtok = sb("xtok", [P, 2, D])
                xs = sb("xs", [NS, D])
                xjunk = sb("xjunk", [P, D])
                rows = sb("rows", [P, 4, P])
                crow = sb("crow", [P, 2, P])
                ce = sb("ce", [P, 3, 16 + P])
                cst = sb("cst", [P, KT, NC])
                xss = sb("xss", [P, 3, 3])
                lbx = sb("lbx", [P, 6, HH])
                atmp = sb("atmp", [P, 2, T])
                bg = sb("bg", [2 * GH, 5, T])
                bgc = sb("bgc", [2 * GH, 3])
                bgT = sb("bgT", [P, 3, 2 * GH])
                gx = sb("gx", [P, 2, 2, GH])
                gxs = sb("gxs", [NS, NB, GH])
                bgs = sb("bgs", [P, 576])
            with ExitStack() as part:
                sb = scoped(part)
                hq, hf, hk, hlf, hG, hi_, he, hden, hsg, hse = (sb(f"h_{n}", [P, T]) for n in
                                                                ("q", "f", "k", "lf", "G", "i", "e", "den", "sg", "se"))
                hsq, hrs, ht1, hof = (sb(f"h_{n}", [P, T]) for n in ("sq", "rs", "t1", "of"))
                hD = sb("h_D", [P, 2, T])
                hE = sb("h_E", [P, 4, T])
                hX = sb("h_X", [P, 4, T])
                htok = sb("h_tok", [P, 4, P])
                htoks = sb("h_toks", [NS, 2, P])
                hAT = sb("h_AT", [P, T])
                hiX = sb("h_iX", [P, 2, 4, P])
                hiXs = sb("h_iXs", [NS, NB, P])
                hS = sb("h_S", [P, NHC, P])
                hS0 = sb("h_S0", [P, NB, P])
                hSn = sb("h_Sn", [P, NB, P])
                hsc = sb("h_sc", [P, 2])
        UW = 3 + TP + NB * (3 + TS)
        CW = UW - 3
        with ExitStack() as part:
            sb = scoped(part)
            gU = sb("g_U", [P, 4, UW])
            gca = sb("g_ca", [P, UW])
            gce = sb("g_ce", [P, UW])
            gC = sb("g_C", [P, 4, T])
            gz = sb("g_z", [P, 2, T])
            gcc = sb("g_cc", [24, 4, P])
            gtail = sb("g_tail", [P, 4, 27])
            gtq = sb("g_tq", [P, 3, P])
            gtk = sb("g_tk", [P, 3, P])
            gbv = sb("g_bv", [P, 3, 2, P])
            gbek = sb("g_bek", [P, 3, 2, P])
            gkl = sb("g_kl", [P, 3, 2, P])
            gqp = sb("g_qp", [P, 3, 2, P])
            gvn = gqp
            gqT = sb("g_qT", [P, T])
            gkT = sb("g_kT", [P, T])
            gqpT = sb("g_qpT", [P, 2, TP])
            gGR = sb("g_GR", [P, 2, 2, 2, P])
            gGRs = sb("g_GRs", [NS, 2, 2, NS])
            gA = sb("g_A", [P, 4, P])
            gAs = sb("g_As", [NS, 2, NS])
            glev = sb("g_lev", [P, 2, 4, P])
            glevs = sb("g_levs", [NS, 2, 2, NS])
            gQKm = sb("g_QKm", [P, 2, P])
            gQKms = sb("g_QKms", [NS, NS])
            gat = sb("g_at", [P, 2, 2, P])
            gats = sb("g_ats", [NS, 2, NS])
            gT = sb("g_T", [P, 4, P])
            gUi = sb("g_Ui", [P, 4, P])
            gTs = sb("g_Ts", [NS, 2, NS])
            gUs = sb("g_Us", [NS, 2, NS])
            gPU = sb("g_PU", [P, 4, P])
            gPUs = sb("g_PUs", [NS, 2, NS])
            gQW = sb("g_QW", [P, 2, NB, 2, TS])
            gqws = sb("g_qws", [P, 2, NB, 2, TS])
            guTs = sb("g_uTs", [P, 2, NS])
            gvns = sb("g_vns", [NS, 2, P])
            gvX = sb("g_vX", [NS, NB, P])
            gS = sb("g_S", [P, 4, 2, P])
            gS0 = sb("g_S0", [P, 2, NB, P])
            go = sb("g_o", [P, 2, T])
            gn1 = sb("g_n1", [P, 2, T])
            gn2 = sb("g_n2", [P, 2, T])
            gjunk = sb("g_junk", [P, P])
            gto = sb("g_to", [27, 4, P])
            gsc = sb("g_sc", [P, 2, 27])
            gcw = sb("g_cw", [P, 4, 4])
            gss = sb("g_ss", [P, 3, 3, 2])
        with ExitStack() as part:
            sb = scoped(part)
            mix = sb("mix", [P, KT, T])
            tt = sb("tt", [P, 2, T])
            tu = sb("tu", [P, 2, T])
            tin = sb("tin", [P, 2, 3, T])
            tsum = sb("tsum", [P, T])
            tsum2 = sb("tsum2", [P, T])
            trs = sb("trs", [P, T])
            ytok = sb("ytok", [P, 2, 3, P])
            xrow = sb("xrow", [P, 2, 3, P])
            with ExitStack() as merged:
                sb = scoped(merged)
                mhi = sb("mhi", [P, KT, T], F32R)
                mlo = sb("mlo", [P, KT, T], F32R)
            res = scoped(part)("res", [P, KT, T])

        acc = [ctx.enter_context(nc.psum_tensor(f"acc{i}", [P, 512], F32)) for i in range(2)]
        R = {b: ctx.enter_context(nc.psum_tensor(f"bank{b}", [P, 512], F32)) for b in range(2, 8)}
        block = ctx.enter_context(nc.Block())

        def halves(ap):
            return ap[:, 0:TP], ap[:, TP:T].rearrange("p (b t) -> p b t", t=TS)

        def loop(eng, body, slab, slabs, count, apart=0):
            for n in range(apart):
                body(At(slab, n, slabs), n)
            with eng.Fori(apart, count) as n:
                body(At(slab, n, slabs), n)

        def repeat(eng, body, count):
            body(0)
            with eng.Fori(1, count) as n:
                body(n)

        ada_bias = vec[:, 1, :]
        taps = vec[:, 2:4, :].rearrange("p a (c b) -> p (a c) b", b=2 * GJ + GH)
        TAIL = UW - NB * (3 + TS)

        @block.sync
        def _(sp):
            sp.wait_ge(sg["rows_zeroed"], 1)
            sp.dma_start(rows[0:4 * KT, 0, :], norm_g[0].rearrange("g (k p) -> (g k) p", p=P)).then_inc(sg["rows_in"], 16)
            sp.dma_start(rows[4 * KT:6 * KT, 0, :], lb_logits.rearrange("g (k p) -> (g k) p", p=P)).then_inc(sg["rows_in"], 16)
            sp.dma_start(rows[6 * KT:6 * KT + 1, 0, :], hg_norm_g).then_inc(sg["rows_in"], 16)
            sp.dma_start(rows[6 * KT + 1:6 * KT + 2, 0, :], gdn_norm_g).then_inc(sg["rows_in"], 16)
            sp.dma_start(rows[0:6 * KT, 1, :], b_ada.rearrange("o (k p) -> (o k) p", p=P)).then_inc(sg["rows_in"], 16)
            for a in range(2):
                sp.dma_start(rows[:, 2 + a, :], conv_w[0, 2 * a:2 * a + 2, :].rearrange("c (k p) -> (c k) p", p=P)).then_inc(sg["rows_in"], 16)
            sp.dma_start(crow[0:KT, 0, :], c_prompt.rearrange("o (k p) -> (o k) p", p=P)).then_inc(sg["rows_in"], 16)
            sp.dma_start(crow[:, 1, :], c_sample.rearrange("b (k p) -> (b k) p", p=P)).then_inc(sg["rows_in"], 16)
            for a in range(2):
                sp.dma_start(xtok[:, a, :], x_prompt[0, a * P:(a + 1) * P, :]).then_inc(sg["x_in"], 16)
            sp.dma_start(xs[:, :], x_sample.rearrange("b t d -> (b t) d")).then_inc(sg["x_in"], 16)

            def ada(n, first):
                for h in range(4):
                    if not first:
                        sp.wait_ge(sg["ada_used"], 4 * n + h - 3)
                    col = (2 * n + h // 2) * P
                    src = wada[:, 8 * (h % 2):8 * (h % 2) + 8, bass.ds(col, P)]
                    sp.dma_start(raw[:, 2 * h:2 * h + 2].rearrange("p a k c -> p (a k) c"), src).then_inc(raw_in[h], 16)
            ada(0, True)
            with sp.Fori(1, 3 * KT) as n:
                ada(n, False)

            def slab(at, k, weights, row, col):
                for h in range(2):
                    piece = 4 * k + 2 * h
                    free = at.pieces_before(piece) - 6
                    if isinstance(free, int) and free <= 0:
                        sp.wait_ge(sg["ada_used"], ADA_HALVES)
                    else:
                        sp.wait_ge(sg["lo_made"], free)
                    s = at.slot(piece, RAW)
                    k0 = row + 8 * h
                    sp.dma_start(raw[:, s:s + 2].rearrange("p a k c -> p (a k) c"),
                                 weights[:, bass.ds(k0, 8) if not isinstance(k0, int) else slice(k0, k0 + 8),
                                         bass.ds(col, P)]).then_inc(raw_in[s // 2], 16)

            def hgrn(at, i):
                for k, off in enumerate((OQ, OF, OI, OG)):
                    slab(at, k, win, 0, off + i * P)

            def gdn(at, j):
                for k, col in enumerate((GQ + j * P, GK + j * P, GV + j * (2 * P), GV + P + j * (2 * P),
                                         GZ + j * (2 * P), GZ + P + j * (2 * P))):
                    slab(at, k, win, 0, col)

            def pair(weights, row, off):
                def body(at, n):
                    for k in range(2):
                        slab(at, k, weights, row, off + k * P + n * (2 * P))
                return body

            slab(At(S_BG), 0, win, 0, GB)
            hgrn(At(S_H0), 0)
            loop(sp, lambda at, n: hgrn(at, n + 1), S_H1, 4, HH - 1)
            for k in range(4):
                slab(At(S_GA0), k, win, 0, GATE_A + k * P)
            loop(sp, pair(win, 0, GATE_A + 4 * P), S_GA1, 2, (KT - 4) // 2)
            loop(sp, pair(whg, 0, 0), S_WA, 2, KT // 2)
            gdn(At(S_G0), 0)
            loop(sp, lambda at, n: gdn(at, n + 1), S_G1, 6, HALF)
            loop(sp, pair(wgdn, 0, 0), S_WB1, 2, KT // 2)
            loop(sp, lambda at, n: gdn(at, n + 1 + HALF), S_G2, 6, GJ - 1 - HALF)
            for k in range(6):
                slab(At(S_GB0), k, win, 0, GATE_B + k * P)
            loop(sp, pair(win, 0, GATE_B + 6 * P), S_GB1, 2, (KT - 6) // 2)
            loop(sp, pair(wgdn, KT, 0), S_WB2, 2, KT // 2)
            loop(sp, pair(wo, 0, 0), S_WO, 2, KT // 2)
            with sp.Fori(0, FG) as g:
                with sp.Fori(0, KT // 2) as n:
                    at = At(S_FF, n + g * KT, 2)
                    for k in range(2):
                        slab(at, k, wup, 0, g * D + n * (2 * P) + k * P)
                with sp.Fori(0, KT // 2) as n:
                    at = At(S_FF, n + g * KT + KT // 2, 2)
                    for k in range(2):
                        slab(at, k, wdown, g * KT, n * (2 * P) + k * P)
            at = At(S_END)
            sp.wait_ge(sg["lo_made"], at.pieces_before(0) - 6)
            sp.dma_start(raw[:, at.slot(0, RAW):at.slot(0, RAW) + 2].rearrange("p a k c -> p (a k) c"),
                         wo[:, 0:8, 0:P]).then_inc(raw_in[at.slot(0, RAW) // 2], 16)
            def store_y(n):
                for k in range(2):
                    sp.wait_ge(sg["y_out"], 2 * n + k + 1)
                    col = bass.ds(n * (2 * P) + k * P, P)
                    sp.dma_start(y_prompt[0].rearrange("(a p) d -> p a d", p=P)[:, :, col], ytok[:, k, 0:2, :]).then_inc(sg["y_stored"], 16)
                    sp.dma_start(y_sample.rearrange("b t d -> (b t) d")[:, col], ytok[0:NS, k, 2, :]).then_inc(sg["y_stored"], 16)
            with sp.Fori(0, KT // 2) as n:
                store_y(n)
            sp.wait_ge(sg["y_stored"], 32 * KT)
            sp.wait_ge(sg["h_stored"], 32 * HH)
            sp.wait_ge(sg["g_stored"], 16 * GJ)
            sp.wait_ge(sg["g_stored_s"], 32 * GJ)
            sp.wait_ge(sg["g_tail_stored"], 96 * GJ)

        M_WA, M_WB1, M_GB, M_WB2 = KT, 2 * KT, 3 * KT, 4 * KT

        @block.tensor
        def _(pe):
            mm, turn = nc.tensor.matmul, nc.tensor.transpose

            pe.wait_ge(sg["rows_in"], 16 * 9)
            pe.wait_ge(sg["consts_made"], 1)
            for q in range(4):
                last = turn(R[2][:, q * P:(q + 1) * P], rows[:, q, :], ident[:, :])
            last.then_inc(sg["vec_turned"], 1)
            turn(R[3][:, 0:KT], crow[0:KT, 0, :], ident[0:KT, 0:KT])
            turn(R[3][:, P:2 * P], crow[:, 1, :], ident[:, :]).then_inc(sg["c_turned"], 1)

            pe.wait_ge(sg["cs_made"], 1)

            def ada(n, first):
                for k in range(2):
                    if not first:
                        pe.wait_ge(sg["ada_free"], 2 * n + k - 1)
                    for h in range(2):
                        pe.wait_ge(raw_in[2 * k + h], 16 * n + 16)
                        for r in range(8):
                            last = mm(acc[k][:, 0:NC], raw[:, 4 * k + 2 * h + r // PK, r % PK, :], cst[:, 8 * h + r, :],
                                      start=(h + r == 0), stop=(h == 1 and r == 7))
                        last.then_inc(sg["ada_used"], 1)
            ada(0, True)
            with pe.Fori(1, 3 * KT) as n:
                ada(n, False)

            pe.wait_ge(sg["x_scaled"], 1)
            pe.wait_ge(sg["cs_made"], 1)
            pe.wait_ge(sg["vec_made"], 1)
            for j in range(KT):
                pe.wait_ge(sg["a_tmp"], max(j - 3, 0))
                bank = R[2 + j % 4]
                for a in range(2):
                    turn(bank[:, a * P:(a + 1) * P], xtok[:, a, j * P:(j + 1) * P], ident[:, :])
                turn(bank[:, TP:T], xs[:, j * P:(j + 1) * P], ident[0:NS, 0:NS]).then_inc(sg["x_turned"], 1)

            def products(at, k, hi, lo, between=None):
                bank = acc[at.bank(k)]
                pe.wait_ge(sg[f"acc_free{at.bank(k)}"], at.drained(k))
                for q in range(4):
                    pe.wait_ge(sg["lo_made"], at.pieces_before(4 * k + q) + 1)
                    s = at.slot(4 * k + q, SPLIT)
                    for r in range(PK):
                        if between and r % 2 == 0:
                            between(8 * k + 2 * q + r // 2)
                        kt = PK * q + r
                        mm(bank[:, 0:T], whi[:, s, r, :], hi[:, kt, :], start=(kt == 0), stop=False, skip_group_check=True)
                        mm(bank[:, 0:T], whi[:, s, r, :], lo[:, kt, :], start=False, stop=False, skip_group_check=True)
                        last = mm(bank[:, 0:T], wlo[:, s, r, :], hi[:, kt, :], start=False, stop=(kt == KT - 1), skip_group_check=True)
                    last.then_inc(sg["piece_used"], 1)

            pe.wait_ge(sg["a_lo"], KT)
            products(At(S_BG), 0, ahi, alo)
            pe.wait_ge(sg["bg_made"], 1)
            pe.wait_ge(sg["a_tmp"], KT)
            for a in range(3):
                rows_ = P if a < 2 else NS
                last = turn(R[4][0:rows_, 64 * a:64 * a + 64], bg[:, 0, a * P:a * P + rows_], ident[0:64, 0:64])
            last.then_inc(sg["bg_turned"], 1)
            pe.wait_ge(sg["bg_taken"], 1)
            mm(R[5][:, 0:64], m_incl[:, :], bgT[:, 0:2, GH:2 * GH], start=True, stop=True)
            mm(R[5][:, 64:128], m_str[:, :], bgT[:, 0:2, GH:2 * GH], start=True, stop=True)
            mm(R[5][0:NS, 128:160], smask[:, :], bgT[0:NS, 2, GH:2 * GH], start=True, stop=True)
            mm(R[5][0:NS, 160:192], m_str_s[:, :], bgT[0:NS, 2, GH:2 * GH], start=True, stop=True)
            mm(R[3][:, 0:128], ones[:, :], gx[:, :, :, :].rearrange("p a c h -> p (a c h)"), start=True, stop=True)
            mm(R[3][:, 128:384], ones[0:NS, :], gxs[:, :, :].rearrange("p b h -> p (b h)"), start=True,
               stop=True).then_inc(sg["chunk_sums"], 1)
            pe.wait_ge(sg["chunk_exp"], 1)

            def hgrn_steps(s, n):
                if s == 0:
                    pe.wait_ge(sg["h_decayed"], n + 1)
                    pe.wait_ge(sg["h_decayed_p"], n + 1)
                    pe.wait_ge(sg["h_new"], 8 * n)
                    pe.wait_ge(sg["h_rs"], n)
                    for a in range(2):
                        turn(R[2][:, a * P:(a + 1) * P], hX[:, 3, a * P:(a + 1) * P], ident[:, :])
                        turn(R[2][:, (2 + a) * P:(3 + a) * P], hi_[:, a * P:(a + 1) * P], ident[:, :])
                    turn(R[3][0:NS, 0:P], hX[:, 3, TP:T], ident[:, :])
                    turn(R[3][0:NS, P:2 * P], hi_[:, TP:T], ident[:, :])
                    for a in range(2):
                        mm(R[4][:, a * P:(a + 1) * P], hX[:, 1, a * P:(a + 1) * P], hX[:, 0, a * P:(a + 1) * P], start=True, stop=True)
                    mm(R[4][0:NS, TP:T], hX[:, 1, TP:T], hX[:, 0, TP:T], start=True, stop=True).then_inc(sg["h_turned"], 1)
                if s == 4:
                    pe.wait_ge(sg["h_tok"], n + 1)
                    pe.wait_ge(sg["h_spread"], n + 1)
                    pe.wait_ge(sg["h_step"], 8 * n)
                    for a in range(2):
                        mm(R[5 + a][:, :], htok[:, a, :], hiX[:, a].rearrange("p c v -> p (c v)"), start=True, stop=True)
                    for a in range(2):
                        last = mm(R[2 + a][:, :], htoks[:, 0, :], hiXs[:, 4 * a:4 * a + 4, :].rearrange("p c v -> p (c v)"),
                                  start=True, stop=True)
                    last.then_inc(sg["h_ds"], 1)
                if s == 10:
                    pe.wait_ge(sg["h_at"], n + 1)
                    pe.wait_ge(sg["h_step"], 8 * (n + 1))
                    pe.wait_ge(sg["h_s0"], 16 * (n + 1))
                    pe.wait_ge(sg["h_t1"], n)
                    for a in range(2):
                        mm(R[7][:, a * P:(a + 1) * P], htok[:, 2 + a, :], hAT[:, a * P:(a + 1) * P], start=(a == 0), stop=False,
                           skip_group_check=True)
                    mm(R[7][:, TP:T], htoks[:, 1, :], hAT[0:NS, TP:T], start=False, stop=False, skip_group_check=True)
                    for c in range(1, NHC):
                        mm(R[7][:, c * HC:(c + 1) * HC], hS[:, c - 1, :], hX[:, 2, c * HC:(c + 1) * HC], start=False, stop=False,
                           skip_group_check=True)
                    for b in range(NB):
                        last = mm(R[7][:, TP + b * TS:TP + (b + 1) * TS], hS0[:, b, :], hX[:, 2, TP + b * TS:TP + (b + 1) * TS],
                                  start=False, stop=(b == NB - 1), skip_group_check=True)
                    last.then_inc(sg["h_o"], 1)
                if s == 14:
                    pe.wait_ge(sg["h_sq"], n + 1)
                    mm(R[4][:, 0:T], ones[:, :], hsq[:, :], start=True, stop=True).then_inc(sg["h_ss"], 1)

            for k in range(4):
                products(At(S_H0), k, ahi, alo)

            def hgrn_body(at, n):
                for k in range(4):
                    products(at, k, ahi, alo, lambda s: hgrn_steps(s, n))
            loop(pe, hgrn_body, S_H1, 4, HH - 1, apart=1)
            for k in range(4):
                products(At(S_GA0), k, ahi, alo, lambda s: hgrn_steps(s, HH - 1))

            def plain(hi, lo):
                def body(at, n):
                    for k in range(2):
                        products(at, k, hi, lo)
                return body
            loop(pe, plain(ahi, alo), S_GA1, 2, (KT - 4) // 2)
            pe.wait_ge(sg["h_ohi"], HH)
            pe.wait_ge(sg["h_olo"], HH)
            loop(pe, plain(ohi, olo), S_WA, 2, KT // 2)

            def delta_first(s, j):
                if s == 0:
                    pe.wait_ge(sg["g_cc"], 48 * (j + 1))
                    pe.wait_ge(sg["g_qkt"], EARLIER + j)
                    for k in range(4):
                        last = mm(R[7][:, 24 * k:24 * k + 24], gcc[:, k, :], ident[0:24, 0:24], start=True, stop=True)
                    last.then_inc(sg["g_halo_turned"], 1)
                if s == 42:
                    pe.wait_ge(sg["g_c"], 4 * (j + 1))
                    pe.wait_ge(sg["g_tail"], j + 1)
                    pe.wait_ge(sg["g_vn"], 4 * j)
                    pe.wait_ge(sg["g_wcp"], EARLIER + j)
                    pe.wait_ge(sg["g_st"], 4 * j)
                    for a in range(3):
                        bank, m = (R[2], R[3], R[5])[a], (P, P, NS)[a]
                        for k in range(4):
                            last = turn(bank[0:m, k * P:(k + 1) * P], gC[:, k, a * P:a * P + m], ident[:, :])
                    last.then_inc(sg["g_turned"], 1)
                    for k in range(4):
                        last = turn(R[6][0:27, k * P:(k + 1) * P], gtail[:, k, :], ident[:, :])
                    last.then_inc(sg["g_tail_turned"], 1)
                if s == 45:
                    pe.wait_ge(sg["g_tokqk"], EARLIER + j + 1)
                    pe.wait_ge(sg["g_tokd"], EARLIER + j + 1)
                    pe.wait_ge(sg["g_tokv"], EARLIER + j + 1)
                    pe.wait_ge(sg["g_tail_out"], j + 1)
                    pe.wait_ge(sg["g_ors"], j)
                    for bank, src in ((R[7], lambda a: gtq[:, a]), (R[4], lambda a: gtk[:, a]),
                                      (R[6], lambda a: gqp[:, a, 0]), (R[5], lambda a: gqp[:, a, 1])):
                        for a in range(2):
                            turn(bank[:, a * P:(a + 1) * P], src(a), ident[:, :])
                        last = turn(bank[:, TP:T], src(2)[0:NS], ident[0:NS, 0:NS])
                    last.then_inc(sg["g_qk_turned"], 1)
                if s == 47:
                    pe.wait_ge(sg["g_gr"], EARLIER + j + 1)
                    pe.wait_ge(sg["g_qpt"], EARLIER + j + 1)
                    for a in range(2):
                        mm(R[2 + a][:, 0:2 * P], m_incl[:, :], gGR[:, a, 0].rearrange("p e s -> p (e s)"), start=True, stop=True)
                        mm(R[2 + a][:, 2 * P:4 * P], m_str[:, :], gGR[:, a, 1].rearrange("p e s -> p (e s)"), start=True, stop=True)
                    mm(R[5][0:NS, 0:64], smask[:, :], gGRs[:, 0].rearrange("p e s -> p (e s)"), start=True, stop=True)
                    mm(R[5][0:NS, 64:128], m_str_s[:, :], gGRs[:, 1].rearrange("p e s -> p (e s)"), start=True,
                       stop=True).then_inc(sg["g_d"], 1)

            def delta_second(s, n, halos):
                if s == 2:
                    pe.wait_ge(sg["g_qkt"], EARLIER + n + 1)
                    pe.wait_ge(sg["g_qpt"], EARLIER + n + 1)
                    pe.wait_ge(sg["g_ex"], EARLIER + n + 1)
                    for a in range(2):
                        mm(R[6][:, 2 * a * P:(2 * a + 1) * P], gkT[:, a * P:(a + 1) * P], gkT[:, a * P:(a + 1) * P], start=True, stop=True)
                        mm(R[6][:, (2 * a + 1) * P:(2 * a + 2) * P], gkT[:, a * P:(a + 1) * P], gqT[:, a * P:(a + 1) * P], start=True, stop=True)
                    mm(R[5][0:NS, 128:160], gkT[:, TP:T], gkT[:, TP:T], start=True, stop=True)
                    mm(R[5][0:NS, 160:192], gkT[:, TP:T], gqT[:, TP:T], start=True, stop=True).then_inc(sg["g_kk"], 1)
                if s == 4:
                    pe.wait_ge(sg["g_lev"], 6 * n + 1)
                    for p in range(4):
                        turn(R[2][:, p * P:(p + 1) * P], glev[:, 0, p, :], ident[:, :])
                    for e in range(2):
                        last = turn(R[4][0:NS, e * NS:(e + 1) * NS], glevs[:, 0, e, :], ident[0:NS, 0:NS])
                    last.then_inc(sg["g_l1"], 1)
                if s in (6, 10, 14, 18, 22):
                    l = (s - 2) // 4
                    pe.wait_ge(sg["g_lev"], 6 * n + l + 1)
                    if l == 1:
                        pe.wait_ge(sg["g_u1"], EARLIER + n + 1)
                    else:
                        pe.wait_ge(sg["g_unew"], 5 * n + l - 1)
                    for p in range(4):
                        last = mm(R[3][:, p * P:(p + 1) * P], glev[:, l % 2, p, :], gUi[:, p, :], start=True, stop=True)
                    if l == 1:
                        for e in range(2):
                            last = mm(R[5][0:NS, e * NS:(e + 1) * NS], glevs[:, 1, e, :], gUs[:, e, :], start=True, stop=True)
                    last.then_inc(sg["g_pu"], 1)
                if s in (8, 12, 16, 20, 24):
                    l = (s - 4) // 4
                    pe.wait_ge(sg["g_pucp"], 5 * n + l)
                    if l == 1:
                        pe.wait_ge(sg["g_t1"], n + 1)
                        pe.wait_ge(sg["g_qkm"], EARLIER + n + 1)
                    else:
                        pe.wait_ge(sg["g_tnew"], 4 * n + l - 1)
                    for p in range(4):
                        last = mm(R[2][:, p * P:(p + 1) * P], gT[:, p, :], gPU[:, p, :], start=True, stop=True)
                    if l < 5:
                        for p in range(4):
                            last = mm(R[6][:, p * P:(p + 1) * P], gPU[:, p, :], gT[:, p, :], start=True, stop=True)
                    if l == 1:
                        for e in range(2):
                            last = mm(R[4][0:NS, e * NS:(e + 1) * NS], gTs[:, e, :], gPUs[:, e, :], start=True, stop=True)
                    last.then_inc(sg["g_ut"], 1)
                if s == 11:
                    pe.wait_ge(sg["g_unew"], 5 * n + 1)
                    pe.wait_ge(sg["g_halo"], halos)
                    for e in range(2):
                        mm(R[7][:, e * NS:(e + 1) * NS], gbek[0:NS, 2, e, :], gUs[:, e, :], start=True, stop=True)
                    for e in range(2):
                        last = mm(R[7][:, 64 + e * NS:64 + (e + 1) * NS], gbv[0:NS, 2, e, :], gUs[:, e, :], start=True, stop=True)
                    last.then_inc(sg["g_uts"], 1)
                if s == 13:
                    pe.wait_ge(sg["g_qw"], n + 1)
                    pe.wait_ge(sg["g_s0"], 32 * (n + 1))
                    for e in range(2):
                        for b in range(NB):
                            last = mm(R[4][:, 64 * e + 8 * b:64 * e + 8 * b + 8], gS0[:, e, b, :],
                                      gQW[:, e, b].rearrange("p k t -> p (k t)"), start=True, stop=True)
                    last.then_inc(sg["g_sw"], 1)
                if s == 17:
                    pe.wait_ge(sg["g_vt"], EARLIER + n + 1)
                    for e in range(2):
                        last = turn(R[5][0:NS, e * P:(e + 1) * P], guTs[:, e, :], ident[:, :])
                    last.then_inc(sg["g_vtt"], 1)
                if s in (19, 25):
                    e = (s - 19) // 6
                    pe.wait_ge(sg["g_vx"], 2 * n + e + 1)
                    pe.wait_ge(sg["g_qws"], n + 1)
                    pe.wait_ge(sg["g_vns"], n + 1)
                    pe.wait_ge(sg["g_snew"], 2 * n + e)
                    for a in range(2):
                        last = mm(R[4 + a][:, :], gkl[0:NS, 2, e, :], gvX[:, 4 * a:4 * a + 4, :].rearrange("p b v -> p (b v)"),
                                  start=True, stop=True)
                    last.then_inc(sg["g_dss"], 1)
                if s == 27:
                    pe.wait_ge(sg["g_unew"], 5 * n + 5)
                    pe.wait_ge(sg["g_tnew"], 4 * n + 4)
                    for p in range(4):
                        mm(R[3][:, p * P:(p + 1) * P], gbek[:, p // 2, p % 2, :], gUi[:, p, :], start=True, stop=True)
                    for p in range(4):
                        bank = (R[2], R[6])[p // 2]
                        last = mm(bank[:, (p % 2) * P:(p % 2 + 1) * P], gUi[:, p, :], gbv[:, p // 2, p % 2, :], start=(p % 2 == 0),
                                  stop=False, skip_group_check=True)
                    last.then_inc(sg["g_w"], 1)
                if s in (29, 33, 37, 40):
                    c = {29: 0, 33: 1, 37: 2, 40: 3}[s]
                    pe.wait_ge(sg["g_vn"], 4 * n + c + 1)
                    pe.wait_ge(sg["g_snew"], 2 * n + 2)
                    pe.wait_ge(sg["g_st"], 4 * n + max(c - 1, 0))
                    a, r0, col = c // 2, GC * (c % 2), 2 * P * (c % 2)
                    for e in range(2):
                        last = mm(R[5][:, col + e * P:col + (e + 1) * P], gkl[r0:r0 + GC, a, e, :], gvn[r0:r0 + GC, a, e, :],
                                  start=True, stop=True, skip_group_check=True)
                    last.then_inc(sg["g_ds"], 1)
                if s in (31, 35, 39):
                    c = {31: 1, 35: 2, 39: 3}[s]
                    pe.wait_ge(sg["g_st"], 4 * n + c)
                    pe.wait_ge(sg["g_wcp"], EARLIER + n + 1)
                    a, r0 = c // 2, GC * (c % 2)
                    bank = (R[2], R[6])[a]
                    for e in range(2):
                        last = mm(bank[r0:r0 + GC, e * P:(e + 1) * P], gPU[:, 2 * a + e, r0:r0 + GC], gS[:, c - 1, e, :],
                                  start=False, stop=False, skip_group_check=True)
                    last.then_inc(sg["g_ws"], 1)
                if s == 41:
                    pe.wait_ge(sg["g_attn"], n + 1)
                    pe.wait_ge(sg["g_st"], 4 * n + 3)
                    pe.wait_ge(sg["g_vt"], EARLIER + n + 1)
                    for e in range(2):
                        bank = (R[7], R[4])[e]
                        for a in range(2):
                            mm(bank[:, a * P:(a + 1) * P], gvn[:, a, e, :], gat[:, a, e, :], start=(a == 0), stop=False, skip_group_check=True)
                        mm(bank[:, TP:T], gvns[:, e, :], gats[:, e, :], start=False, stop=False, skip_group_check=True)
                        for c in range(1, NGC):
                            last = mm(bank[:, c * GC:(c + 1) * GC], gS[:, c - 1, e, :], gqpT[:, e, c * GC:(c + 1) * GC],
                                      start=False, stop=(c == NGC - 1), skip_group_check=True)
                    last.then_inc(sg["g_o"], 1)
                if s == 44:
                    pe.wait_ge(sg["g_osq"], n + 1)
                    pe.wait_ge(sg["g_oadd"], EARLIER + n + 1)
                    mm(R[7][:, 0:T], ones[:, :], gn1[:, 0, :], start=True, stop=True)
                    mm(R[4][:, 0:T], ones[:, :], gn1[:, 1, :], start=True, stop=True).then_inc(sg["g_oss"], 1)

            pe.wait_ge(sg["h_rs"], HH)
            pe.wait_ge(sg["h_t1"], HH)
            pe.wait_ge(sg["h_new"], 8 * HH)
            pe.wait_ge(sg["h_step"], 8 * HH)
            pe.wait_ge(sg["g_zero"], 1)
            for k in range(6):
                products(At(S_G0), k, ahi, alo, lambda s: delta_first(s, 0))

            def delta_body(first):
                def body(at, n):
                    def between(s):
                        delta_first(s, n + first + 1) if s < 40 else None
                        delta_second(s, n + first, n + first + 2)
                        delta_first(s, n + first + 1) if s >= 40 else None
                    for k in range(6):
                        products(at, k, ahi, alo, between)
                return body
            loop(pe, delta_body(0), S_G1, 6, HALF, apart=1)
            pe.wait_ge(sg["g_ohi"], HALF)
            pe.wait_ge(sg["g_olo"], HALF)
            loop(pe, plain(ohi, olo), S_WB1, 2, KT // 2)
            loop(pe, delta_body(HALF), S_G2, 6, GJ - 1 - HALF)
            for k in range(6):
                products(At(S_GB0), k, ahi, alo, lambda s: delta_second(s, GJ - 1, GJ))
            loop(pe, plain(ahi, alo), S_GB1, 2, (KT - 6) // 2)
            pe.wait_ge(sg["g_ohi"], GJ)
            pe.wait_ge(sg["g_olo"], GJ)
            loop(pe, plain(ohi, olo), S_WB2, 2, KT // 2)
            pe.wait_ge(sg["m_lo"], KT)
            loop(pe, plain(mhi, mlo), S_WO, 2, KT // 2)

            def sum_channels(v):
                pe.wait_ge(sg["w_sum"], v * KT)
                mm(R[2][:, 0:T], ones[:, :], tsum[:, :], start=True, stop=True).then_inc(sg["w_ss"], 1)

            sum_channels(1)
            def token_turn(n):
                for k in range(2):
                    pe.wait_ge(sg[f"w_xin{k}"], 32 * n + 32)
                    pe.wait_ge(sg["w_h"], 2 * n)
                    for a in range(2):
                        turn(R[3 + k][:, a * P:(a + 1) * P], xrow[:, k, a, :], ident[:, :])
                    turn(R[3 + k][:, TP:T], xrow[0:NS, k, 2, :], ident[0:NS, 0:NS]).then_inc(sg["w_xturned"], 1)
            repeat(pe, token_turn, KT // 2)
            sum_channels(2)
            pe.wait_ge(sg["b_lo"], KT)
            with pe.Fori(0, FG) as g:
                with pe.Fori(0, KT // 2) as n:
                    at = At(S_FF, n + g * KT, 2)
                    for k in range(2):
                        products(at, k, ahi, alo)
                with pe.Fori(0, KT // 2) as n:
                    at = At(S_FF, n + g * KT + KT // 2, 2)
                    pe.wait_ge(sg["f_lo"], EARLIER + g * KT + KT)
                    for k in range(2):
                        products(at, k, ohi, olo)
            sum_channels(3)
            def result_turn(n):
                for k in range(2):
                    pe.wait_ge(sg["w_h"], KT + 2 * n + k + 1)
                    pe.wait_ge(sg["y_out"], 2 * n)
                    for a in range(2):
                        turn(R[3 + k][:, a * P:(a + 1) * P], tu[:, k, a * P:(a + 1) * P], ident[:, :])
                    turn(R[3 + k][0:NS, 2 * P:3 * P], tu[:, k, TP:T], ident[:, :]).then_inc(sg["y_turned"], 1)

            repeat(pe, result_turn, KT // 2)
        def sample_of(ap, width):
            return ap[..., TAIL:UW].rearrange("p (b s) -> p b s", s=3 + TS) if ap.ndim == 2 else \
                ap[:, :, TAIL:UW].rearrange("p c (b s) -> p c b s", s=3 + TS)

        @block.scalar
        def _(act):
            f = nc.scalar.activation
            nc.scalar.preload_act_table_set(TABLE_SET)

            act.wait_ge(sg["c_turned"], 1)
            f(ce[:, 0, 0:KT], R[3][:, 0:KT], ACT.Exp, scale=-1.0)
            f(ce[:, 0, 16:16 + P], R[3][:, P:2 * P], ACT.Exp, scale=-1.0).then_inc(sg["c_exp"], 1)
            act.wait_ge(sg["lb_diff"], 1)
            f(lbx[:, 2:4, :], lbx[:, 0:2, :], ACT.Exp).then_inc(sg["lb_exp"], 1)
            act.wait_ge(sg["x_in"], 48)
            act.wait_ge(sg["rows_zeroed"], 1)
            for a in range(2):
                f(xjunk[:, :], xtok[:, a, :], ACT.Square, accum_out=xss[:, 0, a:a + 1]).then_inc(sg["pro_act"], 1)
                act.wait_ge(sg["pro_act"], a + 1)
            f(xjunk[0:NS, :], xs[:, :], ACT.Square, accum_out=xss[0:NS, 0, 2:3]).then_inc(sg["pro_act"], 1)
            act.wait_ge(sg["pro_act"], 3)
            f(xss[:, 1, :], xss[:, 0, :], ACT.Ln, scale=1.0 / D, bias=eps[:, :]).then_inc(sg["pro_act"], 1)
            act.wait_ge(sg["pro_act"], 4)
            f(xss[:, 2, :], xss[:, 1, :], ACT.Exp, scale=-0.5).then_inc(sg["x_rs"], 1)
            for j in range(KT):
                act.wait_ge(sg["a_tmp"], j + 1)
                f(ahi[:, j, :], atmp[:, j % 2, :], ACT.Copy).then_inc(sg["a_hi"], 1)

            def split_hi(at, k):
                k += AHEAD
                s, r = at.slot(k, SPLIT), at.slot(k, RAW)
                act.wait_ge(raw_in[r // 2], ADA_LOADS + at.loads_done(k))
                act.wait_ge(sg["piece_used"], atleast0(at.pieces_before(k) - SPLIT + 1))
                f(whi[:, s], raw[:, r], ACT.Copy).then_inc(sg["hi_made"], 1)

            def slab_done(at, k):
                act.wait_ge(sg["piece_used"], at.pieces_before(4 * k + 4))

            def slab_hi(at, k):
                for q in range(4):
                    split_hi(at, 4 * k + q)

            for k in range(AHEAD):
                split_hi(At(S_BG), k - AHEAD)
            slab_hi(At(S_BG), 0)

            slab_done(At(S_BG), 0)
            f(bg[0:GH, 1, :], acc[0][0:GH, 0:T], ACT.Exp, scale=-1.0).then_inc(sg["beta_exp"], 1)
            act.wait_ge(sg["acc_free0"], 1)
            f(bg[GH:2 * GH, 2, :], bg[GH:2 * GH, 1, :], ACT.Abs).then_inc(sg["soft_exp"], 1)
            act.wait_ge(sg["soft_exp"], 1)
            f(bg[GH:2 * GH, 3, :], bg[GH:2 * GH, 2, :], ACT.Exp, scale=-1.0)
            f(bgc[GH:2 * GH, 2:3], bgc[GH:2 * GH, 1:2], ACT.Exp).then_inc(sg["soft_exp"], 1)
            act.wait_ge(sg["soft_den"], 1)
            f(bg[GH:2 * GH, 2, :], bg[GH:2 * GH, 4, :], ACT.Ln).then_inc(sg["soft_ln"], 1)
            act.wait_ge(sg["chunk_sums"], 1)
            f(bgs[:, 0:128], R[5][:, 0:128], ACT.Exp)
            f(bgs[0:NS, 128:192], R[5][0:NS, 128:192], ACT.Exp)
            f(bgs[:, 192:576], R[3][:, 0:384], ACT.Exp).then_inc(sg["chunk_exp"], 1)

            def hgrn_own(at, s, i):
                if s == 8:
                    slab_done(at, 0)
                    act.wait_ge(sg["h_gden"], i)
                    f(he[:, :], acc[at.bank(0)][:, 0:T], ACT.Exp, scale=-1.0).then_inc(sg["h_qexp"], 1)
                if s == 16:
                    slab_done(at, 1)
                    act.wait_ge(sg["h_qden"], i + 1)
                    f(he[:, :], acc[at.bank(1)][:, 0:T], ACT.Exp,
                      scale=-1.0).then_inc(sg[f"acc_free{at.bank(1)}"], 1)
                if s == 19:
                    act.wait_ge(sg["h_f"], i + 1)
                    f(hlf[:, :], hf[:, :], ACT.Ln).then_inc(sg["h_ln"], 1)
                if s == 22:
                    act.wait_ge(sg["h_diff"], i + 1)
                    act.wait_ge(sg["h_new"], 8 * i)
                    act.wait_ge(sg["h_decayed"], i)
                    act.wait_ge(sg["h_decayed_p"], i)
                    f(hE[:, 0, :], hD[:, 0, :], ACT.Exp)
                    f(hE[:, 1, :], hD[:, 0, :], ACT.Exp, scale=-1.0)
                    f(hE[:, 2, :], hG[:, :], ACT.Exp)
                    f(hE[:, 3, :], hD[:, 1, :], ACT.Exp).then_inc(sg["h_e"], 1)
                if s == 24:
                    slab_done(at, 2)
                    act.wait_ge(sg["h_turned"], i)
                    f(hi_[:, :], acc[at.bank(2)][:, 0:T], ACT.Copy).then_inc(sg[f"acc_free{at.bank(2)}"], 1)
                if s == 32:
                    slab_done(at, 3)
                    act.wait_ge(sg["h_fden"], i + 1)
                    f(he[:, :], acc[at.bank(3)][:, 0:T], ACT.Exp, scale=-1.0).then_inc(sg["h_gexp"], 1)

            def hgrn_prev(s, n):
                if s == 1:
                    act.wait_ge(sg["h_turned"], n + 1)
                    act.wait_ge(sg["h_o"], n)
                    f(htok[:, :, :], R[2][:, :].rearrange("p (a d) -> p a d", d=P), ACT.Copy)
                    f(htoks[:, :, :], R[3][0:NS, 0:2 * P].rearrange("p (k d) -> p k d", d=P), ACT.Copy).then_inc(sg["h_tok"], 1)
                if s == 12:
                    act.wait_ge(sg["h_o"], n + 1)
                    act.wait_ge(sg["h_ss"], n)
                    f(hsq[:, :], R[7][:, 0:T], ACT.Square).then_inc(sg["h_sq"], 1)
                if s == 15:
                    act.wait_ge(sg["h_ss"], n + 1)
                    act.wait_ge(sg["h_t1"], n)
                    f(hse[:, :], R[4][:, 0:T], ACT.Ln, scale=1.0 / P, bias=eps[:, :]).then_inc(sg["h_ssln"], 1)
                    act.wait_ge(sg["h_ssln"], n + 1)
                    f(hrs[:, :], hse[:, :], ACT.Exp, scale=-0.5).then_inc(sg["h_rs"], 1)
                if s == 18:
                    act.wait_ge(sg["h_out"], n + 1)
                    f(ohi[:, n, :] if isinstance(n, int) else ohi[:, bass.ds(n, 1), :].squeeze(1), hof[:, :], ACT.Copy).then_inc(sg["h_ohi"], 1)

            def hgrn(at, i, n):
                for s in range(33):
                    if s % 2 == 0 and s < 32:
                        split_hi(at, s // 2)
                    if n is not None:
                        hgrn_prev(s, n)
                    hgrn_own(at, s, i)

            hgrn(At(S_H0), 0, None)
            loop(act, lambda at, n: hgrn(at, n + 1, n), S_H1, 4, HH - 1, apart=1)

            def gate(at, k, g):
                slab_done(at, k)
                act.wait_ge(sg["t_out"], atleast0(g - 1))
                f(pa[:, k % 2, :], acc[at.bank(k)][:, 0:T], ACT.Exp,
                  scale=-1.0).then_inc(sg[f"acc_free{at.bank(k)}"], 1)

            for s in range(33):
                if s % 2 == 0 and s < 32:
                    split_hi(At(S_GA0), s // 2)
                hgrn_prev(s, HH - 1)
                if s % 8 == 0 and s > 0:
                    gate(At(S_GA0), s // 8 - 1, s // 8 - 1)

            def gates(first):
                def body(at, n):
                    for k in range(2):
                        slab_hi(at, k)
                        gate(at, k, first + 2 * n + k)
                return body
            loop(act, gates(4), S_GA1, 2, (KT - 4) // 2)

            def only_hi(at, n):
                for k in range(2):
                    slab_hi(at, k)
            loop(act, only_hi, S_WA, 2, KT // 2)

            def delta_own(at, s, j):
                if s in (8, 16, 24, 32):
                    k = s // 8 - 1
                    slab_done(at, k)
                    act.wait_ge(sg["g_tail"], j)
                    src = acc[at.bank(k)]
                    f(gU[:, k, 3:3 + TP], src[:, 0:TP], ACT.Copy)
                    f(sample_of(gU[:, k, :], TS)[:, :, 3:], src[:, TP:T].rearrange("p (b t) -> p b t", t=TS),
                      ACT.Copy).then_inc(sg[f"acc_free{at.bank(k)}"], 1)
                if s in (12, 20, 28, 36):
                    k = (s - 12) // 8
                    act.wait_ge(sg["g_tap"], 4 * j + k + 1)
                    act.wait_ge(sg["g_z"], 2 * j)
                    act.wait_ge(sg["g_c"], 4 * j + k)
                    f(gce[:, 0:CW], gca[:, 0:CW], ACT.Exp, scale=-1.0).then_inc(sg["g_cexp"], 1)
                if s == 43:
                    act.wait_ge(sg["g_turned"], j + 1)
                    for a in range(3):
                        m = P if a < 2 else NS
                        for k in range(2):
                            last = f(gjunk[0:m, :], (R[2], R[3], R[5])[a][0:m, k * P:(k + 1) * P], ACT.Square,
                                     accum_out=gss[0:m, 0, a, k:k + 1]).then_inc(sg["g_ss"], 1)
                            act.wait_ge(sg["g_ss"], EARLIER + 6 * j + 2 * a + k + 1)
                    f(gss[:, 1], gss[:, 0], ACT.Ln, bias=eps[:, :]).then_inc(sg["g_ssln"], 1)
                    act.wait_ge(sg["g_ssln"], EARLIER + j + 1)
                    f(gss[:, 2], gss[:, 1], ACT.Exp, scale=-0.5).then_inc(sg["g_rs"], 1)
                    act.wait_ge(sg["g_tail_turned"], j + 1)
                    act.wait_ge(sg["g_tail_stored"], 96 * j)
                    f(gto[:, :, :], R[6][0:27, :].rearrange("p (k d) -> p k d", d=P), ACT.Copy).then_inc(sg["g_tail_out"], 1)
                if s == 46:
                    act.wait_ge(sg["g_qk_turned"], j + 1)
                    f(gqT[:, :], R[7][:, 0:T], ACT.Copy)
                    f(gkT[:, :], R[4][:, 0:T], ACT.Copy).then_inc(sg["g_qkt"], 1)
                    for e in range(2):
                        bank = (R[6], R[5])[e]
                        f(gqpT[:, e, :], bank[:, 0:TP], ACT.Copy)
                        last = f(gQW[:, e, :, 0, :], bank[:, TP:T].rearrange("p (b t) -> p b t", t=TS), ACT.Copy)
                    last.then_inc(sg["g_qpt"], 1)
                if s in (47, 48):
                    k = s - 47
                    slab_done(at, 4 + k)
                    act.wait_ge(sg["g_c"], 4 * j + 4)
                    act.wait_ge(sg["g_z"], 2 * j + k)
                    f(gce[:, 0:T], acc[at.bank(4 + k)][:, 0:T], ACT.Exp, scale=-1.0).then_inc(sg["g_zexp"], 1)

            def delta_prev(s, n, slot):
                if s == 0:
                    act.wait_ge(sg["g_d"], EARLIER + n + 1)
                    for a in range(2):
                        f(gGR[:, a].rearrange("p k e s -> p (k e s)"), R[2 + a][:, :], ACT.Exp)
                    f(gGRs[:, :].rearrange("p k e s -> p (k e s)"), R[5][0:NS, 0:128], ACT.Exp).then_inc(sg["g_ex"], 1)
                if s in (7, 11, 15, 19, 23):
                    l = (s - 3) // 4
                    act.wait_ge(sg["g_pu"], 5 * n + l)
                    last = f(gPU[:, :, :], R[3][:, :].rearrange("p (q s) -> p q s", s=P), ACT.Copy)
                    if l == 1:
                        last = f(gPUs[:, :, :], R[5][0:NS, 0:2 * NS].rearrange("p (e s) -> p e s", s=NS), ACT.Copy)
                    last.then_inc(sg["g_pucp"], 1)
                if s == 12:
                    act.wait_ge(sg["g_uts"], EARLIER + n + 1)
                    f(gQW[:, :, :, 1, :], R[7][:, 0:2 * NS].rearrange("p (e b t) -> p e b t", e=2, t=TS), ACT.Copy,
                      scale=-1.0).then_inc(sg["g_qw"], 1)
                if s == 14:
                    act.wait_ge(sg["g_sw"], n + 1)
                    act.wait_ge(sg["g_oadd"], EARLIER + n)
                    f(gqws[:, :].rearrange("p e b k t -> p (e b k t)"), R[4][:, 0:128], ACT.Copy).then_inc(sg["g_qws"], 1)
                if s == 18:
                    act.wait_ge(sg["g_vtt"], n + 1)
                    f(gvns[:, :, :], R[5][0:NS, 0:2 * P].rearrange("p (e v) -> p e v", v=P), ACT.Copy).then_inc(sg["g_vns"], 1)
                if s == 28:
                    act.wait_ge(sg["g_w"], n + 1)
                    f(gPU[:, :, :], R[3][:, :].rearrange("p (q s) -> p q s", s=P), ACT.Copy, scale=-1.0).then_inc(sg["g_wcp"], 1)
                if s in (28, 32, 36, 39):
                    c = {28: 0, 32: 1, 36: 2, 39: 3}[s]
                    act.wait_ge(sg["g_ws"], 3 * n + c)
                    a, r0 = c // 2, GC * (c % 2)
                    f(gvn[r0:r0 + GC, a], (R[2], R[6])[a][r0:r0 + GC, 0:2 * P].rearrange("p (e v) -> p e v", v=P),
                      ACT.Copy).then_inc(sg["g_vn"], 1)
                if s == 42:
                    act.wait_ge(sg["g_o"], n + 1)
                    act.wait_ge(sg["g_out"], EARLIER + n)
                    for e in range(2):
                        last = f(go[:, e, 0:TP], (R[7], R[4])[e][:, 0:TP], ACT.Copy)
                    last.then_inc(sg["g_ocp"], 1)
                    act.wait_ge(sg["g_oadd"], EARLIER + n + 1)
                    f(gn1[:, :, :], go[:, :, :], ACT.Square).then_inc(sg["g_osq"], 1)
                if s == 44:
                    act.wait_ge(sg["g_oss"], n + 1)
                    act.wait_ge(sg["g_olo"], n)
                    for e in range(2):
                        f(gn2[:, e, :], (R[7], R[4])[e][:, 0:T], ACT.Ln, scale=1.0 / P, bias=eps[:, :]).then_inc(sg["g_ossln"], 1)
                    act.wait_ge(sg["g_ossln"], 2 * n + 2)
                    f(gn1[:, :, :], gn2[:, :, :], ACT.Exp, scale=-0.5).then_inc(sg["g_ors"], 1)
                if s == 47:
                    act.wait_ge(sg["g_out"], EARLIER + n + 1)
                    f(ohi[:, bass.ds(2 * slot, 2), :] if not isinstance(slot, int) else ohi[:, 2 * slot:2 * slot + 2, :],
                      gn2[:, :, :], ACT.Copy).then_inc(sg["g_ohi"], 1)

            def delta(at, j, n, slot):
                for s in range(49):
                    if s % 2 == 0 and s < 48:
                        split_hi(at, s // 2)
                    if n is not None:
                        delta_prev(s, n, slot)
                    delta_own(at, s, j)

            act.wait_ge(sg["g_zero"], 1)
            delta(At(S_G0), 0, None, None)
            loop(act, lambda at, n: delta(at, n + 1, n, n), S_G1, 6, HALF, apart=1)

            def first_half(at, n):
                for k in range(2):
                    slab_hi(at, k)
                    slab_done(at, k)
                    act.wait_ge(sg[f"t_stored{k}"], 16 * (M_WB1 // 2 + n))
                    f(pb[:, k, :], acc[at.bank(k)][:, 0:T], ACT.Copy).then_inc(sg[f"acc_free{at.bank(k)}"], 1)
            loop(act, first_half, S_WB1, 2, KT // 2)
            loop(act, lambda at, n: delta(at, n + 1 + HALF, n + HALF, n), S_G2, 6, GJ - 1 - HALF)
            for s in range(49):
                if s % 2 == 0 and s < 48:
                    split_hi(At(S_GB0), s // 2)
                delta_prev(s, GJ - 1, HALF - 1)
                if s % 8 == 0 and s > 0:
                    gate(At(S_GB0), s // 8 - 1, KT + s // 8 - 1)
            loop(act, gates(KT + 6), S_GB1, 2, (KT - 6) // 2)

            def both(at, n):
                for k in range(2):
                    slab_hi(at, k)
                    act.wait_ge(sg["t_s3"], 2 * n + k + 1)
                    f(mhi[:, bass.ds(2 * n + k, 1), :].squeeze(1), tt[:, k, :], ACT.Copy).then_inc(sg["m_hi"], 1)
            loop(act, both, S_WB2, 2, KT // 2)

            def block_of(t, n, k):
                return t[:, bass.ds(2 * n + k, 1), :].squeeze(1)

            def mixed(at, n):
                for k in range(2):
                    slab_hi(at, k)
                    slab_done(at, k)
                    act.wait_ge(sg["w_sum"], 2 * n)
                    f(block_of(mix, n, k), acc[at.bank(k)][:, 0:T], ACT.Copy)
                    f(tt[:, k, :], acc[at.bank(k)][:, 0:T], ACT.Square).then_inc(sg[f"acc_free{at.bank(k)}"], 1)
            loop(act, mixed, S_WO, 2, KT // 2, apart=1)

            def norm(v):
                act.wait_ge(sg["w_ss"], v)
                act.wait_ge(sg["w_t1"], EARLIER + KT * (v - 1))
                f(tsum2[:, :], R[2][:, 0:T], ACT.Ln, scale=1.0 / D, bias=eps[:, :]).then_inc(sg["w_ln"], 1)
                act.wait_ge(sg["w_ln"], v)
                f(trs[:, :], tsum2[:, :], ACT.Exp, scale=-0.5).then_inc(sg["w_rs"], 1)

            norm(1)
            def residual_squares(n):
                for k in range(2):
                    act.wait_ge(sg["w_h"], 2 * n + k + 1)
                    act.wait_ge(sg["w_sum"], KT + 2 * n)
                    f(tt[:, k, :], block_of(res, n, k), ACT.Square).then_inc(sg["w_hsq"], 1)
            repeat(act, residual_squares, KT // 2)
            norm(2)
            with act.Fori(0, KT // 2) as n:
                for k in range(2):
                    act.wait_ge(sg["b_tmp"], EARLIER + 2 * n + k + 1)
                    f(block_of(ahi, n, k), tu[:, k, :], ACT.Copy).then_inc(sg["b_hi"], 1)
            with act.Fori(0, FG) as g:
                with act.Fori(0, KT // 2) as n:
                    at = At(S_FF, n + g * KT, 2)
                    for k in range(2):
                        slab_hi(at, k)
                        slab_done(at, k)
                        act.wait_ge(sg["f_sq"], EARLIER + g * KT + 2 * n)
                        f(tt[:, k, :], acc[at.bank(k)][:, 0:T], ACT.Relu).then_inc(sg[f"acc_free{at.bank(k)}"], 1)
                        act.wait_ge(sg["f_sq"], EARLIER + g * KT + 2 * n + k + 1)
                        f(block_of(ohi, n, k), tu[:, k, :], ACT.Copy).then_inc(sg["f_hi"], 1)
                with act.Fori(0, KT // 2) as n:
                    at = At(S_FF, n + g * KT + KT // 2, 2)
                    for k in range(2):
                        slab_hi(at, k)
            def result_squares(n):
                for k in range(2):
                    for b in range(2):
                        act.wait_ge(sg[f"acc_free{At(S_END).bank(b)}"], At(S_END).drained(b))
                    act.wait_ge(sg["w_sum"], 2 * KT + 2 * n)
                    f(tt[:, k, :], block_of(mix, n, k), ACT.Square).then_inc(sg["w_hsq"], 1)
            repeat(act, result_squares, KT // 2)
            norm(3)
            def result_out(n):
                for k in range(2):
                    act.wait_ge(sg["y_turned"], 2 * n + k + 1)
                    act.wait_ge(sg["y_stored"], 64 * n)
                    f(ytok[:, k, 0:2, :], R[3 + k][:, 0:TP].rearrange("p (a d) -> p a d", d=P), ACT.Copy)
                    f(ytok[0:NS, k, 2, :], R[3 + k][0:NS, TP:TP + P], ACT.Copy).then_inc(sg["y_out"], 1)

            repeat(act, result_out, KT // 2)
        @block.vector
        def _(dve):
            ts, tt_, stt, rec = nc.vector.tensor_scalar, nc.vector.tensor_tensor, nc.vector.scalar_tensor_tensor, nc.vector.reciprocal
            copy = nc.vector.tensor_copy
            MUL, ADD, SUB = ALU.mult, ALU.add, ALU.subtract
            steps = [0]

            def step(ins):
                steps[0] += 1
                ins.then_inc(sg["pro_dve"], 1)
                dve.wait_ge(sg["pro_dve"], steps[0])

            nc.vector.memset(rows[:, :, :], 0.0)
            nc.vector.memset(xss[:, :, :], 1.0).then_inc(sg["rows_zeroed"], 1)
            nc.vector.memset(tab[:, :, :], 0.0)
            dve.wait_ge(sg["vec_turned"], 1)
            copy(vec[:, :, :], R[2][:, :].rearrange("p (q c) -> p q c", c=P)).then_inc(sg["vec_made"], 1)
            dve.wait_ge(sg["vec_made"], 1)
            l0, l1 = vec[:, 0, 4 * KT:5 * KT], vec[:, 0, 5 * KT:6 * KT]
            step(tt_(lbx[:, 4, :], l0, l1, ALU.max))
            step(tt_(lbx[:, 0, :], l0, lbx[:, 4, :], SUB))
            tt_(lbx[:, 1, :], l1, lbx[:, 4, :], SUB).then_inc(sg["lb_diff"], 1)
            dve.wait_ge(sg["c_exp"], 1)
            step(ts(ce[:, 1, :], ce[:, 0, :], 1.0, None, ADD))
            step(rec(ce[:, 2, :], ce[:, 1, :]))
            tt_(cst[:, :, 0], R[3][:, 0:KT], ce[:, 2, 0:KT], MUL)
            tt_(cst[:, :, 1:NC], R[3][:, P:2 * P].rearrange("p (b k) -> p k b", k=KT),
                ce[:, 2, 16:16 + P].rearrange("p (b k) -> p k b", k=KT), MUL).then_inc(sg["cs_made"], 1)
            dve.wait_ge(sg["lb_exp"], 1)
            step(tt_(lbx[:, 4, :], lbx[:, 2, :], lbx[:, 3, :], ADD))
            step(rec(lbx[:, 5, :], lbx[:, 4, :]))
            step(tt_(lbt[:, :, 0], lbx[:, 2, :], lbx[:, 5, :], MUL))
            step(ts(lbt[:, :, 1], lbt[:, :, 0], -1.0, 1.0, MUL, ADD))
            dve.wait_ge(sg["x_rs"], 1)
            for a in range(2):
                ts(xtok[:, a, :], xtok[:, a, :], xss[:, 2, a:a + 1], None, MUL)
            ts(xs[:, :], xs[:, :], xss[0:NS, 2, 2:3], None, MUL).then_inc(sg["x_scaled"], 1)
            with dve.Fori(0, 3 * KT) as n:
                for k in range(2):
                    dve.wait_ge(sg["ada_used"], 4 * n + 2 * k + 2)
                    ts(mod[:, bass.ds(2 * n + k, 1), :].squeeze(1), acc[k][:, 0:NC], vec[:, 1, bass.ds(2 * n + k, 1)], None,
                       ADD).then_inc(sg["ada_free"], 1)
            dve.wait_ge(sg["ada_free"], 6 * KT)
            for g, j in ((0, 1), (2, 4)):
                step(ts(mod[:, j * KT:(j + 1) * KT, :], mod[:, j * KT:(j + 1) * KT, :], 1.0, None, ADD))
            for g, j in ((0, 1), (1, 2), (2, 4), (3, 5)):
                m = mod[:, j * KT:(j + 1) * KT, :]
                step(tt_(m, m, vec[:, 0, g * KT:(g + 1) * KT].unsqueeze(2).to_broadcast([P, KT, NC]), MUL))

            def modulate(out, src, scale, shift, inner, last):
                po, so = halves(out)
                ps_, ss_ = halves(src)
                ts(po, ps_, scale(0), shift(0), MUL, ADD)
                tt_(so, ss_, scale(1), MUL).then_inc(sg[inner[0]], 1)
                dve.wait_ge(sg[inner[0]], inner[1])
                tt_(so, so, shift(1), ADD).then_inc(sg[last], 1)

            def mods(j):
                return lambda part: mod[:, j, 0:1] if part == 0 else mod[:, j, 1:NC].unsqueeze(2).to_broadcast([P, NB, TS])

            for j in range(KT):
                dve.wait_ge(sg["x_turned"], j + 1)
                dve.wait_ge(sg["a_hi"], max(j - 1, 0))
                steps[0] += 1
                modulate(atmp[:, j % 2, :], R[2 + j % 4][:, 0:T], mods(KT + j), mods(j), ("pro_dve", steps[0]), "a_tmp")
                dve.wait_ge(sg["a_hi"], j + 1)
                tt_(alo[:, j, :], atmp[:, j % 2, :], ahi[:, j, :].bitcast(F32), SUB).then_inc(sg["a_lo"], 1)

            def split_lo(at, k):
                k += AHEAD
                s, r = at.slot(k, SPLIT), at.slot(k, RAW)
                dve.wait_ge(sg["hi_made"], at.pieces_before(k) + 1)
                dve.wait_ge(sg["piece_used"], atleast0(at.pieces_before(k) - SPLIT + 1))
                tt_(wlo[:, s], raw[:, r], whi[:, s].bitcast(F32), SUB).then_inc(sg["lo_made"], 1)

            def slab_lo(at, k):
                for q in range(4):
                    split_lo(at, 4 * k + q)

            def drained(at, k):
                dve.wait_ge(sg[f"acc_free{at.bank(k)}"], at.drained(k) + 1)

            for k in range(AHEAD):
                split_lo(At(S_BG), k - AHEAD)
            slab_lo(At(S_BG), 0)

            lo_, hi2 = slice(0, GH), slice(GH, 2 * GH)
            dve.wait_ge(sg["beta_exp"], 1)
            dve.wait_ge(sg["small_in"], 32)
            step(ts(bg[lo_, 2, :], bg[lo_, 1, :], 1.0, None, ADD))
            step(rec(bg[lo_, 0, :], bg[lo_, 2, :]))
            ts(bg[hi2, 1, :], acc[0][hi2, 0:T], bgc[hi2, 0:1], None, ADD).then_inc(sg["acc_free0"], 1)
            dve.wait_ge(sg["acc_free0"], 1)
            dve.wait_ge(sg["soft_exp"], 2)
            ts(bg[hi2, 4, :], bg[hi2, 3, :], 1.0, None, ADD).then_inc(sg["soft_den"], 1)
            dve.wait_ge(sg["soft_ln"], 1)
            step(ts(bg[hi2, 3, :], bg[hi2, 1, :], 0.0, None, ALU.max))
            step(tt_(bg[hi2, 4, :], bg[hi2, 3, :], bg[hi2, 2, :], ADD))
            ts(bg[hi2, 0, :], bg[hi2, 4, :], bgc[hi2, 2:3], -1.0, MUL, MUL).then_inc(sg["bg_made"], 1)
            dve.wait_ge(sg["bg_turned"], 1)
            step(copy(bgT[:, 0:2, :], R[4][:, 0:128].rearrange("p (a h) -> p a h", h=2 * GH)))
            step(copy(bgT[0:NS, 2, :], R[4][0:NS, 128:192]))
            for a in range(2):
                for c in range(2):
                    ts(gx[:, a, c, :], bgT[:, a, GH:2 * GH], cm64[:, c:c + 1], None, MUL)
            for b in range(NB):
                last = ts(gxs[:, b, :], bgT[0:NS, 2, GH:2 * GH], cm4[:, b:b + 1], None, MUL)
            last.then_inc(sg["bg_taken"], 1)
            dve.wait_ge(sg["chunk_exp"], 1)
            for a in range(3):
                m = P if a < 2 else NS
                sums = bgs[:, 0:128].rearrange("p (k a h) -> p k a h", k=2, a=2)[:, :, a] if a < 2 else \
                    bgs[0:NS, 128:192].rearrange("p (k h) -> p k h", k=2)
                copy(tab[0:m, :, a], bgT[0:m, a, 0:GH])
                copy(tab[0:m, :, 12 + a], bgT[0:m, a, GH:2 * GH])
                for k in range(2):
                    copy(tab[0:m, :, 3 + 3 * k + a], sums[:, k])
                step(tt_(tab[0:m, :, 9 + a], bgT[0:m, a, 0:GH], sums[:, 0], MUL))
            copy(tab[:, :, 15:27], bgs[:, 192:576].rearrange("p (c h) -> p h c", h=GH)).then_inc(sg["tab_made"], 1)

            def at_chunk(ap, which):
                p_, s_ = ap[:, 0:TP].rearrange("p (c t) -> p c t", t=HC), ap[:, TP:T].rearrange("p (b t) -> p b t", t=TS)
                kp, ks = (HC // 2, TS // 2) if which == "middle" else (HC - 1, TS - 1)
                return (p_[:, :, kp:kp + 1].to_broadcast([P, NHC, HC]), s_[:, :, ks:ks + 1].to_broadcast([P, NB, TS]))

            def by_chunk(ap):
                return ap[:, 0:TP].rearrange("p (c t) -> p c t", t=HC), ap[:, TP:T].rearrange("p (b t) -> p b t", t=TS)

            def silu(at, k, i, name, out):
                dve.wait_ge(sg[f"h_{name}exp"], i + 1)
                ts(hden[:, :], he[:, :], 1.0, None, ADD).then_inc(sg[f"h_{name}den"], 1)
                dve.wait_ge(sg[f"h_{name}den"], i + 1)
                rec(hden[:, :], hden[:, :]).then_inc(sg[f"h_{name}rec"], 1)
                dve.wait_ge(sg[f"h_{name}rec"], i + 1)
                tt_(out, acc[at.bank(k)][:, 0:T], hden[:, :], MUL).then_inc(sg[f"acc_free{at.bank(k)}"], 1)

            def hgrn_own(at, s, i):
                if s == 9:
                    dve.wait_ge(sg["h_decayed_p"], i)
                    silu(at, 0, i, "q", hq[:, :])
                    copy(hsc[:, :], lbt[:, i, :] if isinstance(i, int) else lbt[:, bass.ds(i, 1), :].squeeze(1)).then_inc(sg["h_sc"], 1)
                if s == 17:
                    drained(at, 1)
                    dve.wait_ge(sg["h_sc"], i + 1)
                    drained(at, 0)
                    ts(hden[:, :], he[:, :], 1.0, None, ADD).then_inc(sg["h_fden"], 1)
                    dve.wait_ge(sg["h_fden"], i + 1)
                    rec(hden[:, :], hden[:, :]).then_inc(sg["h_frec"], 1)
                    dve.wait_ge(sg["h_frec"], i + 1)
                    ts(hf[:, :], hden[:, :], hsc[:, 1:2], hsc[:, 0:1], MUL, ADD).then_inc(sg["h_f"], 1)
                    dve.wait_ge(sg["h_f"], i + 1)
                    ts(hk[:, :], hf[:, :], -1.0, 1.0, MUL, ADD).then_inc(sg["h_k"], 1)
                if s == 20:
                    dve.wait_ge(sg["h_ln"], i + 1)
                    nc.vector.tensor_tensor_scan(hG[:, :], reset[:, :], hlf[:, :], 0.0, MUL, ADD).then_inc(sg["h_scan"], 1)
                    dve.wait_ge(sg["h_scan"], i + 1)
                    g_, mid, end = by_chunk(hG), at_chunk(hG, "middle"), at_chunk(hG, "end")
                    d0, d1 = by_chunk(hD[:, 0, :]), by_chunk(hD[:, 1, :])
                    for a in range(2):
                        tt_(d0[a], g_[a], mid[a], SUB)
                        last = tt_(d1[a], end[a], g_[a], SUB)
                    last.then_inc(sg["h_diff"], 1)
                if s == 23:
                    dve.wait_ge(sg["h_e"], i + 1)
                    dve.wait_ge(sg["h_o"], i)
                    dve.wait_ge(sg["h_k"], i + 1)
                    tt_(hX[:, 0, :], hq[:, :], hE[:, 0, :], MUL)
                    tt_(hX[:, 1, :], hk[:, :], hE[:, 1, :], MUL).then_inc(sg["h_decayed"], 1)
                if s == 32:
                    silu(at, 3, i, "g", hsg[:, :])

            def hgrn_prev(at, s, n):
                if s == 1:
                    dve.wait_ge(sg["h_turned"], n + 1)
                    dve.wait_ge(sg["h_o"], n)
                    tt_(hAT[:, 0:TP].rearrange("p (a t) -> p a t", a=2), R[4][:, 0:TP].rearrange("p (a t) -> p a t", a=2),
                        hmask[:, :].unsqueeze(1).to_broadcast([P, 2, P]), MUL)
                    tt_(hAT[0:NS, TP:T], R[4][0:NS, TP:T], smask[:, :], MUL).then_inc(sg["h_at"], 1)
                if s == 6:
                    dve.wait_ge(sg["h_ds"], n + 1)
                    dve.wait_ge(sg["h_o"], n)
                    dve.wait_ge(sg["h_stored"], 32 * n)
                    for c in range(NHC):
                        add = R[5 + c // 4][:, (c % 4) * P:(c % 4 + 1) * P]
                        if c == 0:
                            copy(hS[:, 0, :], add).then_inc(sg["h_step"], 1)
                        else:
                            dve.wait_ge(sg["h_step"], 8 * n + c)
                            end = c * HC + HC - 1
                            stt(hS[:, c, :], hS[:, c - 1, :], hE[:, 2, end:end + 1], add, MUL, ADD).then_inc(sg["h_step"], 1)
                    dve.wait_ge(sg["h_s0"], 16 * (n + 1))
                    for b in range(NB):
                        end = TP + b * TS + TS - 1
                        stt(hSn[:, b, :], hS0[:, b, :], hE[:, 2, end:end + 1], R[2 + b // 4][:, (b % 4) * P:(b % 4 + 1) * P],
                            MUL, ADD).then_inc(sg["h_new"], 1)
                if s == 16:
                    dve.wait_ge(sg["h_rs"], n + 1)
                    stt(ht1[:, :], R[7][:, 0:T], vec[:, 0, 6 * KT:6 * KT + 1], hrs[:, :], MUL, MUL).then_inc(sg["h_t1"], 1)
                    dve.wait_ge(sg["h_t1"], n + 1)
                    dve.wait_ge(sg["h_ohi"], n)
                    dve.wait_ge(sg[f"acc_free{at.bank(1)}"], at.drained(1))
                    tt_(hof[:, :], ht1[:, :], hsg[:, :], MUL).then_inc(sg["h_out"], 1)
                if s == 19:
                    dve.wait_ge(sg["h_ohi"], n + 1)
                    o_, h_ = (olo[:, n, :], ohi[:, n, :]) if isinstance(n, int) else \
                        (olo[:, bass.ds(n, 1), :].squeeze(1), ohi[:, bass.ds(n, 1), :].squeeze(1))
                    tt_(o_, hof[:, :], h_.bitcast(F32), SUB).then_inc(sg["h_olo"], 1)

            def hgrn(at, i, n):
                for s in range(33):
                    if s % 2 == 0 and s < 32:
                        split_lo(at, s // 2)
                    if n is not None:
                        hgrn_prev(at, s, n)
                    hgrn_own(at, s, i)

            hgrn(At(S_H0), 0, None)
            loop(dve, lambda at, n: hgrn(at, n + 1, n), S_H1, 4, HH - 1, apart=1)

            def gate(at, k, g, pairs):
                drained(at, k)
                ts(pa[:, k % 2, :], pa[:, k % 2, :], 1.0, None, ADD).then_inc(sg["t_den"], 1)
                dve.wait_ge(sg["t_den"], g + 1)
                dve.wait_ge(sg[f"t_stored{k % 2}"], 16 * pairs)
                rec(pb[:, k % 2, :], pa[:, k % 2, :]).then_inc(sg["t_out"], 1)

            for s in range(33):
                if s % 2 == 0 and s < 32:
                    split_lo(At(S_GA0), s // 2)
                hgrn_prev(At(S_GA0), s, HH - 1)
                if s % 8 == 0 and s > 0:
                    gate(At(S_GA0), s // 8 - 1, s // 8 - 1, (s // 8 - 1) // 2)

            def gates(first, m0):
                def body(at, n):
                    for k in range(2):
                        slab_lo(at, k)
                        gate(at, k, first + 2 * n + k, m0 // 2 + n)
                return body
            loop(dve, gates(4, 4), S_GA1, 2, (KT - 4) // 2)

            def gated(at, n):
                for k in range(2):
                    slab_lo(at, k)
                    dve.wait_ge(sg[f"t_in{k}"], 16 * n + 16)
                    dve.wait_ge(sg[f"t_stored{k}"], 16 * (M_WA // 2 + n))
                    dve.wait_ge(sg["piece_used"], at.pieces_before(4 * k + 4))
                    tt_(pb[:, k, :], acc[at.bank(k)][:, 0:T], pa[:, k, :], MUL).then_inc(sg[f"acc_free{at.bank(k)}"], 1)
            loop(dve, gated, S_WA, 2, KT // 2)

            drained(At(S_WA, KT // 2 - 1, 2), 0)
            drained(At(S_WA, KT // 2 - 1, 2), 1)
            dve.wait_ge(sg["h_olo"], HH)
            dve.wait_ge(sg["h_stored"], 32 * HH)
            nc.vector.memset(gU[:, :, 0:3], 0.0)
            nc.vector.memset(gss[:, :, :, :], 1.0).then_inc(sg["g_zero"], 1)

            def head(t, i, size=1):
                return t[:, i:i + size] if isinstance(i, int) else t[:, bass.ds(i, size)]

            def delta_own(at, s, j):
                if s == 0:
                    for k, (first, mul, size) in enumerate(((0, 1, 1), (GJ, 1, 1), (2 * GJ, 2, 2))):
                        src = taps[:, :, first + j * mul:first + j * mul + size] if isinstance(j, int) else \
                            taps[:, :, bass.ds(first + j * mul, size)]
                        last = copy(gcw[:, k:k + size, :].rearrange("p b a -> p a b"), src)
                    last.then_inc(sg["g_cw"], 1)
                    dve.wait_ge(sg["g_halo_turned"], j + 1)
                    copy(sample_of(gU[:, :, :], 0)[:, :, :, 0:3], R[7][:, 0:96].rearrange("p (c b s) -> p c b s", c=4, b=NB)
                         ).then_inc(sg["g_halo"], 1)
                if s in (10, 18, 26, 34):
                    k = (s - 10) // 8
                    drained(at, k)
                    dve.wait_ge(sg["g_cw"], EARLIER + j + 1)
                    dve.wait_ge(sg["g_halo"], j + 1)
                    dve.wait_ge(sg["g_cexp"], 4 * j + k)
                    dve.wait_ge(sg["g_c"], 4 * j + k)
                    dve.wait_ge(sg["g_z"], 2 * j)
                    ts(gca[:, 0:CW], gU[:, k, 0:CW], gcw[:, k, 0:1], None, MUL).then_inc(sg["g_part"], 1)
                    for a in range(1, 4):
                        dve.wait_ge(sg["g_part"], EARLIER + 3 * (4 * j + k) + a)
                        stt(gca[:, 0:CW], gU[:, k, a:a + CW], gcw[:, k, a:a + 1], gca[:, 0:CW], MUL,
                            ADD).then_inc(sg["g_part" if a < 3 else "g_tap"], 1)
                if s in (13, 21, 29, 37):
                    k = (s - 13) // 8
                    m = 4 * j + k + 1
                    dve.wait_ge(sg["g_cexp"], m)
                    ts(gce[:, 0:CW], gce[:, 0:CW], 1.0, None, ADD).then_inc(sg["g_cden"], 1)
                    dve.wait_ge(sg["g_cden"], EARLIER + m)
                    rec(gce[:, 0:CW], gce[:, 0:CW]).then_inc(sg["g_crec"], 1)
                    dve.wait_ge(sg["g_crec"], EARLIER + m)
                    dve.wait_ge(sg["g_turned"], j)
                    tt_(gC[:, k, 0:TP], gca[:, 0:TP], gce[:, 0:TP], MUL)
                    tt_(gC[:, k, TP:T].rearrange("p (b t) -> p b t", t=TS), sample_of(gca[:, :], TS)[:, :, 0:TS],
                        sample_of(gce[:, :], TS)[:, :, 0:TS], MUL).then_inc(sg["g_c"], 1)
                if s == 38:
                    dve.wait_ge(sg["g_tail_turned"], j)
                    copy(gtail[:, :, 0:3], gU[:, :, TP:TP + 3])
                    copy(gtail[:, :, 3:27].rearrange("p c (b s) -> p c b s", s=3), sample_of(gU[:, :, :], 0)[:, :, :, 4:7]
                         ).then_inc(sg["g_tail"], 1)
                if s == 41:
                    dve.wait_ge(sg["g_sdec"], 2 * j)
                    dve.wait_ge(sg["g_st"], 4 * j)
                    dve.wait_ge(sg["g_tokd"], EARLIER + j)
                    copy(gsc[:, :, :], head(tab, 2 * j, 2)).then_inc(sg["g_sc"], 1)
                if s == 44:
                    dve.wait_ge(sg["g_rs"], EARLIER + j + 1)
                    dve.wait_ge(sg["g_sc"], EARLIER + j + 1)
                    dve.wait_ge(sg["g_qk_turned"], j)
                    for a in range(3):
                        m, bank = (P if a < 2 else NS), (R[2], R[3], R[5])[a]
                        ts(gtq[0:m, a, :], bank[0:m, 0:P], gss[0:m, 2, a, 0:1], QSCALE, MUL, MUL)
                        last = ts(gtk[0:m, a, :], bank[0:m, P:2 * P], gss[0:m, 2, a, 1:2], None, MUL)
                    last.then_inc(sg["g_tokqk"], 1)
                    for a in range(3):
                        m, bank = (P if a < 2 else NS), (R[2], R[3], R[5])[a]
                        for e in range(2):
                            last = ts(gbv[0:m, a, e, :], bank[0:m, (2 + e) * P:(3 + e) * P], gsc[0:m, e, a:a + 1], None, MUL)
                    last.then_inc(sg["g_tokv"], 1)
                if s in (47, 48):
                    k = s - 47
                    m = 2 * j + k + 1
                    dve.wait_ge(sg["g_zexp"], m)
                    ts(gce[:, 0:T], gce[:, 0:T], 1.0, None, ADD).then_inc(sg["g_zden"], 1)
                    dve.wait_ge(sg["g_zden"], EARLIER + m)
                    rec(gce[:, 0:T], gce[:, 0:T]).then_inc(sg["g_zrec"], 1)
                    dve.wait_ge(sg["g_zrec"], EARLIER + m)
                    dve.wait_ge(sg["g_c"], 4 * j + 4)
                    dve.wait_ge(sg["g_z"], 2 * j + k)
                    copy(gca[:, 0:T], acc[at.bank(4 + k)][:, 0:T]).then_inc(sg[f"acc_free{at.bank(4 + k)}"], 1)
                    drained(at, 4 + k)
                    tt_(gz[:, k, :], gca[:, 0:T], gce[:, 0:T], MUL).then_inc(sg["g_z"], 1)

            def delta_prev(s, n, slot):
                if s == 3:
                    dve.wait_ge(sg["g_kk"], EARLIER + n + 1)
                    dve.wait_ge(sg["g_lev"], 6 * n)
                    dve.wait_ge(sg["g_attn"], n)
                    for a in range(2):
                        for e in range(2):
                            stt(gA[:, 2 * a + e, :], gGR[:, a, 0, e, :], gsc[:, e, a:a + 1], R[6][:, 2 * a * P:(2 * a + 1) * P], MUL, MUL)
                    for e in range(2):
                        last = stt(gAs[:, e, :], gGRs[:, 0, e, :], gsc[0:NS, e, 2:3], R[5][0:NS, 128:160], MUL, MUL)
                    last.then_inc(sg["g_a"], 1)
                    for a in range(2):
                        tt_(gQKm[:, a, :], R[6][:, (2 * a + 1) * P:(2 * a + 2) * P], m_incl[:, :], MUL)
                    tt_(gQKms[:, :], R[5][0:NS, 160:192], smask[:, :], MUL).then_inc(sg["g_qkm"], 1)
                if s == 5:
                    dve.wait_ge(sg["g_l1"], EARLIER + n + 1)
                    tt_(gUi[:, :, :], ident[:, :].unsqueeze(1).to_broadcast([P, 4, P]), R[2][:, :].rearrange("p (q s) -> p q s", s=P), SUB)
                    tt_(gUs[:, :, :], ident[0:NS, 0:NS].unsqueeze(1).to_broadcast([NS, 2, NS]),
                        R[4][0:NS, 0:2 * NS].rearrange("p (e s) -> p e s", s=NS), SUB).then_inc(sg["g_u1"], 1)
                if s in (9, 13, 17, 21, 25):
                    l = (s - 5) // 4
                    dve.wait_ge(sg["g_ut"], 5 * n + l)
                    dve.wait_ge(sg["g_u1"], EARLIER + n + 1)
                    dve.wait_ge(sg["g_t1"], n + 1)
                    dve.wait_ge(sg["g_unew"], 5 * n + l - 1)
                    if l == 1:
                        tt_(gUs[:, :, :], gUs[:, :, :], R[4][0:NS, 0:2 * NS].rearrange("p (e s) -> p e s", s=NS), SUB)
                    tt_(gUi[:, :, :], gUi[:, :, :], R[2][:, :].rearrange("p (q s) -> p q s", s=P), SUB).then_inc(sg["g_unew"], 1)
                    if l < 5:
                        dve.wait_ge(sg["g_tnew"], 4 * n + l - 1)
                        tt_(gT[:, :, :], gT[:, :, :], R[6][:, :].rearrange("p (q s) -> p q s", s=P), SUB).then_inc(sg["g_tnew"], 1)
                if s == 15:
                    dve.wait_ge(sg["g_qws"], n + 1)
                    tt_(guTs[:, :, :].rearrange("p e (b t) -> p e b t", t=TS), R[7][:, 64:128].rearrange("p (e b t) -> p e b t", e=2, t=TS),
                        gqws[:, :, :, 1, :], ADD).then_inc(sg["g_vt"], 1)
                if s in (20, 26):
                    e = (s - 20) // 6
                    dve.wait_ge(sg["g_dss"], 2 * n + e + 1)
                    dve.wait_ge(sg["g_sdec"], 2 * n + e + 1)
                    for a in range(2):
                        h_ = gS0[:, e, 4 * a:4 * a + 4, :]
                        last = tt_(h_, h_, R[4 + a][:, :].rearrange("p (b v) -> p b v", v=P), ADD)
                    last.then_inc(sg["g_snew"], 1)
                if s in (30, 34, 38, 41):
                    c = {30: 0, 34: 1, 38: 2, 41: 3}[s]
                    dve.wait_ge(sg["g_ds"], 4 * n + c + 1)
                    dve.wait_ge(sg["g_o"], n)
                    dve.wait_ge(sg["g_stored"], 16 * n)
                    dve.wait_ge(sg["g_st"], 4 * n + c)
                    for e in range(2):
                        add = R[5][:, 2 * P * (c % 2) + e * P:2 * P * (c % 2) + (e + 1) * P]
                        if c == 0:
                            last = copy(gS[:, 0, e, :], add)
                        else:
                            last = stt(gS[:, c, e, :], gS[:, c - 1, e, :], gsc[:, e, 15 + c:16 + c], add, MUL, ADD)
                    last.then_inc(sg["g_st"], 1)
                if s == 42:
                    dve.wait_ge(sg["g_ocp"], EARLIER + n + 1)
                    for e in range(2):
                        last = tt_(go[:, e, TP:T].rearrange("p (b t) -> p b t", t=TS),
                                   (R[7], R[4])[e][:, TP:T].rearrange("p (b t) -> p b t", t=TS), gqws[:, e, :, 0, :], ADD)
                    last.then_inc(sg["g_oadd"], 1)
                if s == 46:
                    dve.wait_ge(sg["g_ors"], n + 1)
                    dve.wait_ge(sg["g_ohi"], n)
                    dve.wait_ge(sg["g_oadd"], EARLIER + n + 1)
                    dve.wait_ge(sg["g_z"], 2 * (n + 1))
                    stt(go[:, :, :], go[:, :, :], vec[:, 0, 6 * KT + 1:6 * KT + 2], gn1[:, :, :], MUL, MUL).then_inc(sg["g_ot1"], 1)
                    dve.wait_ge(sg["g_ot1"], EARLIER + n + 1)
                    tt_(gn2[:, :, :], go[:, :, :], gz[:, :, :], MUL).then_inc(sg["g_out"], 1)
                    dve.wait_ge(sg["g_ohi"], n + 1)
                    tt_(head(olo, 2 * slot, 2), gn2[:, :, :], head(ohi, 2 * slot, 2).bitcast(F32), SUB).then_inc(sg["g_olo"], 1)

            def delta(at, j, n, slot):
                for s in range(49):
                    if s % 2 == 0 and s < 48:
                        split_lo(at, s // 2)
                    if s == 41:
                        if n is not None:
                            delta_prev(s, n, slot)
                        delta_own(at, s, j)
                        continue
                    if n is not None:
                        delta_prev(s, n, slot)
                    delta_own(at, s, j)

            dve.wait_ge(sg["g_zero"], 1)
            dve.wait_ge(sg["tab_made"], 1)
            delta(At(S_G0), 0, None, None)
            loop(dve, lambda at, n: delta(at, n + 1, n, n), S_G1, 6, HALF, apart=1)

            def only_lo(at, n):
                for k in range(2):
                    slab_lo(at, k)
            loop(dve, only_lo, S_WB1, 2, KT // 2)
            loop(dve, lambda at, n: delta(at, n + 1 + HALF, n + HALF, n), S_G2, 6, GJ - 1 - HALF)
            for s in range(49):
                if s % 2 == 0 and s < 48:
                    split_lo(At(S_GB0), s // 2)
                delta_prev(s, GJ - 1, HALF - 1)
                if s % 8 == 0 and s > 0:
                    gate(At(S_GB0), s // 8 - 1, KT + s // 8 - 1, M_GB // 2 + (s // 8 - 1) // 2)
            loop(dve, gates(KT + 6, M_GB + 6), S_GB1, 2, (KT - 6) // 2)

            def block_of(t, n, k):
                return t[:, bass.ds(2 * n + k, 1), :].squeeze(1)

            def both(at, n):
                for k in range(2):
                    slab_lo(at, k)
                    m = 2 * n + k
                    dve.wait_ge(sg[f"t_in{k}"], 8 * KT + 48 * n + 48)
                    dve.wait_ge(sg["piece_used"], at.pieces_before(4 * k + 4))
                    tt_(tu[:, k, :], acc[at.bank(k)][:, 0:T], tin[:, k, 1, :], ADD).then_inc(sg[f"acc_free{at.bank(k)}"], 1)
                    drained(at, k)
                    tt_(tu[:, k, :], tu[:, k, :], tin[:, k, 2, :], MUL).then_inc(sg["t_s2"], 1)
                    dve.wait_ge(sg["t_s2"], m + 1)
                    tt_(tt[:, k, :], tu[:, k, :], tin[:, k, 0, :], ADD).then_inc(sg["t_s3"], 1)
                    dve.wait_ge(sg["m_hi"], m + 1)
                    tt_(block_of(mlo, n, k), tt[:, k, :], block_of(mhi, n, k).bitcast(F32), SUB).then_inc(sg["m_lo"], 1)
            dve.wait_ge(sg["g_stored"], 16 * GJ)
            loop(dve, both, S_WB2, 2, KT // 2)

            def clear_sum(v):
                dve.wait_ge(sg["w_ss"], v)
                nc.vector.memset(tsum[:, :], 0.0).then_inc(sg["w_clear"], 1)

            clear_sum(0)

            def add_square(total, k):
                dve.wait_ge(sg["w_sum"], total)
                tt_(tsum[:, :], tsum[:, :], tt[:, k, :], ADD).then_inc(sg["w_sum"], 1)

            dve.wait_ge(sg["w_clear"], 1)

            def mixed(at, n):
                for k in range(2):
                    slab_lo(at, k)
                    drained(at, k)
                    add_square(2 * n + k, k)
            loop(dve, mixed, S_WO, 2, KT // 2, apart=1)
            clear_sum(1)
            dve.wait_ge(sg["w_clear"], 2)
            dve.wait_ge(sg["w_rs"], 1)
            def residual(n):
                for k in range(2):
                    m = 2 * n + k
                    dve.wait_ge(sg["w_xturned"], m + 1)
                    dve.wait_ge(sg["w_hsq"], 2 * n)
                    tt_(tu[:, k, :], block_of(mix, n, k), trs[:, :], MUL).then_inc(sg["w_t1"], 1)
                    dve.wait_ge(sg["w_t1"], EARLIER + m + 1)
                    up, us = halves(tu[:, k, :])
                    rp, rs_ = halves(block_of(res, n, k))
                    xp, xsm = halves(R[3 + k][:, 0:T])
                    g1 = mod[:, bass.ds(2 * KT + m, 1), :].squeeze(1)
                    stt(rp, up, g1[:, 0:1], xp, MUL, ADD)
                    tt_(us, us, g1[:, 1:NC].unsqueeze(2).to_broadcast([P, NB, TS]), MUL).then_inc(sg["w_t2"], 1)
                    dve.wait_ge(sg["w_t2"], m + 1)
                    tt_(rs_, us, xsm, ADD).then_inc(sg["w_h"], 1)
                    dve.wait_ge(sg["w_hsq"], m + 1)
                    add_square(KT + m, k)
            repeat(dve, residual, KT // 2)
            clear_sum(2)
            dve.wait_ge(sg["w_clear"], 3)
            dve.wait_ge(sg["w_rs"], 2)
            def feed_input(n):
                for k in range(2):
                    m = 2 * n + k
                    dve.wait_ge(sg["b_hi"], 2 * n)
                    tt_(tin[:, k, 0, :], block_of(res, n, k), trs[:, :], MUL).then_inc(sg["w_t1"], 1)
                    dve.wait_ge(sg["w_t1"], EARLIER + KT + m + 1)
                    sc_ = mod[:, bass.ds(4 * KT + m, 1), :].squeeze(1)
                    sh_ = mod[:, bass.ds(3 * KT + m, 1), :].squeeze(1)
                    wide = lambda v: v[:, 1:NC].unsqueeze(2).to_broadcast([P, NB, TS])
                    ip, is_ = halves(tin[:, k, 0, :])
                    up, us = halves(tu[:, k, :])
                    ts(up, ip, sc_[:, 0:1], sh_[:, 0:1], MUL, ADD)
                    tt_(is_, is_, wide(sc_), MUL).then_inc(sg["w_t2"], 1)
                    dve.wait_ge(sg["w_t2"], KT + m + 1)
                    tt_(us, is_, wide(sh_), ADD).then_inc(sg["b_tmp"], 1)
                    dve.wait_ge(sg["b_hi"], m + 1)
                    tt_(block_of(alo, n, k), tu[:, k, :], block_of(ahi, n, k).bitcast(F32), SUB).then_inc(sg["b_lo"], 1)
            repeat(dve, feed_input, KT // 2)
            nc.vector.memset(mix[:, :, :], 0.0).then_inc(sg["w_clear"], 1)
            dve.wait_ge(sg["w_clear"], 4)
            with dve.Fori(0, FG) as g:
                with dve.Fori(0, KT // 2) as n:
                    at = At(S_FF, n + g * KT, 2)
                    for k in range(2):
                        slab_lo(at, k)
                        drained(at, k)
                        m = g * KT + 2 * n
                        dve.wait_ge(sg["f_lo"], EARLIER + m)
                        dve.wait_ge(sg["f_hi"], EARLIER + m)
                        tt_(tu[:, k, :], tt[:, k, :], tt[:, k, :], MUL).then_inc(sg["f_sq"], 1)
                        dve.wait_ge(sg["f_hi"], EARLIER + m + k + 1)
                        tt_(block_of(olo, n, k), tu[:, k, :], block_of(ohi, n, k).bitcast(F32), SUB).then_inc(sg["f_lo"], 1)
                with dve.Fori(0, KT // 2) as n:
                    at = At(S_FF, n + g * KT + KT // 2, 2)
                    for k in range(2):
                        slab_lo(at, k)
                        dve.wait_ge(sg["piece_used"], at.pieces_before(4 * k + 4))
                        dve.wait_ge(sg[f"acc_free{at.bank(k)}"], at.drained(k))
                        mb = block_of(mix, n, k)
                        tt_(mb, mb, acc[at.bank(k)][:, 0:T], ADD).then_inc(sg[f"acc_free{at.bank(k)}"], 1)
            with dve.Fori(0, KT // 2) as n:
                for k in range(2):
                    dve.wait_ge(sg["w_hsq"], KT + 2 * n + k + 1)
                    add_square(2 * KT + 2 * n + k, k)
            dve.wait_ge(sg["w_rs"], 3)
            def result_rows(n):
                for k in range(2):
                    m = 2 * n + k
                    dve.wait_ge(sg["y_turned"], 2 * n)
                    tt_(tin[:, k, 0, :], block_of(mix, n, k), trs[:, :], MUL).then_inc(sg["w_t1"], 1)
                    dve.wait_ge(sg["w_t1"], EARLIER + 2 * KT + m + 1)
                    ip, is_ = halves(tin[:, k, 0, :])
                    up, us = halves(tu[:, k, :])
                    rp, rs_ = halves(block_of(res, n, k))
                    g2_ = mod[:, bass.ds(5 * KT + m, 1), :].squeeze(1)
                    stt(up, ip, g2_[:, 0:1], rp, MUL, ADD)
                    tt_(is_, is_, g2_[:, 1:NC].unsqueeze(2).to_broadcast([P, NB, TS]), MUL).then_inc(sg["w_t2"], 1)
                    dve.wait_ge(sg["w_t2"], 2 * KT + m + 1)
                    tt_(us, is_, rs_, ADD).then_inc(sg["w_h"], 1)

            repeat(dve, result_rows, KT // 2)
        @block.gpsimd
        def _(pool):
            pt, ps = nc.gpsimd.tensor_tensor, nc.gpsimd.tensor_scalar
            MUL, SUB = ALU.mult, ALU.subtract
            steps = [0]

            def step(ins):
                steps[0] += 1
                ins.then_inc(sg["const_step"], 1)
                pool.wait_ge(sg["const_step"], steps[0])

            def keep(view, pattern, base, by_row):
                step(nc.gpsimd.affine_select(out=view, in_=view, compare_op=ALU.is_ge, fill=0.0, base=base,
                                             pattern=pattern, channel_multiplier=by_row))

            pool.dma_start(bgc[GH:2 * GH, 0:1], dt_bias.rearrange("o h -> h o")).then_inc(sg["small_in"], 16)
            pool.dma_start(bgc[GH:2 * GH, 1:2], A_log.rearrange("o h -> h o")).then_inc(sg["small_in"], 16)
            nc.gpsimd.memset(eps[:, :], EPS)
            nc.gpsimd.memset(ident[:, :], 0.0)
            for t in (ones, hmask, smask, reset, cm32, cm4, cm64, m_incl, m_str, m_str_s):
                nc.gpsimd.memset(t[:, :], 1.0)
            step(nc.gpsimd.memset(levm[:, :, :], 1.0))
            step(nc.gpsimd.affine_select(out=ident[:, :], in_=ident[:, :], compare_op=ALU.not_equal, fill=1.0, base=0,
                                         pattern=[[-1, P]], channel_multiplier=1))
            nc.gpsimd.memset(reset[:, 0:TP].rearrange("p (c t) -> p c t", t=HC)[:, :, 0:1], 0.0)
            nc.gpsimd.memset(reset[:, TP:T].rearrange("p (c t) -> p c t", t=TS)[:, :, 0:1], 0.0)

            def chunked(t, c, m):
                return t[:, :].rearrange("p (a b) -> p a b", b=m)
            for t, n_, m in ((hmask, P // HC, HC), (smask, NB, TS), (m_incl, 2, GC)):
                keep(chunked(t, n_, m), [[-m, n_], [0, m]], 0, 1)
                keep(chunked(t, n_, m), [[m, n_], [1, m]], 0, -1)
            for t, n_, m in ((m_str, 2, GC), (m_str_s, NB, TS)):
                keep(chunked(t, n_, m), [[-m, n_], [-1, m]], -1, 1)
                keep(chunked(t, n_, m), [[m, n_], [0, m]], m - 1, -1)
            for t, n_, m in ((cm32, P // HC, HC), (cm4, NB, TS), (cm64, 2, GC)):
                keep(t[:, :], [[-m, n_]], 0, 1)
                keep(t[:, :], [[m, n_]], m - 1, -1)
            for l in range(LEV):
                b = 1 << l
                n_ = P // (2 * b)
                v = levm[:, l, :].rearrange("p (k s) -> p k s", s=2 * b)
                keep(v, [[-2 * b, n_], [0, 2 * b]], -b, 1)
                keep(v, [[2 * b, n_], [0, 2 * b]], 2 * b - 1, -1)
                keep(v, [[0, n_], [-1, 2 * b]], b - 1, 0)
            nc.gpsimd.memset(eps[:, :], EPS).then_inc(sg["consts_made"], 1)

            def row(t, i):
                return t[i] if isinstance(i, int) else t[bass.ds(i, 1)].squeeze(0)

            def load_state(i):
                pool.wait_ge(sg["h_new"], 8 * i)
                pool.wait_ge(sg["h_o"], i)
                pool.dma_start(hS0[:, :, :], head_of(state_hgrn, i)).then_inc(sg["h_s0"], 16)

            def head_of(t, i):
                v = t[0].rearrange("b h d v -> d b h v")
                return v[:, :, i, :] if isinstance(i, int) else v[:, :, bass.ds(i, 1), :].squeeze(2)

            def spread(n):
                pool.wait_ge(sg["h_tok"], n + 1)
                pool.wait_ge(sg["h_ds"], n)
                for a in range(2):
                    pt(hiX[:, a], htok[:, 2 + a, :].unsqueeze(1).to_broadcast([P, P // HC, P]),
                       cm32[:, :].unsqueeze(2).to_broadcast([P, P // HC, P]), MUL)
                pt(hiXs[:, :, :], htoks[:, 1, :].unsqueeze(1).to_broadcast([NS, NB, P]),
                   cm4[:, :].unsqueeze(2).to_broadcast([NS, NB, P]), MUL).then_inc(sg["h_spread"], 1)

            def decayed(i):
                pool.wait_ge(sg["h_e"], i + 1)
                pool.wait_ge(sg["h_k"], i + 1)
                pool.wait_ge(sg["h_o"], i)
                pt(hX[:, 2, :], hq[:, :], hE[:, 2, :], MUL)
                pt(hX[:, 3, :], hk[:, :], hE[:, 3, :], MUL).then_inc(sg["h_decayed_p"], 1)

            def store(n):
                pool.wait_ge(sg["h_new"], 8 * (n + 1))
                out = hg_prompt[0, 0].rearrange("h d v -> d h v")
                out = out[:, n, :] if isinstance(n, int) else out[:, bass.ds(n, 1), :].squeeze(1)
                pool.dma_start(out, hS[:, NHC - 1, :]).then_inc(sg["h_stored"], 16)
                pool.dma_start(head_of(hg_sample, n), hSn[:, :, :]).then_inc(sg["h_stored"], 16)

            pool.wait_ge(sg["chunk_exp"], 1)
            pool.wait_ge(sg["tab_made"], 1)
            load_state(0)
            decayed(0)
            def hgrn(n):
                spread(n)
                store(n)
                load_state(n + 1)
                decayed(n + 1)
            repeat(pool, hgrn, HH - 1)
            spread(HH - 1)
            store(HH - 1)

            def scratch(t, j):
                return t[j] if isinstance(j, int) else t[bass.ds(j, 1)].squeeze(0)

            def save(t, j, k):
                pool.dma_start(scratch(t, j), pb[:, k, :]).then_inc(sg[f"t_stored{k}"], 16)

            def saved(blocks):
                for k in range(2):
                    pool.wait_ge(sg[f"t_stored{k}"], 8 * blocks)

            with pool.Fori(0, KT // 2) as n:
                for k in range(2):
                    pool.wait_ge(sg["t_out"], 2 * n + k + 1)
                    save(gate_d, 2 * n + k, k)
            saved(KT)
            def load_gate(j, k):
                pool.dma_start(pa[:, k, :], scratch(gate_d, j)).then_inc(sg[f"t_in{k}"], 16)

            for k in range(2):
                pool.wait_ge(sg[f"acc_free{At(S_WA).bank(k)}"], At(S_WA).drained(k))
                load_gate(k, k)
            with pool.Fori(1, KT // 2) as n:
                at = At(S_WA, n, 2)
                for k in range(2):
                    pool.wait_ge(sg[f"acc_free{at.bank(k)}"], at.drained(k))
                    save(merged_d, 2 * n - 2 + k, k)
                    load_gate(2 * n + k, k)
            for k in range(2):
                at = At(S_WA + KT - 2)
                pool.wait_ge(sg[f"acc_free{at.bank(k)}"], at.drained(k) + 1)
                save(merged_d, KT - 2 + k, k)

            cols = ((0, 1, 1), (GJ, 1, 1), (2 * GJ, 2, 2))

            def conv_cols(t, j, c):
                first, mul, size = cols[c]
                v = t.rearrange("r (c p) -> r c p", p=P)
                return v[:, first + mul * j:first + mul * j + size, :] if isinstance(j, int) else \
                    v[:, bass.ds(first + mul * j, size), :]

            places = (slice(0, 1), slice(1, 2), slice(2, 4))

            def load_cache(j):
                for c in range(3):
                    pool.dma_start(gcc[:, places[c], :], conv_cols(cache_conv[0].rearrange("b s c -> (b s) c"), j, c)
                                   ).then_inc(sg["g_cc"], 16)

            def store_tail(j, and_state=False):
                if and_state:
                    pool.wait_ge(sg["g_st"], 4 * j)
                pool.wait_ge(sg["g_tail_out"], j + 1)
                for c in range(3):
                    pool.dma_start(conv_cols(conv_prompt[0, 0], j, c), gto[0:3, places[c], :]).then_inc(sg["g_tail_stored"], 16)
                    pool.dma_start(conv_cols(conv_sample[0].rearrange("b s c -> (b s) c"), j, c), gto[3:27, places[c], :]
                                   ).then_inc(sg["g_tail_stored"], 16)

            def pair_of(t, j):
                v = t[0].rearrange("b (j e) d v -> j e d b v", e=2)
                return v[j] if isinstance(j, int) else v[bass.ds(j, 1)].squeeze(0)

            def load_delta(j):
                for e in range(2):
                    pool.dma_start(gS0[:, e], pair_of(state_gdn, j)[e]).then_inc(sg["g_s0"], 16)

            def own(j):
                pool.wait_ge(sg["g_sc"], EARLIER + j + 1)
                pool.wait_ge(sg["g_attn"], j)
                pool.wait_ge(sg["g_a"], EARLIER + j)
                def g_of(rows_, a):
                    return gsc[0:rows_, :, 12 + a:13 + a].to_broadcast([rows_, 2, rows_])
                for a in range(2):
                    pt(gGR[:, a, 0], m_str[:, :].unsqueeze(1).to_broadcast([P, 2, P]), g_of(P, a), MUL)
                    pt(gGR[:, a, 1], m_incl[:, :].unsqueeze(1).to_broadcast([P, 2, P]), g_of(P, a), MUL)
                pt(gGRs[:, 0], m_str_s[:, :].unsqueeze(1).to_broadcast([NS, 2, NS]), g_of(NS, 2), MUL)
                last = pt(gGRs[:, 1], smask[:, :].unsqueeze(1).to_broadcast([NS, 2, NS]), g_of(NS, 2), MUL)
                last.then_inc(sg["g_gr"], 1)
                pool.wait_ge(sg["g_tokqk"], EARLIER + j + 1)
                pool.wait_ge(sg["g_o"], j)
                pool.wait_ge(sg["g_ds"], 4 * j)
                for out, src, col in ((gqp, gtq, 3), (gbek, gtk, 9), (gkl, gtk, 6)):
                    for a in range(3):
                        m = P if a < 2 else NS
                        last = pt(out[0:m, a], src[0:m, a, :].unsqueeze(1).to_broadcast([m, 2, P]),
                                  gsc[0:m, :, col + a:col + a + 1].to_broadcast([m, 2, P]), MUL)
                last.then_inc(sg["g_tokd"], 1)

            def level(n, l):
                if l == 0:
                    pool.wait_ge(sg["g_a"], EARLIER + n + 1)
                    pool.wait_ge(sg["g_pu"], 5 * n)
                if l == 2:
                    pool.wait_ge(sg["g_l1"], EARLIER + n + 1)
                    pool.wait_ge(sg["g_t1"], n + 1)
                if l > 2:
                    pool.wait_ge(sg["g_pu"], 5 * n + l - 2)
                last = pt(glev[:, l % 2], gA[:, :, :], levm[:, l, :].unsqueeze(1).to_broadcast([P, 4, P]), MUL)
                if l < 2:
                    last = pt(glevs[:, l], gAs[:, :, :], levm[0:NS, l, 0:NS].unsqueeze(1).to_broadcast([NS, 2, NS]), MUL)
                last.then_inc(sg["g_lev"], 1)

            def prev(n, between=None):
                level(n, 0)
                pool.wait_ge(sg["g_lev"], 6 * n + 1)
                pool.wait_ge(sg["g_tnew"], 4 * n)
                pt(gT[:, :, :], ident[:, :].unsqueeze(1).to_broadcast([P, 4, P]), glev[:, 0], SUB)
                pt(gTs[:, :, :], ident[0:NS, 0:NS].unsqueeze(1).to_broadcast([NS, 2, NS]), glevs[:, 0], SUB).then_inc(sg["g_t1"], 1)
                level(n, 1)
                level(n, 2)
                pool.wait_ge(sg["g_qkm"], EARLIER + n + 1)
                pool.wait_ge(sg["g_o"], n)
                for a in range(2):
                    pt(gat[:, a], gGR[:, a, 1], gQKm[:, a, :].unsqueeze(1).to_broadcast([P, 2, P]), MUL)
                pt(gats[:, :, :], gGRs[:, 1], gQKms[:, :].unsqueeze(1).to_broadcast([NS, 2, NS]), MUL).then_inc(sg["g_attn"], 1)
                level(n, 3)
                level(n, 4)
                pool.wait_ge(sg["g_sw"], n + 1)
                for e in range(2):
                    pt(gS0[:, e], gS0[:, e], gsc[:, e, 19:27].unsqueeze(2).to_broadcast([P, NB, P]), MUL).then_inc(sg["g_sdec"], 1)
                pool.wait_ge(sg["g_vns"], n + 1)
                for e in range(2):
                    pool.wait_ge(sg["g_dss"], 2 * n + e)
                    if e == 1:
                        level(n, 5)
                        pool.wait_ge(sg["g_dss"], 2 * n + 1)
                    pt(gvX[:, :, :], gvns[:, e, :].unsqueeze(1).to_broadcast([NS, NB, P]),
                       cm4[:, :].unsqueeze(2).to_broadcast([NS, NB, P]), MUL).then_inc(sg["g_vx"], 1)
                if between:
                    between()
                pool.wait_ge(sg["g_snew"], 2 * n + 2)
                for e in range(2):
                    pool.dma_start(pair_of(gdn_sample, n)[e], gS0[:, e]).then_inc(sg["g_stored_s"], 16)

            def store_prompt(n):
                out = gdn_prompt[0, 0].rearrange("(j e) d v -> j d e v", e=2)
                pool.dma_start(row(out, n), gS[:, NGC - 1]).then_inc(sg["g_stored"], 16)

            pool.wait_ge(sg["g_zero"], 1)
            load_cache(0)
            load_delta(0)
            own(0)
            store_tail(0)
            pool.wait_ge(sg["g_halo_turned"], 1)
            load_cache(1)

            def delta(n, cache):
                prev(n)
                pool.wait_ge(sg["g_stored_s"], 32 * (n + 1))
                load_delta(n + 1)
                own(n + 1)
                if cache:
                    pool.wait_ge(sg["g_halo_turned"], n + 2)
                    load_cache(n + 2)
                store_tail(n + 1, True)
                store_prompt(n)

            def delta_and_cache(n):
                delta(n, True)
            repeat(pool, delta_and_cache, HALF)
            with pool.Fori(0, KT // 2) as n:
                at = At(S_WB1, n, 2)
                for k in range(2):
                    pool.wait_ge(sg[f"acc_free{at.bank(k)}"], at.drained(k) + 1)
                    save(half_d, 2 * n + k, k)
            with pool.Fori(HALF, GJ - 2) as n:
                delta(n, True)
            delta(GJ - 2, False)

            def save_gates(first, count):
                for k in range(first, first + count):
                    pool.wait_ge(sg["t_out"], KT + k + 1)
                    save(gate_d, k, k % 2)
            prev(GJ - 1, lambda: save_gates(0, 2))
            save_gates(2, 2)
            pool.wait_ge(sg["g_st"], 4 * GJ)
            store_prompt(GJ - 1)
            save_gates(4, 2)
            with pool.Fori(3, KT // 2) as n:
                for k in range(2):
                    pool.wait_ge(sg["t_out"], KT + 2 * n + k + 1)
                    save(gate_d, 2 * n + k, k)
            saved(4 * KT)
            pool.wait_ge(sg["g_stored"], 16 * GJ)
            pool.wait_ge(sg["g_stored_s"], 32 * GJ)
            pool.wait_ge(sg["g_olo"], GJ)
            def load_branches(n):
                pool.wait_ge(sg["t_s3"], 2 * n)
                for k in range(2):
                    for a, t in enumerate((merged_d, half_d, gate_d)):
                        pool.dma_start(tin[:, k, a, :], scratch(t, 2 * n + k)).then_inc(sg[f"t_in{k}"], 16)
            repeat(pool, load_branches, KT // 2)
            def load_tokens(n):
                pool.wait_ge(sg["w_xturned"], 2 * n)
                for k in range(2):
                    col = bass.ds(n * (2 * P) + k * P, P)
                    pool.dma_start(xrow[:, k, 0:2, :], x_prompt[0].rearrange("(a p) d -> p a d", p=P)[:, :, col]
                                   ).then_inc(sg[f"w_xin{k}"], 16)
                    pool.dma_start(xrow[0:NS, k, 2, :], x_sample.rearrange("b t d -> (b t) d")[:, col]
                                   ).then_inc(sg[f"w_xin{k}"], 16)


            repeat(pool, load_tokens, KT // 2)
INPUTS = ("x_prompt", "x_sample", "state_hgrn", "state_gdn", "cache_conv", "c_prompt", "c_sample", "lb_logits",
          "w_ada", "b_ada", "norm_g", "w_in", "conv_w", "A_log", "dt_bias", "hg_norm_g", "gdn_norm_g",
          "w_out_hg", "w_out_gdn", "w_o", "w_up", "w_down")


def kernel(**inputs):
    import numpy as np
    import concourse.bacc as bacc
    from concourse.bass_utils import run_bass_kernel_spmd

    nc = bacc.Bacc("TRN2", target_bir_lowering=False, num_devices=1)
    arrays, args = {}, []
    for name in INPUTS:
        a = np.ascontiguousarray(inputs[name])
        arrays[f"in_{name}"] = a
        args.append(nc.dram_tensor(f"in_{name}", a.shape, mybir.dt.from_np(a.dtype), kind="ExternalInput").ap())
    depth, batch = inputs["w_in"].shape[0], inputs["x_prompt"].shape[0]
    conv, hg, gdn = inputs["cache_conv"].shape, inputs["state_hgrn"].shape, inputs["state_gdn"].shape
    shapes = (inputs["x_prompt"].shape, inputs["x_sample"].shape, (depth, batch, *hg[2:]), (depth, batch, *gdn[2:]),
              (depth, batch, *conv[2:]), hg, gdn, conv)
    for i, shape in enumerate(shapes):
        args.append(nc.dram_tensor(f"out_{i}", shape, F32, kind="ExternalOutput").ap())
    hybrid_layer(nc, *args)
    r = run_bass_kernel_spmd(nc, [arrays], core_ids=[0])
    return tuple(r.results[0][f"out_{i}"] for i in range(len(shapes)))
```

```python
from contextlib import ExitStack

import concourse.bass as bass
from concourse import mybir

F32 = mybir.dt.float32
F32R = mybir.dt.float32r
ALU = mybir.AluOpType
ACT = mybir.ActivationFunctionType
TABLE_SET = "natural_log_exp_and_others"

P = 128
RAW = 8
SPLIT = 4
PK = 4
AHEAD = 3
EPS = 1e-6

SIGNALS = (
    "rows_zeroed rows_in small_in x_in const_step consts_made vec_turned vec_made c_turned c_exp cs_made "
    "x_rs x_scaled x_turned a_tmp a_hi a_lo ada_used ada_rows ada_turned ada_free pro_dve pro_act "
    "lb_diff lb_exp beta_exp soft_exp soft_den soft_ln bg_made bg_turned bg_taken chunk_sums "
    "chunk_exp tab_made "
    "hi_made lo_made piece_used acc_free0 acc_free1 "
    "h_qexp h_qden h_qrec h_sc h_fden h_frec h_f h_k h_ln h_scan h_diff h_e h_decayed h_decayed_p "
    "h_gexp h_gden h_grec h_turned h_at h_tok h_spread h_ds h_step h_s0 h_new h_o h_sq h_ss h_ssln h_rs "
    "h_t1 h_out h_ohi h_olo h_stored "
    "g_zero g_cc g_halo_turned g_halo g_tap g_cexp g_c g_tail g_tail_turned g_tail_out "
    "g_tail_stored g_turned g_qp g_cw g_part g_qk_turned "
    "g_attn g_lev g_t1 g_pu g_pucp g_ut g_unew g_tnew g_w g_vn g_ds g_st g_ws "
    "g_qw g_sw g_qws g_vtt g_vns g_vx g_dss g_s0 g_sdec g_snew g_o g_osq g_oss g_ossln "
    "g_ors g_ohi g_olo g_zexp g_z g_stored g_stored_s "
    "t_den t_out t_stored0 t_stored1 t_in0 t_in1 t_s2 t_s3 m_hi m_lo w_sum w_ss w_ln w_rs w_h w_hsq "
    "w_xin w_clear w_t2 w_xturned b_lo b_hi y_turned y_out y_stored"
).split()
COUNTS_ON = {
    "g_d": "h_turned", "g_kk": "h_ds", "g_l1": "h_ss", "g_uts": "h_o", "g_ss": "h_qexp", "g_ssln": "h_ln",
    "g_rs": "h_gexp", "g_qkt": "h_tok", "g_qpt": "h_sq", "g_ex": "h_ssln", "g_wcp": "h_rs", "g_ocp": "h_e",
    "g_cden": "h_gden", "g_crec": "h_grec", "g_zden": "h_fden",
    "g_zrec": "h_frec", "g_sc": "h_sc", "g_tokv": "h_f", "g_tokqk": "h_k", "g_a": "h_scan", "g_qkm": "h_diff",
    "g_u1": "h_decayed", "g_oadd": "h_at", "g_ot1": "h_t1", "g_out": "h_out", "g_gr": "h_spread",
    "g_tokd": "h_decayed_p", "g_vt": "h_olo", "f_hi": "m_hi", "f_lo": "m_lo", "w_t1": "t_s3", "b_tmp": "t_s2",
    "f_sq": "b_lo",
}
EARLIER = 16


def atleast0(count):
    return max(count, 0) if isinstance(count, int) else count


class At:

    def __init__(self, slab, n=0, slabs=0):
        self.slab0, self.n, self.slabs = slab, n, slabs
        self.piece0, self.pieces = 4 * slab, 4 * slabs

    def pieces_before(self, k):
        return self.piece0 + k + self.n * self.pieces

    def slot(self, k, ring):
        return (self.piece0 + k) % ring

    def loads_done(self, k):
        return 16 * ((self.piece0 + k) // RAW + 1) + self.n * (16 * self.pieces // RAW)

    def bank(self, slab):
        return (self.slab0 + slab) % 2

    def drained(self, slab):
        return (self.slab0 + slab) // 2 + self.n * (self.slabs // 2)


def hybrid_layer(nc, x_prompt, x_sample, state_hgrn, state_gdn, cache_conv, c_prompt, c_sample, lb_logits,
                 w_ada, b_ada, norm_g, w_in, conv_w, A_log, dt_bias, hg_norm_g, gdn_norm_g,
                 w_out_hg, w_out_gdn, w_o, w_up, w_down,
                 y_prompt, y_sample, hg_prompt, gdn_prompt, conv_prompt, hg_sample, gdn_sample, conv_sample):
    TP, D = x_prompt.shape[1:]
    NB, TS = x_sample.shape[:2]
    NS = NB * TS
    T = TP + NS
    KT = D // P
    HH = state_hgrn.shape[2]
    GH = state_gdn.shape[2]
    GJ = GH // 2
    HC, GC = 32, 64
    NHC, NGC = TP // HC, TP // GC
    LEV = 6
    QSCALE = P ** -0.5
    F = w_up.shape[2]
    FG = F // D
    NC = 1 + NB
    assert (TP, NB, TS, KT, HH, GJ) == (256, 8, 4, 16, 16, 16) and 1 << LEV == GC

    OQ, OF, OI, OG = 0, D, 2 * D, 3 * D
    GQ = 4 * D
    GK = GQ + GJ * P
    GV = GK + GJ * P
    GZ = GV + GH * P
    GB = GZ + GH * P
    GATE_A = GB + 2 * GH
    GATE_B = GATE_A + D

    def by_k(w):
        return w[0].rearrange("(k p) n -> p k n", p=P)

    win, wada, whg, wgdn, wo, wup, wdown = (by_k(w) for w in (w_in, w_ada, w_out_hg, w_out_gdn, w_o, w_up, w_down))
    merged_d = nc.dram_tensor("merged_scratch", (KT, P, T), F32, kind="Internal").ap()
    gate_d = nc.dram_tensor("gate_scratch", (KT, P, T), F32, kind="Internal").ap()
    half_d = nc.dram_tensor("half_scratch", (KT, P, T), F32, kind="Internal").ap()

    S_BG = 0
    S_H0 = 1
    S_H1 = S_H0 + 4
    S_GA0 = S_H1 + 4 * (HH - 1)
    S_GA1 = S_GA0 + 4
    S_WA = S_GA1 + KT - 4
    S_G0 = S_WA + KT
    S_G1 = S_G0 + 6
    HALF = GJ // 2
    S_WB1 = S_G1 + 6 * HALF
    S_G2 = S_WB1 + KT
    S_GB0 = S_G2 + 6 * (GJ - 1 - HALF)
    S_GB1 = S_GB0 + 6
    S_WB2 = S_GB1 + KT - 6
    S_WO = S_WB2 + KT
    S_FF = S_WO + KT
    S_END = S_FF + 2 * KT * FG
    AW = 4 * P
    ADA_BLOCKS = 6 * D // AW
    ADA_PARTS = 8 * ADA_BLOCKS
    ADA_LOADS = 16 * ADA_PARTS // (RAW // 2)

    with ExitStack() as ctx:
        def scoped(stack):
            def sb(name, shape, dt=F32):
                return stack.enter_context(nc.sbuf_tensor(name, shape, dt))
            return sb

        sb = scoped(ctx)
        sg = {n: ctx.enter_context(nc.semaphore(n)) for n in SIGNALS}
        sg.update({later: sg[earlier] for later, earlier in COUNTS_ON.items()})
        assert EARLIER == HH == KT
        raw_in = [ctx.enter_context(nc.semaphore(f"raw_in{i}")) for i in range(RAW // 2)]

        raw = sb("raw", [P, RAW, PK, P])
        whi = sb("whi", [P, SPLIT, PK, P], F32R)
        wlo = sb("wlo", [P, SPLIT, PK, P], F32R)
        with ExitStack() as later:
            xin = scoped(later)("xin", [P, 3, D])
        ahi = sb("ahi", [P, KT, T], F32R)
        alo = sb("alo", [P, KT, T], F32R)
        ohi = sb("ohi", [P, KT, T], F32R)
        olo = sb("olo", [P, KT, T], F32R)
        vec = sb("vec", [P, 4, P])
        mod = sb("mod", [P, 6 * KT, NC])
        ident = sb("ident", [P, P])
        ones = sb("ones", [P, P])
        smask = sb("smask", [NS, NS])
        cm4 = sb("cm4", [NS, NB])
        cm64 = sb("cm64", [P, 2])
        m_incl = sb("m_incl", [P, P])
        m_str = sb("m_str", [P, P])
        m_str_s = sb("m_str_s", [NS, NS])
        levm = sb("levm", [P, LEV, P])
        eps = sb("eps", [P, 1])
        pa = sb("pa", [P, 2, T])
        pb = sb("pb", [P, 2, T])
        tab = sb("tab", [P, GH, 27])

        with ExitStack() as front:
            sb = scoped(front)
            hmask = sb("hmask", [P, P])
            reset = sb("reset", [P, T])
            cm32 = sb("cm32", [P, P // HC])
            lbt = sb("lbt", [P, HH, 2])
            with ExitStack() as part:
                sb = scoped(part)
                xtok = sb("xtok", [P, 2, D])
                xs = sb("xs", [NS, D])
                xjunk = sb("xjunk", [P, D])
                rows = sb("rows", [P, 4, P])
                crow = sb("crow", [P, 2, P])
                ce = sb("ce", [P, 3, 16 + P])
                cst = sb("cst", [P, KT, NC])
                modrow = sb("modrow", [NC, 2, AW])
                xss = sb("xss", [P, 3, 3])
                lbx = sb("lbx", [P, 6, HH])
                atmp = sb("atmp", [P, 2, T])
                bg = sb("bg", [2 * GH, 5, T])
                bgc = sb("bgc", [2 * GH, 3])
                bgT = sb("bgT", [P, 3, 2 * GH])
                gx = sb("gx", [P, 2, 2, GH])
                gxs = sb("gxs", [NS, NB, GH])
                bgs = sb("bgs", [P, 576])
            with ExitStack() as part:
                sb = scoped(part)
                hq, hf, hk, hlf, hG, hi_, he, hsg, hse = (sb(f"h_{n}", [P, T]) for n in
                                                                ("q", "f", "k", "lf", "G", "i", "e", "sg", "se"))
                hsq, hrs, ht1, hof = (sb(f"h_{n}", [P, T]) for n in ("sq", "rs", "t1", "of"))
                hD = sb("h_D", [P, 2, T])
                hE = sb("h_E", [P, 4, T])
                hX = sb("h_X", [P, 4, T])
                htok = sb("h_tok", [P, 4, P])
                htoks = sb("h_toks", [P, 2, P])
                hAT = sb("h_AT", [P, T])
                hiX = sb("h_iX", [P, 2, 4, P])
                hiXs = sb("h_iXs", [P, NB, P])
                hS = sb("h_S", [P, NHC, P])
                hS0 = sb("h_S0", [P, NB, P])
                hSn = sb("h_Sn", [P, NB, P])
                hsc = sb("h_sc", [P, 2])
        UW = 3 + TP + NB * (3 + TS)
        CW = UW - 3
        with ExitStack() as part:
            sb = scoped(part)
            gU = sb("g_U", [P, 4, UW])
            gca = sb("g_ca", [P, UW])
            gce = sb("g_ce", [P, UW])
            gC = sb("g_C", [P, 4, T])
            gz = sb("g_z", [P, 2, T])
            gcc = sb("g_cc", [24, 4, P])
            gtail = sb("g_tail", [P, 4, 27])
            gtq = sb("g_tq", [P, 3, P])
            gtk = sb("g_tk", [P, 3, P])
            gbv = sb("g_bv", [P, 3, 2, P])
            gbek = sb("g_bek", [P, 3, 2, P])
            gkl = sb("g_kl", [P, 3, 2, P])
            gqp = sb("g_qp", [P, 3, 2, P])
            gvn = gqp
            gqT = sb("g_qT", [P, T])
            gkT = sb("g_kT", [P, T])
            gqpT = sb("g_qpT", [P, 2, TP])
            gGR = sb("g_GR", [P, 2, 2, 2, P])
            gGRs = sb("g_GRs", [NS, 2, 2, NS])
            gA = sb("g_A", [P, 4, P])
            gAs = sb("g_As", [NS, 2, NS])
            glev = sb("g_lev", [P, 2, 4, P])
            glevs = sb("g_levs", [NS, 2, 2, NS])
            gQKm = sb("g_QKm", [P, 2, P])
            gQKms = sb("g_QKms", [NS, NS])
            gat = sb("g_at", [P, 2, 2, P])
            gats = sb("g_ats", [NS, 2, NS])
            gT = sb("g_T", [P, 4, P])
            gUi = sb("g_Ui", [P, 4, P])
            gTs = sb("g_Ts", [NS, 2, NS])
            gUs = sb("g_Us", [NS, 2, NS])
            gPU = sb("g_PU", [P, 4, P])
            gPUs = sb("g_PUs", [NS, 2, NS])
            gQW = sb("g_QW", [P, 2, NB, 2, TS])
            gqws = sb("g_qws", [P, 2, NB, 2, TS])
            guTs = sb("g_uTs", [P, 2, NS])
            gvns = sb("g_vns", [NS, 2, P])
            gvX = sb("g_vX", [P, NB, P])
            gS = sb("g_S", [P, 4, 2, P])
            gS0 = sb("g_S0", [P, 2, NB, P])
            go = sb("g_o", [P, 2, T])
            gn1 = sb("g_n1", [P, 2, T])
            gn2 = sb("g_n2", [P, 2, T])
            gjunk = sb("g_junk", [P, P])
            gto = sb("g_to", [27, 4, P])
            gsc = sb("g_sc", [P, 2, 27])
            gcw = sb("g_cw", [P, 4, 4])
            gss = sb("g_ss", [P, 3, 3, 2])
        with ExitStack() as part:
            sb = scoped(part)
            mix = sb("mix", [P, KT, T])
            tt = sb("tt", [P, 2, T])
            tu = sb("tu", [P, 2, T])
            tin = sb("tin", [P, 2, 3, T])
            tsum = sb("tsum", [P, T])
            tsum2 = sb("tsum2", [P, T])
            trs = sb("trs", [P, T])
            ytok = sb("ytok", [P, 2, 3, P])
            with ExitStack() as merged:
                sb = scoped(merged)
                mhi = sb("mhi", [P, KT, T], F32R)
                mlo = sb("mlo", [P, KT, T], F32R)
            res = scoped(part)("res", [P, KT, T])

        acc = [ctx.enter_context(nc.psum_tensor(f"acc{i}", [P, 512], F32)) for i in range(2)]
        R = {b: ctx.enter_context(nc.psum_tensor(f"bank{b}", [P, 512], F32)) for b in range(2, 8)}
        block = ctx.enter_context(nc.Block())

        def halves(ap):
            return ap[:, 0:TP], ap[:, TP:T].rearrange("p (b t) -> p b t", t=TS)

        def loop(eng, body, slab, slabs, count, apart=0):
            for n in range(apart):
                body(At(slab, n, slabs), n)
            with eng.Fori(apart, count) as n:
                body(At(slab, n, slabs), n)

        def repeat(eng, body, count):
            body(0)
            with eng.Fori(1, count) as n:
                body(n)

        ada_bias = vec[:, 1, :]
        taps = vec[:, 2:4, :].rearrange("p a (c b) -> p (a c) b", b=2 * GJ + GH)
        TAIL = UW - NB * (3 + TS)

        @block.sync
        def _(sp):
            sp.wait_ge(sg["rows_zeroed"], 1)
            sp.dma_start(rows[0:4 * KT, 0, :], norm_g[0].rearrange("g (k p) -> (g k) p", p=P)).then_inc(sg["rows_in"], 16)
            sp.dma_start(rows[4 * KT:6 * KT, 0, :], lb_logits.rearrange("g (k p) -> (g k) p", p=P)).then_inc(sg["rows_in"], 16)
            sp.dma_start(rows[6 * KT:6 * KT + 1, 0, :], hg_norm_g).then_inc(sg["rows_in"], 16)
            sp.dma_start(rows[6 * KT + 1:6 * KT + 2, 0, :], gdn_norm_g).then_inc(sg["rows_in"], 16)
            sp.dma_start(rows[0:6 * KT, 1, :], b_ada.rearrange("o (k p) -> (o k) p", p=P)).then_inc(sg["rows_in"], 16)
            for a in range(2):
                sp.dma_start(rows[:, 2 + a, :], conv_w[0, 2 * a:2 * a + 2, :].rearrange("c (k p) -> (c k) p", p=P)).then_inc(sg["rows_in"], 16)
            sp.dma_start(crow[0:KT, 0, :], c_prompt.rearrange("o (k p) -> (o k) p", p=P)).then_inc(sg["rows_in"], 16)
            sp.dma_start(crow[:, 1, :], c_sample.rearrange("b (k p) -> (b k) p", p=P)).then_inc(sg["rows_in"], 16)
            for a in range(2):
                sp.dma_start(xtok[:, a, :], x_prompt[0, a * P:(a + 1) * P, :]).then_inc(sg["x_in"], 16)
            sp.dma_start(xs[:, :], x_sample.rearrange("b t d -> (b t) d")).then_inc(sg["x_in"], 16)

            def ada(c):
                for l in range(8):
                    sp.wait_ge(sg["ada_used"], atleast0(8 * c + l - 3))
                    sp.dma_start(raw[:, 2 * (l % 4):2 * (l % 4) + 2].rearrange("p a k c -> p a (k c)"),
                                 wada[:, 2 * l:2 * l + 2, bass.ds(c * AW, AW)]).then_inc(raw_in[l % 4], 16)
            repeat(sp, ada, ADA_BLOCKS)

            def slab(at, k, weights, row, col):
                for h in range(2):
                    piece = 4 * k + 2 * h
                    free = at.pieces_before(piece) - 6
                    if isinstance(free, int) and free <= 0:
                        sp.wait_ge(sg["ada_used"], ADA_PARTS)
                    else:
                        sp.wait_ge(sg["lo_made"], free)
                    s = at.slot(piece, RAW)
                    k0 = row + 8 * h
                    sp.dma_start(raw[:, s:s + 2].rearrange("p a k c -> p (a k) c"),
                                 weights[:, bass.ds(k0, 8) if not isinstance(k0, int) else slice(k0, k0 + 8),
                                         bass.ds(col, P)]).then_inc(raw_in[s // 2], 16)

            def hgrn(at, i):
                for k, off in enumerate((OQ, OF, OI, OG)):
                    slab(at, k, win, 0, off + i * P)

            def gdn(at, j):
                for k, col in enumerate((GQ + j * P, GK + j * P, GV + j * (2 * P), GV + P + j * (2 * P),
                                         GZ + j * (2 * P), GZ + P + j * (2 * P))):
                    slab(at, k, win, 0, col)

            def pair(weights, row, off):
                def body(at, n):
                    for k in range(2):
                        slab(at, k, weights, row, off + k * P + n * (2 * P))
                return body

            slab(At(S_BG), 0, win, 0, GB)
            hgrn(At(S_H0), 0)
            loop(sp, lambda at, n: hgrn(at, n + 1), S_H1, 4, HH - 1)
            for k in range(4):
                slab(At(S_GA0), k, win, 0, GATE_A + k * P)
            loop(sp, pair(win, 0, GATE_A + 4 * P), S_GA1, 2, (KT - 4) // 2)
            loop(sp, pair(whg, 0, 0), S_WA, 2, KT // 2)
            gdn(At(S_G0), 0)
            loop(sp, lambda at, n: gdn(at, n + 1), S_G1, 6, HALF)
            loop(sp, pair(wgdn, 0, 0), S_WB1, 2, KT // 2)
            loop(sp, lambda at, n: gdn(at, n + 1 + HALF), S_G2, 6, GJ - 1 - HALF)
            for k in range(6):
                slab(At(S_GB0), k, win, 0, GATE_B + k * P)
            loop(sp, pair(win, 0, GATE_B + 6 * P), S_GB1, 2, (KT - 6) // 2)
            loop(sp, pair(wgdn, KT, 0), S_WB2, 2, KT // 2)
            loop(sp, pair(wo, 0, 0), S_WO, 2, KT // 2)
            with sp.Fori(0, FG) as g:
                with sp.Fori(0, KT // 2) as n:
                    at = At(S_FF, n + g * KT, 2)
                    for k in range(2):
                        slab(at, k, wup, 0, g * D + n * (2 * P) + k * P)
                with sp.Fori(0, KT // 2) as n:
                    at = At(S_FF, n + g * KT + KT // 2, 2)
                    for k in range(2):
                        slab(at, k, wdown, g * KT, n * (2 * P) + k * P)
            for h in range(2):
                at = At(S_END)
                sp.wait_ge(sg["lo_made"], at.pieces_before(2 * h) - 6)
                s = at.slot(2 * h, RAW)
                sp.dma_start(raw[:, s:s + 2].rearrange("p a k c -> p (a k) c"), wo[:, 8 * h:8 * h + 8, 0:P]).then_inc(raw_in[s // 2], 16)
            def store_y(n):
                for k in range(2):
                    sp.wait_ge(sg["y_out"], 2 * n + k + 1)
                    col = bass.ds(n * (2 * P) + k * P, P)
                    sp.dma_start(y_prompt[0].rearrange("(a p) d -> p a d", p=P)[:, :, col], ytok[:, k, 0:2, :]).then_inc(sg["y_stored"], 16)
                    sp.dma_start(y_sample.rearrange("b t d -> (b t) d")[:, col], ytok[0:NS, k, 2, :]).then_inc(sg["y_stored"], 16)
            with sp.Fori(0, KT // 2) as n:
                store_y(n)
            sp.wait_ge(sg["y_stored"], 32 * KT)
            sp.wait_ge(sg["h_stored"], 32 * HH)
            sp.wait_ge(sg["g_stored"], 16 * GJ)
            sp.wait_ge(sg["g_stored_s"], 32 * GJ)
            sp.wait_ge(sg["g_tail_stored"], 96 * GJ)

        M_WA, M_WB1, M_GB, M_WB2 = KT, 2 * KT, 3 * KT, 4 * KT

        PU, UT = (8, 12, 15, 18, 21), (10, 14, 17, 20, 23)
        WS, DS = (30, 34, 38), (28, 32, 36, 40)

        @block.tensor
        def _(pe):
            mm, turn = nc.tensor.matmul, nc.tensor.transpose

            pe.wait_ge(sg["rows_in"], 16 * 9)
            pe.wait_ge(sg["consts_made"], 1)
            for q in range(4):
                last = turn(R[2][:, q * P:(q + 1) * P], rows[:, q, :], ident[:, :])
            last.then_inc(sg["vec_turned"], 1)
            turn(R[3][:, 0:KT], crow[0:KT, 0, :], ident[0:KT, 0:KT])
            turn(R[3][:, P:2 * P], crow[:, 1, :], ident[:, :]).then_inc(sg["c_turned"], 1)

            pe.wait_ge(sg["cs_made"], 1)

            def ada_turn_waits(c):
                pe.wait_ge(sg["ada_rows"], c + 1)
                pe.wait_ge(sg["ada_free"], atleast0(c - 1))

            def ada_turn(k):
                for q in range(4):
                    last = turn(R[6 + k][:, q * NC:(q + 1) * NC], modrow[:, k, q * P:(q + 1) * P], ident[0:NC, 0:NC])
                last.then_inc(sg["ada_turned"], 1)

            def ada(n):
                for k in range(2):
                    c = 2 * n + k
                    pe.wait_ge(sg["ada_rows"], atleast0(c - 1))
                    for l in range(8):
                        pe.wait_ge(raw_in[l % 4], 32 * c + 16 * (l // 4) + 16)
                        for a in range(2):
                            if l == 3 and a == 1 and not (isinstance(c, int) and c == 0):
                                ada_turn_waits(c - 1)
                            last = mm(acc[k][0:NC, :], cst[:, 2 * l + a, :],
                                      raw[:, 2 * (l % 4) + a].rearrange("p k c -> p (k c)"), start=(l + a == 0), stop=(l == 7 and a == 1))
                        last.then_inc(sg["ada_used"], 1)
                        if l == 3 and not (isinstance(c, int) and c == 0):
                            ada_turn(1 - k)
            repeat(pe, ada, ADA_BLOCKS // 2)
            ada_turn_waits(ADA_BLOCKS - 1)
            ada_turn(1)

            pe.wait_ge(sg["x_scaled"], 1)
            pe.wait_ge(sg["cs_made"], 1)
            pe.wait_ge(sg["vec_made"], 1)
            for j in range(KT):
                pe.wait_ge(sg["a_tmp"], max(j - 3, 0))
                bank = R[2 + j % 4]
                for a in range(2):
                    turn(bank[:, a * P:(a + 1) * P], xtok[:, a, j * P:(j + 1) * P], ident[:, :])
                turn(bank[:, TP:T], xs[:, j * P:(j + 1) * P], ident[0:NS, 0:NS]).then_inc(sg["x_turned"], 1)

            def products(at, k, hi, lo, between=None, ready=None):
                bank = acc[at.bank(k)]
                pe.wait_ge(sg[f"acc_free{at.bank(k)}"], at.drained(k))
                for q in range(4):
                    pe.wait_ge(sg["lo_made"], at.pieces_before(4 * k + q) + 1)
                    if ready:
                        pe.wait_ge(sg[ready], PK * q + PK)
                    s = at.slot(4 * k + q, SPLIT)
                    for r in range(PK):
                        if between and r % 2 == 0:
                            between(8 * k + 2 * q + r // 2)
                        kt = PK * q + r
                        mm(bank[:, 0:T], whi[:, s, r, :], hi[:, kt, :], start=(kt == 0), stop=False, skip_group_check=True)
                        mm(bank[:, 0:T], whi[:, s, r, :], lo[:, kt, :], start=False, stop=False, skip_group_check=True)
                        last = mm(bank[:, 0:T], wlo[:, s, r, :], hi[:, kt, :], start=False, stop=(kt == KT - 1), skip_group_check=True)
                    last.then_inc(sg["piece_used"], 1)

            pe.wait_ge(sg["a_lo"], KT)
            products(At(S_BG), 0, ahi, alo)
            pe.wait_ge(sg["bg_made"], 1)
            pe.wait_ge(sg["a_tmp"], KT)
            for a in range(3):
                rows_ = P if a < 2 else NS
                last = turn(R[4][0:rows_, 64 * a:64 * a + 64], bg[:, 0, a * P:a * P + rows_], ident[0:64, 0:64])
            last.then_inc(sg["bg_turned"], 1)
            pe.wait_ge(sg["bg_taken"], 1)
            mm(R[5][:, 0:64], m_incl[:, :], bgT[:, 0:2, GH:2 * GH], start=True, stop=True)
            mm(R[5][:, 64:128], m_str[:, :], bgT[:, 0:2, GH:2 * GH], start=True, stop=True)
            mm(R[5][0:NS, 128:160], smask[:, :], bgT[0:NS, 2, GH:2 * GH], start=True, stop=True)
            mm(R[5][0:NS, 160:192], m_str_s[:, :], bgT[0:NS, 2, GH:2 * GH], start=True, stop=True)
            mm(R[3][:, 0:128], ones[:, :], gx[:, :, :, :].rearrange("p a c h -> p (a c h)"), start=True, stop=True)
            mm(R[3][:, 128:384], ones[0:NS, :], gxs[:, :, :].rearrange("p b h -> p (b h)"), start=True,
               stop=True).then_inc(sg["chunk_sums"], 1)
            pe.wait_ge(sg["chunk_exp"], 1)

            def hgrn_steps(s, n):
                if s == 0:
                    pe.wait_ge(sg["h_decayed"], n + 1)
                    pe.wait_ge(sg["h_decayed_p"], n + 1)
                    pe.wait_ge(sg["h_new"], 8 * n)
                    pe.wait_ge(sg["h_rs"], n)
                    for a in range(2):
                        turn(R[2][:, a * P:(a + 1) * P], hX[:, 3, a * P:(a + 1) * P], ident[:, :])
                        turn(R[2][:, (2 + a) * P:(3 + a) * P], hi_[:, a * P:(a + 1) * P], ident[:, :])
                    turn(R[3][0:NS, 0:P], hX[:, 3, TP:T], ident[:, :])
                    turn(R[3][0:NS, P:2 * P], hi_[:, TP:T], ident[:, :])
                    for a in range(2):
                        mm(R[4][:, a * P:(a + 1) * P], hX[:, 1, a * P:(a + 1) * P], hX[:, 0, a * P:(a + 1) * P], start=True, stop=True)
                    mm(R[4][0:NS, TP:T], hX[:, 1, TP:T], hX[:, 0, TP:T], start=True, stop=True).then_inc(sg["h_turned"], 1)
                if s == 8:
                    pe.wait_ge(sg["h_tok"], n + 1)
                    pe.wait_ge(sg["h_spread"], n + 1)
                    pe.wait_ge(sg["h_step"], 8 * n)
                    for a in range(2):
                        mm(R[5 + a][:, :], htok[:, a, :], hiX[:, a].rearrange("p c v -> p (c v)"), start=True, stop=True)
                    for a in range(2):
                        last = mm(R[2 + a][:, :], htoks[:, 0, :], hiXs[:, 4 * a:4 * a + 4, :].rearrange("p c v -> p (c v)"),
                                  start=True, stop=True)
                    last.then_inc(sg["h_ds"], 1)
                if s == 15:
                    pe.wait_ge(sg["h_at"], n + 1)
                    pe.wait_ge(sg["h_step"], 8 * (n + 1))
                    pe.wait_ge(sg["h_s0"], 16 * (n + 1))
                    pe.wait_ge(sg["h_t1"], n)
                    for a in range(2):
                        mm(R[7][:, a * P:(a + 1) * P], htok[:, 2 + a, :], hAT[:, a * P:(a + 1) * P], start=(a == 0), stop=False,
                           skip_group_check=True)
                    mm(R[7][:, TP:T], htoks[0:NS, 1, :], hAT[0:NS, TP:T], start=False, stop=False, skip_group_check=True)
                    for c in range(1, NHC):
                        mm(R[7][:, c * HC:(c + 1) * HC], hS[:, c - 1, :], hX[:, 2, c * HC:(c + 1) * HC], start=False, stop=False,
                           skip_group_check=True)
                    for b in range(NB):
                        last = mm(R[7][:, TP + b * TS:TP + (b + 1) * TS], hS0[:, b, :], hX[:, 2, TP + b * TS:TP + (b + 1) * TS],
                                  start=False, stop=(b == NB - 1), skip_group_check=True)
                    last.then_inc(sg["h_o"], 1)
                if s == 19:
                    pe.wait_ge(sg["h_sq"], n + 1)
                    mm(R[4][:, 0:T], ones[:, :], hsq[:, :], start=True, stop=True).then_inc(sg["h_ss"], 1)

            for k in range(4):
                products(At(S_H0), k, ahi, alo)

            def hgrn_body(at, n):
                for k in range(4):
                    products(at, k, ahi, alo, lambda s: hgrn_steps(s, n))
            loop(pe, hgrn_body, S_H1, 4, HH - 1, apart=1)
            for k in range(4):
                products(At(S_GA0), k, ahi, alo, lambda s: hgrn_steps(s, HH - 1))

            def plain(hi, lo):
                def body(at, n):
                    for k in range(2):
                        products(at, k, hi, lo)
                return body
            loop(pe, plain(ahi, alo), S_GA1, 2, (KT - 4) // 2)
            pe.wait_ge(sg["h_ohi"], HH)
            pe.wait_ge(sg["h_olo"], HH)
            loop(pe, plain(ohi, olo), S_WA, 2, KT // 2)

            def delta_first(s, j):
                if s == 4:
                    pe.wait_ge(sg["g_cc"], 48 * (j + 1))
                    pe.wait_ge(sg["g_qkt"], EARLIER + j)
                    for k in range(4):
                        last = mm(R[7][:, 24 * k:24 * k + 24], gcc[:, k, :], ident[0:24, 0:24], start=True, stop=True)
                    last.then_inc(sg["g_halo_turned"], 1)
                if s == 42:
                    pe.wait_ge(sg["g_c"], 4 * (j + 1))
                    pe.wait_ge(sg["g_tail"], j + 1)
                    pe.wait_ge(sg["g_vn"], 4 * j)
                    pe.wait_ge(sg["g_wcp"], EARLIER + j)
                    pe.wait_ge(sg["g_st"], 4 * j)
                    for a in range(3):
                        bank, m = (R[2], R[3], R[5])[a], (P, P, NS)[a]
                        for k in range(4):
                            last = turn(bank[0:m, k * P:(k + 1) * P], gC[:, k, a * P:a * P + m], ident[:, :])
                    last.then_inc(sg["g_turned"], 1)
                    for k in range(4):
                        last = turn(R[6][0:27, k * P:(k + 1) * P], gtail[:, k, :], ident[:, :])
                    last.then_inc(sg["g_tail_turned"], 1)

            def delta_second(s, n, halos):
                if s == 0:
                    pe.wait_ge(sg["g_tokqk"], EARLIER + n + 1)
                    pe.wait_ge(sg["g_ors"], n)
                    for bank, src in ((R[7], lambda a: gtq[:, a]), (R[4], lambda a: gtk[:, a]),
                                      (R[6], lambda a: gqp[:, a, 0]), (R[5], lambda a: gqp[:, a, 1])):
                        if bank is R[6]:
                            pe.wait_ge(sg["g_qp"], n + 1)
                            pe.wait_ge(sg["g_tail_out"], n + 1)
                        if bank is R[5]:
                            pe.wait_ge(sg["g_tokv"], EARLIER + n + 1)
                        for a in range(2):
                            turn(bank[:, a * P:(a + 1) * P], src(a), ident[:, :])
                        last = turn(bank[:, TP:T], src(2)[0:NS], ident[0:NS, 0:NS])
                    last.then_inc(sg["g_qk_turned"], 1)
                if s == 2:
                    pe.wait_ge(sg["g_gr"], EARLIER + n + 1)
                    for a in range(2):
                        if a == 1:
                            pe.wait_ge(sg["g_qpt"], EARLIER + n + 1)
                        mm(R[2 + a][:, 0:2 * P], m_incl[:, :], gGR[:, a, 0].rearrange("p e s -> p (e s)"), start=True, stop=True)
                        mm(R[2 + a][:, 2 * P:4 * P], m_str[:, :], gGR[:, a, 1].rearrange("p e s -> p (e s)"), start=True, stop=True)
                    mm(R[5][0:NS, 0:64], smask[:, :], gGRs[:, 0].rearrange("p e s -> p (e s)"), start=True, stop=True)
                    mm(R[5][0:NS, 64:128], m_str_s[:, :], gGRs[:, 1].rearrange("p e s -> p (e s)"), start=True,
                       stop=True).then_inc(sg["g_d"], 1)
                if s == 3:
                    pe.wait_ge(sg["g_qkt"], EARLIER + n + 1)
                    pe.wait_ge(sg["g_qpt"], EARLIER + n + 1)
                    for a in range(2):
                        if a == 1:
                            pe.wait_ge(sg["g_ex"], EARLIER + n + 1)
                        mm(R[6][:, 2 * a * P:(2 * a + 1) * P], gkT[:, a * P:(a + 1) * P], gkT[:, a * P:(a + 1) * P], start=True, stop=True)
                        mm(R[6][:, (2 * a + 1) * P:(2 * a + 2) * P], gkT[:, a * P:(a + 1) * P], gqT[:, a * P:(a + 1) * P], start=True, stop=True)
                    mm(R[5][0:NS, 128:160], gkT[:, TP:T], gkT[:, TP:T], start=True, stop=True)
                    mm(R[5][0:NS, 160:192], gkT[:, TP:T], gqT[:, TP:T], start=True, stop=True).then_inc(sg["g_kk"], 1)
                if s == 6:
                    pe.wait_ge(sg["g_lev"], 6 * n + 1)
                    for p in range(4):
                        turn(R[2][:, p * P:(p + 1) * P], glev[:, 0, p, :], ident[:, :])
                    for e in range(2):
                        last = turn(R[4][0:NS, e * NS:(e + 1) * NS], glevs[:, 0, e, :], ident[0:NS, 0:NS])
                    last.then_inc(sg["g_l1"], 1)
                if s in PU:
                    l = PU.index(s) + 1
                    pe.wait_ge(sg["g_lev"], 6 * n + l + 1)
                    if l == 1:
                        pe.wait_ge(sg["g_u1"], EARLIER + n + 1)
                    else:
                        pe.wait_ge(sg["g_unew"], 5 * n + l - 1)
                    for p in range(4):
                        last = mm(R[3][:, p * P:(p + 1) * P], glev[:, l % 2, p, :], gUi[:, p, :], start=True, stop=True)
                    if l == 1:
                        for e in range(2):
                            last = mm(R[5][0:NS, e * NS:(e + 1) * NS], glevs[:, 1, e, :], gUs[:, e, :], start=True, stop=True)
                    last.then_inc(sg["g_pu"], 1)
                if s in UT:
                    l = UT.index(s) + 1
                    pe.wait_ge(sg["g_pucp"], 5 * n + l)
                    if l == 1:
                        pe.wait_ge(sg["g_t1"], n + 1)
                        pe.wait_ge(sg["g_qkm"], EARLIER + n + 1)
                    else:
                        pe.wait_ge(sg["g_tnew"], 4 * n + l - 1)
                    for p in range(4):
                        last = mm(R[2][:, p * P:(p + 1) * P], gT[:, p, :], gPU[:, p, :], start=True, stop=True)
                    if l < 5:
                        for p in range(4):
                            last = mm(R[6][:, p * P:(p + 1) * P], gPU[:, p, :], gT[:, p, :], start=True, stop=True)
                    if l == 1:
                        for e in range(2):
                            last = mm(R[4][0:NS, e * NS:(e + 1) * NS], gTs[:, e, :], gPUs[:, e, :], start=True, stop=True)
                    last.then_inc(sg["g_ut"], 1)
                if s == 12:
                    pe.wait_ge(sg["g_unew"], 5 * n + 1)
                    pe.wait_ge(sg["g_tokd"], EARLIER + n + 1)
                    pe.wait_ge(sg["g_halo"], halos)
                    for e in range(2):
                        mm(R[7][:, e * NS:(e + 1) * NS], gbek[0:NS, 2, e, :], gUs[:, e, :], start=True, stop=True)
                    for e in range(2):
                        last = mm(R[7][:, 64 + e * NS:64 + (e + 1) * NS], gbv[0:NS, 2, e, :], gUs[:, e, :], start=True, stop=True)
                    last.then_inc(sg["g_uts"], 1)
                if s == 13:
                    pe.wait_ge(sg["g_qw"], n + 1)
                    pe.wait_ge(sg["g_s0"], 32 * (n + 1))
                    for e in range(2):
                        for b in range(NB):
                            last = mm(R[4][:, 64 * e + 8 * b:64 * e + 8 * b + 8], gS0[:, e, b, :],
                                      gQW[:, e, b].rearrange("p k t -> p (k t)"), start=True, stop=True)
                    last.then_inc(sg["g_sw"], 1)
                if s == 16:
                    pe.wait_ge(sg["g_vt"], EARLIER + n + 1)
                    for e in range(2):
                        last = turn(R[5][0:NS, e * P:(e + 1) * P], guTs[:, e, :], ident[:, :])
                    last.then_inc(sg["g_vtt"], 1)
                if s in (20, 24):
                    e = (s - 20) // 4
                    pe.wait_ge(sg["g_vx"], 2 * n + e + 1)
                    pe.wait_ge(sg["g_qws"], n + 1)
                    pe.wait_ge(sg["g_vns"], n + 1)
                    pe.wait_ge(sg["g_snew"], 2 * n + e)
                    for a in range(2):
                        last = mm(R[4 + a][:, :], gkl[:, 2, e, :], gvX[:, 4 * a:4 * a + 4, :].rearrange("p b v -> p (b v)"),
                                  start=True, stop=True)
                    last.then_inc(sg["g_dss"], 1)
                if s == 25:
                    pe.wait_ge(sg["g_unew"], 5 * n + 5)
                    pe.wait_ge(sg["g_tnew"], 4 * n + 4)
                    for p in range(4):
                        mm(R[3][:, p * P:(p + 1) * P], gbek[:, p // 2, p % 2, :], gUi[:, p, :], start=True, stop=True)
                    for p in range(4):
                        bank = (R[2], R[6])[p // 2]
                        last = mm(bank[:, (p % 2) * P:(p % 2 + 1) * P], gUi[:, p, :], gbv[:, p // 2, p % 2, :], start=(p % 2 == 0),
                                  stop=False, skip_group_check=True)
                    last.then_inc(sg["g_w"], 1)
                if s in DS:
                    c = DS.index(s)
                    pe.wait_ge(sg["g_vn"], 4 * n + c + 1)
                    pe.wait_ge(sg["g_snew"], 2 * n + 2)
                    pe.wait_ge(sg["g_st"], 4 * n + max(c - 1, 0))
                    a, r0, col = c // 2, GC * (c % 2), 2 * P * (c % 2)
                    for e in range(2):
                        last = mm(R[5][:, col + e * P:col + (e + 1) * P], gkl[r0:r0 + GC, a, e, :], gvn[r0:r0 + GC, a, e, :],
                                  start=True, stop=True, skip_group_check=True)
                    last.then_inc(sg["g_ds"], 1)
                if s in WS:
                    c = WS.index(s) + 1
                    pe.wait_ge(sg["g_st"], 4 * n + c)
                    pe.wait_ge(sg["g_wcp"], EARLIER + n + 1)
                    a, r0 = c // 2, GC * (c % 2)
                    bank = (R[2], R[6])[a]
                    for e in range(2):
                        last = mm(bank[r0:r0 + GC, e * P:(e + 1) * P], gPU[:, 2 * a + e, r0:r0 + GC], gS[:, c - 1, e, :],
                                  start=False, stop=False, skip_group_check=True)
                    last.then_inc(sg["g_ws"], 1)
                if s == 41:
                    pe.wait_ge(sg["g_attn"], n + 1)
                    pe.wait_ge(sg["g_st"], 4 * n + 3)
                    pe.wait_ge(sg["g_vt"], EARLIER + n + 1)
                    for e in range(2):
                        bank = (R[7], R[4])[e]
                        for a in range(2):
                            mm(bank[:, a * P:(a + 1) * P], gvn[:, a, e, :], gat[:, a, e, :], start=(a == 0), stop=False, skip_group_check=True)
                        mm(bank[:, TP:T], gvns[:, e, :], gats[:, e, :], start=False, stop=False, skip_group_check=True)
                        for c in range(1, NGC):
                            last = mm(bank[:, c * GC:(c + 1) * GC], gS[:, c - 1, e, :], gqpT[:, e, c * GC:(c + 1) * GC],
                                      start=False, stop=(c == NGC - 1), skip_group_check=True)
                    last.then_inc(sg["g_o"], 1)
                if s == 44:
                    pe.wait_ge(sg["g_osq"], n + 1)
                    pe.wait_ge(sg["g_oadd"], EARLIER + n + 1)
                    mm(R[7][:, 0:T], ones[:, :], gn1[:, 0, :], start=True, stop=True)
                    mm(R[4][:, 0:T], ones[:, :], gn1[:, 1, :], start=True, stop=True).then_inc(sg["g_oss"], 1)

            pe.wait_ge(sg["h_rs"], HH)
            pe.wait_ge(sg["h_t1"], HH)
            pe.wait_ge(sg["h_new"], 8 * HH)
            pe.wait_ge(sg["h_step"], 8 * HH)
            pe.wait_ge(sg["g_zero"], 1)
            for k in range(6):
                products(At(S_G0), k, ahi, alo, lambda s: delta_first(s, 0))

            def delta_body(first):
                def body(at, n):
                    def between(s):
                        delta_first(s, n + first + 1) if s < 40 else None
                        delta_second(s, n + first, n + first + 2)
                        delta_first(s, n + first + 1) if s >= 40 else None
                    for k in range(6):
                        products(at, k, ahi, alo, between)
                return body
            loop(pe, delta_body(0), S_G1, 6, HALF, apart=1)
            pe.wait_ge(sg["g_ohi"], HALF)
            pe.wait_ge(sg["g_olo"], HALF)
            loop(pe, plain(ohi, olo), S_WB1, 2, KT // 2)
            loop(pe, delta_body(HALF), S_G2, 6, GJ - 1 - HALF)
            for k in range(6):
                products(At(S_GB0), k, ahi, alo, lambda s: delta_second(s, GJ - 1, GJ))
            loop(pe, plain(ahi, alo), S_GB1, 2, (KT - 6) // 2)
            pe.wait_ge(sg["g_ohi"], GJ)
            pe.wait_ge(sg["g_olo"], GJ)
            loop(pe, plain(ohi, olo), S_WB2, 2, KT // 2)
            pe.wait_ge(sg["m_lo"], KT)
            loop(pe, plain(mhi, mlo), S_WO, 2, KT // 2)

            def sum_channels(v):
                pe.wait_ge(sg["w_sum"], v * KT)
                mm(R[2][:, 0:T], ones[:, :], tsum[:, :], start=True, stop=True).then_inc(sg["w_ss"], 1)

            sum_channels(1)
            pe.wait_ge(sg["w_xin"], 32)
            for j in range(KT):
                pe.wait_ge(sg["w_h"], max(j - 1, 0))
                for a in range(2):
                    turn(R[3 + j % 2][:, a * P:(a + 1) * P], xin[:, a, j * P:(j + 1) * P], ident[:, :])
                turn(R[3 + j % 2][:, TP:T], xin[0:NS, 2, j * P:(j + 1) * P], ident[0:NS, 0:NS]).then_inc(sg["w_xturned"], 1)
            sum_channels(2)
            with pe.Fori(0, FG) as g:
                with pe.Fori(0, KT // 2) as n:
                    at = At(S_FF, n + g * KT, 2)
                    for k in range(2):
                        products(at, k, ahi, alo, ready="b_lo")
                with pe.Fori(0, KT // 2) as n:
                    at = At(S_FF, n + g * KT + KT // 2, 2)
                    pe.wait_ge(sg["f_lo"], EARLIER + g * KT + KT)
                    for k in range(2):
                        products(at, k, ohi, olo)
            sum_channels(3)
            def result_turn(n):
                for k in range(2):
                    pe.wait_ge(sg["w_h"], KT + 2 * n + k + 1)
                    pe.wait_ge(sg["y_out"], 2 * n)
                    for a in range(2):
                        turn(R[3 + k][:, a * P:(a + 1) * P], tu[:, k, a * P:(a + 1) * P], ident[:, :])
                    turn(R[3 + k][0:NS, 2 * P:3 * P], tu[:, k, TP:T], ident[:, :]).then_inc(sg["y_turned"], 1)

            repeat(pe, result_turn, KT // 2)
        def sample_of(ap, width):
            return ap[..., TAIL:UW].rearrange("p (b s) -> p b s", s=3 + TS) if ap.ndim == 2 else \
                ap[:, :, TAIL:UW].rearrange("p c (b s) -> p c b s", s=3 + TS)

        @block.scalar
        def _(act):
            f = nc.scalar.activation
            nc.scalar.preload_act_table_set(TABLE_SET)

            act.wait_ge(sg["c_turned"], 1)
            f(ce[:, 0, 0:KT], R[3][:, 0:KT], ACT.Exp, scale=-1.0)
            f(ce[:, 0, 16:16 + P], R[3][:, P:2 * P], ACT.Exp, scale=-1.0).then_inc(sg["c_exp"], 1)
            act.wait_ge(sg["lb_diff"], 1)
            f(lbx[:, 2:4, :], lbx[:, 0:2, :], ACT.Exp).then_inc(sg["lb_exp"], 1)
            act.wait_ge(sg["x_in"], 48)
            act.wait_ge(sg["rows_zeroed"], 1)
            for a in range(2):
                f(xjunk[:, :], xtok[:, a, :], ACT.Square, accum_out=xss[:, 0, a:a + 1]).then_inc(sg["pro_act"], 1)
                act.wait_ge(sg["pro_act"], a + 1)
            f(xjunk[0:NS, :], xs[:, :], ACT.Square, accum_out=xss[0:NS, 0, 2:3]).then_inc(sg["pro_act"], 1)
            act.wait_ge(sg["pro_act"], 3)
            f(xss[:, 1, :], xss[:, 0, :], ACT.Ln, scale=1.0 / D, bias=eps[:, :]).then_inc(sg["pro_act"], 1)
            act.wait_ge(sg["pro_act"], 4)
            f(xss[:, 2, :], xss[:, 1, :], ACT.Exp, scale=-0.5).then_inc(sg["x_rs"], 1)

            def ada(n):
                for k in range(2):
                    c = 2 * n + k
                    act.wait_ge(sg["ada_used"], 8 * c + 8)
                    act.wait_ge(sg["ada_turned"], atleast0(c - 1))
                    f(modrow[:, k, :], acc[k][0:NC, :], ACT.Copy).then_inc(sg["ada_rows"], 1)
            repeat(act, ada, ADA_BLOCKS // 2)
            for j in range(KT):
                act.wait_ge(sg["a_tmp"], j + 1)
                f(ahi[:, j, :], atmp[:, j % 2, :], ACT.Copy).then_inc(sg["a_hi"], 1)

            def split_hi(at, k):
                k += AHEAD
                s, r = at.slot(k, SPLIT), at.slot(k, RAW)
                act.wait_ge(raw_in[r // 2], ADA_LOADS + at.loads_done(k))
                act.wait_ge(sg["piece_used"], atleast0(at.pieces_before(k) - SPLIT + 1))
                f(whi[:, s], raw[:, r], ACT.Copy).then_inc(sg["hi_made"], 1)

            def slab_done(at, k):
                act.wait_ge(sg["piece_used"], at.pieces_before(4 * k + 4))

            def slab_hi(at, k):
                for q in range(4):
                    split_hi(at, 4 * k + q)

            for k in range(AHEAD):
                split_hi(At(S_BG), k - AHEAD)
            slab_hi(At(S_BG), 0)

            slab_done(At(S_BG), 0)
            f(bg[0:GH, 1, :], acc[0][0:GH, 0:T], ACT.Exp, scale=-1.0).then_inc(sg["beta_exp"], 1)
            act.wait_ge(sg["acc_free0"], 1)
            f(bg[GH:2 * GH, 2, :], bg[GH:2 * GH, 1, :], ACT.Abs).then_inc(sg["soft_exp"], 1)
            act.wait_ge(sg["soft_exp"], 1)
            f(bg[GH:2 * GH, 3, :], bg[GH:2 * GH, 2, :], ACT.Exp, scale=-1.0)
            f(bgc[GH:2 * GH, 2:3], bgc[GH:2 * GH, 1:2], ACT.Exp).then_inc(sg["soft_exp"], 1)
            act.wait_ge(sg["soft_den"], 1)
            f(bg[GH:2 * GH, 2, :], bg[GH:2 * GH, 4, :], ACT.Ln).then_inc(sg["soft_ln"], 1)
            act.wait_ge(sg["chunk_sums"], 1)
            f(bgs[:, 0:128], R[5][:, 0:128], ACT.Exp)
            f(bgs[0:NS, 128:192], R[5][0:NS, 128:192], ACT.Exp)
            f(bgs[:, 192:576], R[3][:, 0:384], ACT.Exp).then_inc(sg["chunk_exp"], 1)

            def sigmoid(buf, out, exp_done, log_done, result):
                act.wait_ge(*exp_done)
                f(buf, buf, ACT.Ln, bias=ones[:, 0:1]).then_inc(log_done[0], 1)
                act.wait_ge(*log_done)
                f(out, buf, ACT.Exp, scale=-1.0).then_inc(result, 1)

            def hgrn_own(at, s, i):
                if s == 8:
                    slab_done(at, 0)
                    act.wait_ge(sg[f"acc_free{at.bank(1)}"], at.drained(1))
                    f(he[:, :], acc[at.bank(0)][:, 0:T], ACT.Exp, scale=-1.0).then_inc(sg["h_qexp"], 1)
                    sigmoid(he[:, :], he[:, :], (sg["h_qexp"], i + 1), (sg["h_qden"], i + 1), sg["h_qrec"])
                if s == 16:
                    slab_done(at, 1)
                    act.wait_ge(sg[f"acc_free{at.bank(0)}"], at.drained(0) + 1)
                    f(he[:, :], acc[at.bank(1)][:, 0:T], ACT.Exp,
                      scale=-1.0).then_inc(sg[f"acc_free{at.bank(1)}"], 1)
                    sigmoid(he[:, :], he[:, :], (sg[f"acc_free{at.bank(1)}"], at.drained(1) + 1), (sg["h_fden"], i + 1),
                            sg["h_frec"])
                if s == 19:
                    act.wait_ge(sg["h_f"], i + 1)
                    f(hlf[:, :], hf[:, :], ACT.Ln).then_inc(sg["h_ln"], 1)
                if s == 22:
                    act.wait_ge(sg["h_diff"], i + 1)
                    act.wait_ge(sg["h_new"], 8 * i)
                    act.wait_ge(sg["h_decayed"], i)
                    act.wait_ge(sg["h_decayed_p"], i)
                    f(hE[:, 0, :], hD[:, 0, :], ACT.Exp)
                    f(hE[:, 1, :], hD[:, 0, :], ACT.Exp, scale=-1.0)
                    f(hE[:, 2, :], hG[:, :], ACT.Exp)
                    f(hE[:, 3, :], hD[:, 1, :], ACT.Exp).then_inc(sg["h_e"], 1)
                if s == 24:
                    slab_done(at, 2)
                    act.wait_ge(sg["h_turned"], i)
                    f(hi_[:, :], acc[at.bank(2)][:, 0:T], ACT.Copy).then_inc(sg[f"acc_free{at.bank(2)}"], 1)
                if s == 32:
                    slab_done(at, 3)
                    act.wait_ge(sg["h_f"], i + 1)
                    f(he[:, :], acc[at.bank(3)][:, 0:T], ACT.Exp, scale=-1.0).then_inc(sg["h_gexp"], 1)
                    sigmoid(he[:, :], he[:, :], (sg["h_gexp"], i + 1), (sg["h_gden"], i + 1), sg["h_grec"])

            def hgrn_prev(s, n):
                if s == 1:
                    act.wait_ge(sg["h_turned"], n + 1)
                    act.wait_ge(sg["h_o"], n)
                    f(htok[:, :, :], R[2][:, :].rearrange("p (a d) -> p a d", d=P), ACT.Copy)
                    f(htoks[0:NS, :, :], R[3][0:NS, 0:2 * P].rearrange("p (k d) -> p k d", d=P), ACT.Copy).then_inc(sg["h_tok"], 1)
                if s == 17:
                    act.wait_ge(sg["h_o"], n + 1)
                    act.wait_ge(sg["h_ss"], n)
                    f(hsq[:, :], R[7][:, 0:T], ACT.Square).then_inc(sg["h_sq"], 1)
                if s == 20:
                    act.wait_ge(sg["h_ss"], n + 1)
                    act.wait_ge(sg["h_t1"], n)
                    f(hse[:, :], R[4][:, 0:T], ACT.Ln, scale=1.0 / P, bias=eps[:, :]).then_inc(sg["h_ssln"], 1)
                    act.wait_ge(sg["h_ssln"], n + 1)
                    f(hrs[:, :], hse[:, :], ACT.Exp, scale=-0.5).then_inc(sg["h_rs"], 1)
                if s == 23:
                    act.wait_ge(sg["h_out"], n + 1)
                    f(ohi[:, n, :] if isinstance(n, int) else ohi[:, bass.ds(n, 1), :].squeeze(1), hof[:, :], ACT.Copy).then_inc(sg["h_ohi"], 1)

            def hgrn(at, i, n):
                for s in range(33):
                    if s % 2 == 0 and s < 32:
                        split_hi(at, s // 2)
                    if n is not None:
                        hgrn_prev(s, n)
                    hgrn_own(at, s, i)

            hgrn(At(S_H0), 0, None)
            loop(act, lambda at, n: hgrn(at, n + 1, n), S_H1, 4, HH - 1, apart=1)

            def gate(at, k, g, pairs):
                slab_done(at, k)
                act.wait_ge(sg["t_out"], atleast0(g - 1))
                f(pa[:, k % 2, :], acc[at.bank(k)][:, 0:T], ACT.Exp,
                  scale=-1.0).then_inc(sg[f"acc_free{at.bank(k)}"], 1)
                act.wait_ge(sg[f"t_stored{k % 2}"], 16 * pairs)
                sigmoid(pa[:, k % 2, :], pb[:, k % 2, :], (sg[f"acc_free{at.bank(k)}"], at.drained(k) + 1),
                        (sg["t_den"], g + 1), sg["t_out"])

            for s in range(33):
                if s % 2 == 0 and s < 32:
                    split_hi(At(S_GA0), s // 2)
                hgrn_prev(s, HH - 1)
                if s % 8 == 0 and s > 0:
                    gate(At(S_GA0), s // 8 - 1, s // 8 - 1, (s // 8 - 1) // 2)

            def gates(first, m0):
                def body(at, n):
                    for k in range(2):
                        slab_hi(at, k)
                        gate(at, k, first + 2 * n + k, m0 // 2 + n)
                return body
            loop(act, gates(4, 4), S_GA1, 2, (KT - 4) // 2)

            def only_hi(at, n):
                for k in range(2):
                    slab_hi(at, k)
            loop(act, only_hi, S_WA, 2, KT // 2)

            def delta_own(at, s, j):
                if s in (8, 16, 24, 32):
                    k = s // 8 - 1
                    slab_done(at, k)
                    act.wait_ge(sg["g_tail"], j)
                    src = acc[at.bank(k)]
                    f(gU[:, k, 3:3 + TP], src[:, 0:TP], ACT.Copy)
                    f(sample_of(gU[:, k, :], TS)[:, :, 3:], src[:, TP:T].rearrange("p (b t) -> p b t", t=TS),
                      ACT.Copy).then_inc(sg[f"acc_free{at.bank(k)}"], 1)
                if s in (12, 20, 28, 36):
                    k = (s - 12) // 8
                    act.wait_ge(sg["g_tap"], 4 * j + k + 1)
                    act.wait_ge(sg["g_z"], 2 * j)
                    act.wait_ge(sg["g_c"], 4 * j + k)
                    f(gce[:, 0:CW], gca[:, 0:CW], ACT.Exp, scale=-1.0).then_inc(sg["g_cexp"], 1)
                    m = 4 * j + k + 1
                    sigmoid(gce[:, 0:CW], gce[:, 0:CW], (sg["g_cexp"], m), (sg["g_cden"], EARLIER + m), sg["g_crec"])
                if s == 43:
                    act.wait_ge(sg["g_turned"], j + 1)
                    for a in range(3):
                        m = P if a < 2 else NS
                        for k in range(2):
                            last = f(gjunk[0:m, :], (R[2], R[3], R[5])[a][0:m, k * P:(k + 1) * P], ACT.Square,
                                     accum_out=gss[0:m, 0, a, k:k + 1]).then_inc(sg["g_ss"], 1)
                            act.wait_ge(sg["g_ss"], EARLIER + 6 * j + 2 * a + k + 1)
                    f(gss[:, 1], gss[:, 0], ACT.Ln, bias=eps[:, :]).then_inc(sg["g_ssln"], 1)
                    act.wait_ge(sg["g_ssln"], EARLIER + j + 1)
                    f(gss[:, 2], gss[:, 1], ACT.Exp, scale=-0.5).then_inc(sg["g_rs"], 1)
                    act.wait_ge(sg["g_tail_turned"], j + 1)
                    act.wait_ge(sg["g_tail_stored"], 96 * j)
                    f(gto[:, :, :], R[6][0:27, :].rearrange("p (k d) -> p k d", d=P), ACT.Copy).then_inc(sg["g_tail_out"], 1)
                if s == 45:
                    act.wait_ge(sg["g_tokqk"], EARLIER + j + 1)
                    act.wait_ge(sg["g_o"], j)
                    act.wait_ge(sg["g_ds"], 4 * j)
                    for a in range(3):
                        m = P if a < 2 else NS
                        for e in range(2):
                            last = f(gqp[0:m, a, e, :], gtq[0:m, a, :], ACT.Copy, scale=gsc[0:m, e, 3 + a:4 + a])
                    last.then_inc(sg["g_qp"], 1)
                if s in (42, 48):
                    k = (s - 42) // 6
                    slab_done(at, 4 + k)
                    act.wait_ge(sg["g_c"], 4 * j + 4)
                    act.wait_ge(sg["g_z"], 2 * j + k)
                    f(gce[:, 0:T], acc[at.bank(4 + k)][:, 0:T], ACT.Exp, scale=-1.0).then_inc(sg["g_zexp"], 1)
                if s == 46:
                    sigmoid_z(2 * j + 1)

            def sigmoid_z(m):
                sigmoid(gce[:, 0:T], gce[:, 0:T], (sg["g_zexp"], m), (sg["g_zden"], EARLIER + m), sg["g_zrec"])

            VN = (26, *WS)

            def delta_prev(s, n, slot):
                if s == 0:
                    act.wait_ge(sg["g_qk_turned"], n + 1)
                    f(gqT[:, :], R[7][:, 0:T], ACT.Copy)
                    f(gkT[:, :], R[4][:, 0:T], ACT.Copy).then_inc(sg["g_qkt"], 1)
                    for e in range(2):
                        bank = (R[6], R[5])[e]
                        f(gqpT[:, e, :], bank[:, 0:TP], ACT.Copy)
                        last = f(gQW[:, e, :, 0, :], bank[:, TP:T].rearrange("p (b t) -> p b t", t=TS), ACT.Copy)
                    last.then_inc(sg["g_qpt"], 1)
                if s == 2:
                    act.wait_ge(sg["g_d"], EARLIER + n + 1)
                    for a in range(2):
                        f(gGR[:, a].rearrange("p k e s -> p (k e s)"), R[2 + a][:, :], ACT.Exp)
                    f(gGRs[:, :].rearrange("p k e s -> p (k e s)"), R[5][0:NS, 0:128], ACT.Exp).then_inc(sg["g_ex"], 1)
                if s == 4:
                    sigmoid_z(2 * n + 2)
                if s in PU:
                    l = PU.index(s) + 1
                    act.wait_ge(sg["g_pu"], 5 * n + l)
                    last = f(gPU[:, :, :], R[3][:, :].rearrange("p (q s) -> p q s", s=P), ACT.Copy)
                    if l == 1:
                        last = f(gPUs[:, :, :], R[5][0:NS, 0:2 * NS].rearrange("p (e s) -> p e s", s=NS), ACT.Copy)
                    last.then_inc(sg["g_pucp"], 1)
                if s == 12:
                    act.wait_ge(sg["g_uts"], EARLIER + n + 1)
                    f(gQW[:, :, :, 1, :], R[7][:, 0:2 * NS].rearrange("p (e b t) -> p e b t", e=2, t=TS), ACT.Copy,
                      scale=-1.0).then_inc(sg["g_qw"], 1)
                if s == 14:
                    act.wait_ge(sg["g_sw"], n + 1)
                    act.wait_ge(sg["g_oadd"], EARLIER + n)
                    f(gqws[:, :].rearrange("p e b k t -> p (e b k t)"), R[4][:, 0:128], ACT.Copy).then_inc(sg["g_qws"], 1)
                if s == 17:
                    act.wait_ge(sg["g_vtt"], n + 1)
                    f(gvns[:, :, :], R[5][0:NS, 0:2 * P].rearrange("p (e v) -> p e v", v=P), ACT.Copy).then_inc(sg["g_vns"], 1)
                if s == 26:
                    act.wait_ge(sg["g_w"], n + 1)
                    f(gPU[:, :, :], R[3][:, :].rearrange("p (q s) -> p q s", s=P), ACT.Copy, scale=-1.0).then_inc(sg["g_wcp"], 1)
                if s in VN:
                    c = VN.index(s)
                    act.wait_ge(sg["g_ws"], 3 * n + c)
                    a, r0 = c // 2, GC * (c % 2)
                    f(gvn[r0:r0 + GC, a], (R[2], R[6])[a][r0:r0 + GC, 0:2 * P].rearrange("p (e v) -> p e v", v=P),
                      ACT.Copy).then_inc(sg["g_vn"], 1)
                if s == 42:
                    act.wait_ge(sg["g_o"], n + 1)
                    act.wait_ge(sg["g_out"], EARLIER + n)
                    for e in range(2):
                        last = f(go[:, e, 0:TP], (R[7], R[4])[e][:, 0:TP], ACT.Copy)
                    last.then_inc(sg["g_ocp"], 1)
                    act.wait_ge(sg["g_oadd"], EARLIER + n + 1)
                    f(gn1[:, :, :], go[:, :, :], ACT.Square).then_inc(sg["g_osq"], 1)
                if s == 44:
                    act.wait_ge(sg["g_oss"], n + 1)
                    act.wait_ge(sg["g_olo"], n)
                    for e in range(2):
                        f(gn2[:, e, :], (R[7], R[4])[e][:, 0:T], ACT.Ln, scale=1.0 / P, bias=eps[:, :]).then_inc(sg["g_ossln"], 1)
                    act.wait_ge(sg["g_ossln"], 2 * n + 2)
                    f(gn1[:, :, :], gn2[:, :, :], ACT.Exp, scale=-0.5).then_inc(sg["g_ors"], 1)
                if s == 47:
                    act.wait_ge(sg["g_out"], EARLIER + n + 1)
                    f(ohi[:, bass.ds(2 * slot, 2), :] if not isinstance(slot, int) else ohi[:, 2 * slot:2 * slot + 2, :],
                      gn2[:, :, :], ACT.Copy).then_inc(sg["g_ohi"], 1)

            def delta(at, j, n, slot):
                for s in range(49):
                    if n is not None:
                        delta_prev(s, n, slot)
                    delta_own(at, s, j)
                    if s % 2 == 0 and s < 48:
                        split_hi(at, s // 2)

            act.wait_ge(sg["g_zero"], 1)
            delta(At(S_G0), 0, None, None)
            loop(act, lambda at, n: delta(at, n + 1, n, n), S_G1, 6, HALF, apart=1)

            def first_half(at, n):
                for k in range(2):
                    slab_hi(at, k)
                    slab_done(at, k)
                    act.wait_ge(sg[f"t_stored{k}"], 16 * (M_WB1 // 2 + n))
                    f(pb[:, k, :], acc[at.bank(k)][:, 0:T], ACT.Copy).then_inc(sg[f"acc_free{at.bank(k)}"], 1)
            loop(act, first_half, S_WB1, 2, KT // 2)
            loop(act, lambda at, n: delta(at, n + 1 + HALF, n + HALF, n), S_G2, 6, GJ - 1 - HALF)
            for s in range(49):
                if s % 2 == 0 and s < 48:
                    split_hi(At(S_GB0), s // 2)
                delta_prev(s, GJ - 1, HALF - 1)
                if s % 8 == 0 and s > 0:
                    gate(At(S_GB0), s // 8 - 1, KT + s // 8 - 1, M_GB // 2 + (s // 8 - 1) // 2)
            loop(act, gates(KT + 6, M_GB + 6), S_GB1, 2, (KT - 6) // 2)

            def both(at, n):
                for k in range(2):
                    slab_hi(at, k)
                    act.wait_ge(sg["t_s3"], 2 * n + k + 1)
                    f(mhi[:, bass.ds(2 * n + k, 1), :].squeeze(1), tt[:, k, :], ACT.Copy).then_inc(sg["m_hi"], 1)
            loop(act, both, S_WB2, 2, KT // 2)

            def block_of(t, n, k):
                return t[:, bass.ds(2 * n + k, 1), :].squeeze(1)

            def mixed(at, n):
                for k in range(2):
                    slab_hi(at, k)
                    slab_done(at, k)
                    act.wait_ge(sg["w_sum"], 2 * n)
                    f(block_of(mix, n, k), acc[at.bank(k)][:, 0:T], ACT.Copy)
                    f(tt[:, k, :], acc[at.bank(k)][:, 0:T], ACT.Square).then_inc(sg[f"acc_free{at.bank(k)}"], 1)
            loop(act, mixed, S_WO, 2, KT // 2, apart=1)

            def norm(v):
                act.wait_ge(sg["w_ss"], v)
                act.wait_ge(sg["w_t1"], EARLIER + KT * (v - 1))
                f(tsum2[:, :], R[2][:, 0:T], ACT.Ln, scale=1.0 / D, bias=eps[:, :]).then_inc(sg["w_ln"], 1)
                act.wait_ge(sg["w_ln"], v)
                f(trs[:, :], tsum2[:, :], ACT.Exp, scale=-0.5).then_inc(sg["w_rs"], 1)

            norm(1)
            def residual_squares(n):
                for k in range(2):
                    act.wait_ge(sg["w_h"], 2 * n + k + 1)
                    act.wait_ge(sg["w_sum"], KT + 2 * n)
                    f(tt[:, k, :], block_of(res, n, k), ACT.Square).then_inc(sg["w_hsq"], 1)
            repeat(act, residual_squares, KT // 2)
            norm(2)
            with act.Fori(0, KT // 2) as n:
                for k in range(2):
                    act.wait_ge(sg["b_tmp"], EARLIER + 2 * n + k + 1)
                    f(block_of(ahi, n, k), tin[:, k, 1, :], ACT.Copy).then_inc(sg["b_hi"], 1)

            def up(g):
                with act.Fori(0, KT // 2) as n:
                    at = At(S_FF, n + g * KT, 2)
                    for k in range(2):
                        slab_hi(at, k)
                        slab_done(at, k)
                        act.wait_ge(sg["f_sq"], EARLIER + g * KT + 2 * n)
                        f(tt[:, k, :], acc[at.bank(k)][:, 0:T], ACT.Relu).then_inc(sg[f"acc_free{at.bank(k)}"], 1)
                        act.wait_ge(sg["f_sq"], EARLIER + g * KT + 2 * n + k + 1)
                        f(block_of(ohi, n, k), tu[:, k, :], ACT.Copy).then_inc(sg["f_hi"], 1)

            with act.Fori(0, FG - 1) as g:
                up(g)
                with act.Fori(0, KT // 2) as n:
                    for k in range(2):
                        slab_hi(At(S_FF, n + g * KT + KT // 2, 2), k)
            up(FG - 1)
            with act.Fori(0, KT // 2) as n:
                at = At(S_FF, n + FG * KT - KT // 2, 2)
                for k in range(2):
                    slab_hi(at, k)
                    act.wait_ge(sg[f"acc_free{at.bank(k)}"], at.drained(k) + 1)
                    act.wait_ge(sg["w_sum"], 2 * KT + 2 * n + k - 1)
                    f(tt[:, k, :], block_of(mix, n, k), ACT.Square).then_inc(sg["w_hsq"], 1)
            norm(3)
            def result_out(n):
                for k in range(2):
                    act.wait_ge(sg["y_turned"], 2 * n + k + 1)
                    act.wait_ge(sg["y_stored"], 64 * n)
                    f(ytok[:, k, 0:2, :], R[3 + k][:, 0:TP].rearrange("p (a d) -> p a d", d=P), ACT.Copy)
                    f(ytok[0:NS, k, 2, :], R[3 + k][0:NS, TP:TP + P], ACT.Copy).then_inc(sg["y_out"], 1)

            repeat(act, result_out, KT // 2)
        @block.vector
        def _(dve):
            ts, tt_, stt, rec = nc.vector.tensor_scalar, nc.vector.tensor_tensor, nc.vector.scalar_tensor_tensor, nc.vector.reciprocal
            copy = nc.vector.tensor_copy
            MUL, ADD, SUB = ALU.mult, ALU.add, ALU.subtract
            steps = [0]

            def step(ins):
                steps[0] += 1
                ins.then_inc(sg["pro_dve"], 1)
                dve.wait_ge(sg["pro_dve"], steps[0])

            nc.vector.memset(rows[:, :, :], 0.0)
            nc.vector.memset(xss[:, :, :], 1.0).then_inc(sg["rows_zeroed"], 1)
            nc.vector.memset(tab[:, :, :], 0.0)
            dve.wait_ge(sg["vec_turned"], 1)
            copy(vec[:, :, :], R[2][:, :].rearrange("p (q c) -> p q c", c=P)).then_inc(sg["vec_made"], 1)
            dve.wait_ge(sg["vec_made"], 1)
            l0, l1 = vec[:, 0, 4 * KT:5 * KT], vec[:, 0, 5 * KT:6 * KT]
            step(tt_(lbx[:, 4, :], l0, l1, ALU.max))
            step(tt_(lbx[:, 0, :], l0, lbx[:, 4, :], SUB))
            tt_(lbx[:, 1, :], l1, lbx[:, 4, :], SUB).then_inc(sg["lb_diff"], 1)
            dve.wait_ge(sg["c_exp"], 1)
            step(ts(ce[:, 1, :], ce[:, 0, :], 1.0, None, ADD))
            step(rec(ce[:, 2, :], ce[:, 1, :]))
            tt_(cst[:, :, 0], R[3][:, 0:KT], ce[:, 2, 0:KT], MUL)
            tt_(cst[:, :, 1:NC], R[3][:, P:2 * P].rearrange("p (b k) -> p k b", k=KT),
                ce[:, 2, 16:16 + P].rearrange("p (b k) -> p k b", k=KT), MUL).then_inc(sg["cs_made"], 1)
            dve.wait_ge(sg["lb_exp"], 1)
            step(tt_(lbx[:, 4, :], lbx[:, 2, :], lbx[:, 3, :], ADD))
            step(rec(lbx[:, 5, :], lbx[:, 4, :]))
            step(tt_(lbt[:, :, 0], lbx[:, 2, :], lbx[:, 5, :], MUL))
            step(ts(lbt[:, :, 1], lbt[:, :, 0], -1.0, 1.0, MUL, ADD))
            dve.wait_ge(sg["x_rs"], 1)
            for a in range(2):
                ts(xtok[:, a, :], xtok[:, a, :], xss[:, 2, a:a + 1], None, MUL)
            ts(xs[:, :], xs[:, :], xss[0:NS, 2, 2:3], None, MUL).then_inc(sg["x_scaled"], 1)
            def ada(n):
                for k in range(2):
                    c = 2 * n + k
                    dve.wait_ge(sg["ada_turned"], c + 1)
                    tt_(mod[:, bass.ds(4 * c, 4), :], R[6 + k][:, 0:4 * NC].rearrange("p (q v) -> p q v", v=NC),
                        vec[:, 1, bass.ds(4 * c, 4)].unsqueeze(2).to_broadcast([P, 4, NC]), ADD).then_inc(sg["ada_free"], 1)
            repeat(dve, ada, ADA_BLOCKS // 2)
            dve.wait_ge(sg["ada_free"], ADA_BLOCKS)
            for g, j in ((0, 1), (2, 4)):
                step(ts(mod[:, j * KT:(j + 1) * KT, :], mod[:, j * KT:(j + 1) * KT, :], 1.0, None, ADD))
            for g, j in ((0, 1), (1, 2), (2, 4), (3, 5)):
                m = mod[:, j * KT:(j + 1) * KT, :]
                step(tt_(m, m, vec[:, 0, g * KT:(g + 1) * KT].unsqueeze(2).to_broadcast([P, KT, NC]), MUL))

            def modulate(out, src, scale, shift, inner, last):
                po, so = halves(out)
                ps_, ss_ = halves(src)
                ts(po, ps_, scale(0), shift(0), MUL, ADD)
                tt_(so, ss_, scale(1), MUL).then_inc(sg[inner[0]], 1)
                dve.wait_ge(sg[inner[0]], inner[1])
                tt_(so, so, shift(1), ADD).then_inc(sg[last], 1)

            def mods(j):
                return lambda part: mod[:, j, 0:1] if part == 0 else mod[:, j, 1:NC].unsqueeze(2).to_broadcast([P, NB, TS])

            for j in range(KT):
                dve.wait_ge(sg["x_turned"], j + 1)
                dve.wait_ge(sg["a_hi"], max(j - 1, 0))
                steps[0] += 1
                modulate(atmp[:, j % 2, :], R[2 + j % 4][:, 0:T], mods(KT + j), mods(j), ("pro_dve", steps[0]), "a_tmp")
                dve.wait_ge(sg["a_hi"], j + 1)
                tt_(alo[:, j, :], atmp[:, j % 2, :], ahi[:, j, :].bitcast(F32), SUB).then_inc(sg["a_lo"], 1)

            def split_lo(at, k):
                k += AHEAD
                s, r = at.slot(k, SPLIT), at.slot(k, RAW)
                dve.wait_ge(sg["hi_made"], at.pieces_before(k) + 1)
                dve.wait_ge(sg["piece_used"], atleast0(at.pieces_before(k) - SPLIT + 1))
                tt_(wlo[:, s], raw[:, r], whi[:, s].bitcast(F32), SUB).then_inc(sg["lo_made"], 1)

            def slab_lo(at, k):
                for q in range(4):
                    split_lo(at, 4 * k + q)

            def drained(at, k):
                dve.wait_ge(sg[f"acc_free{at.bank(k)}"], at.drained(k) + 1)

            for k in range(AHEAD):
                split_lo(At(S_BG), k - AHEAD)
            slab_lo(At(S_BG), 0)

            lo_, hi2 = slice(0, GH), slice(GH, 2 * GH)
            dve.wait_ge(sg["beta_exp"], 1)
            dve.wait_ge(sg["small_in"], 32)
            step(ts(bg[lo_, 2, :], bg[lo_, 1, :], 1.0, None, ADD))
            step(rec(bg[lo_, 0, :], bg[lo_, 2, :]))
            ts(bg[hi2, 1, :], acc[0][hi2, 0:T], bgc[hi2, 0:1], None, ADD).then_inc(sg["acc_free0"], 1)
            dve.wait_ge(sg["acc_free0"], 1)
            dve.wait_ge(sg["soft_exp"], 2)
            ts(bg[hi2, 4, :], bg[hi2, 3, :], 1.0, None, ADD).then_inc(sg["soft_den"], 1)
            dve.wait_ge(sg["soft_ln"], 1)
            step(ts(bg[hi2, 3, :], bg[hi2, 1, :], 0.0, None, ALU.max))
            step(tt_(bg[hi2, 4, :], bg[hi2, 3, :], bg[hi2, 2, :], ADD))
            ts(bg[hi2, 0, :], bg[hi2, 4, :], bgc[hi2, 2:3], -1.0, MUL, MUL).then_inc(sg["bg_made"], 1)
            dve.wait_ge(sg["bg_turned"], 1)
            step(copy(bgT[:, 0:2, :], R[4][:, 0:128].rearrange("p (a h) -> p a h", h=2 * GH)))
            step(copy(bgT[0:NS, 2, :], R[4][0:NS, 128:192]))
            for a in range(2):
                for c in range(2):
                    ts(gx[:, a, c, :], bgT[:, a, GH:2 * GH], cm64[:, c:c + 1], None, MUL)
            for b in range(NB):
                last = ts(gxs[:, b, :], bgT[0:NS, 2, GH:2 * GH], cm4[:, b:b + 1], None, MUL)
            last.then_inc(sg["bg_taken"], 1)
            dve.wait_ge(sg["chunk_exp"], 1)
            for a in range(3):
                m = P if a < 2 else NS
                sums = bgs[:, 0:128].rearrange("p (k a h) -> p k a h", k=2, a=2)[:, :, a] if a < 2 else \
                    bgs[0:NS, 128:192].rearrange("p (k h) -> p k h", k=2)
                copy(tab[0:m, :, a], bgT[0:m, a, 0:GH])
                copy(tab[0:m, :, 12 + a], bgT[0:m, a, GH:2 * GH])
                for k in range(2):
                    copy(tab[0:m, :, 3 + 3 * k + a], sums[:, k])
                step(tt_(tab[0:m, :, 9 + a], bgT[0:m, a, 0:GH], sums[:, 0], MUL))
            copy(tab[:, :, 15:27], bgs[:, 192:576].rearrange("p (c h) -> p h c", h=GH)).then_inc(sg["tab_made"], 1)
            dve.wait_ge(sg["tab_made"], 1)
            for rows_ in (slice(NS, 2 * NS), slice(2 * NS, P)):
                nc.vector.memset(hiXs[rows_, :, :], 0.0)
                last = nc.vector.memset(htoks[rows_, :, :], 0.0)
            last.then_inc(sg["tab_made"], 1)

            def at_chunk(ap, which):
                p_, s_ = ap[:, 0:TP].rearrange("p (c t) -> p c t", t=HC), ap[:, TP:T].rearrange("p (b t) -> p b t", t=TS)
                kp, ks = (HC // 2, TS // 2) if which == "middle" else (HC - 1, TS - 1)
                return (p_[:, :, kp:kp + 1].to_broadcast([P, NHC, HC]), s_[:, :, ks:ks + 1].to_broadcast([P, NB, TS]))

            def by_chunk(ap):
                return ap[:, 0:TP].rearrange("p (c t) -> p c t", t=HC), ap[:, TP:T].rearrange("p (b t) -> p b t", t=TS)

            def silu(at, k, i, name, out):
                dve.wait_ge(sg[f"h_{name}rec"], i + 1)
                tt_(out, acc[at.bank(k)][:, 0:T], he[:, :], MUL).then_inc(sg[f"acc_free{at.bank(k)}"], 1)

            def hgrn_own(at, s, i):
                if s == 9:
                    dve.wait_ge(sg["h_decayed_p"], i)
                    silu(at, 0, i, "q", hq[:, :])
                    copy(hsc[:, :], lbt[:, i, :] if isinstance(i, int) else lbt[:, bass.ds(i, 1), :].squeeze(1)).then_inc(sg["h_sc"], 1)
                if s == 17:
                    drained(at, 1)
                    dve.wait_ge(sg["h_sc"], i + 1)
                    dve.wait_ge(sg["h_frec"], i + 1)
                    ts(hf[:, :], he[:, :], hsc[:, 1:2], hsc[:, 0:1], MUL, ADD).then_inc(sg["h_f"], 1)
                    dve.wait_ge(sg["h_f"], i + 1)
                    ts(hk[:, :], hf[:, :], -1.0, 1.0, MUL, ADD).then_inc(sg["h_k"], 1)
                if s == 20:
                    dve.wait_ge(sg["h_ln"], i + 1)
                    nc.vector.tensor_tensor_scan(hG[:, :], reset[:, :], hlf[:, :], 0.0, MUL, ADD).then_inc(sg["h_scan"], 1)
                    dve.wait_ge(sg["h_scan"], i + 1)
                    g_, mid, end = by_chunk(hG), at_chunk(hG, "middle"), at_chunk(hG, "end")
                    d0, d1 = by_chunk(hD[:, 0, :]), by_chunk(hD[:, 1, :])
                    for a in range(2):
                        tt_(d0[a], g_[a], mid[a], SUB)
                        last = tt_(d1[a], end[a], g_[a], SUB)
                    last.then_inc(sg["h_diff"], 1)
                if s == 23:
                    dve.wait_ge(sg["h_e"], i + 1)
                    dve.wait_ge(sg["h_o"], i)
                    dve.wait_ge(sg["h_k"], i + 1)
                    tt_(hX[:, 0, :], hq[:, :], hE[:, 0, :], MUL)
                    tt_(hX[:, 1, :], hk[:, :], hE[:, 1, :], MUL).then_inc(sg["h_decayed"], 1)
                if s == 32:
                    silu(at, 3, i, "g", hsg[:, :])

            def hgrn_prev(at, s, n):
                if s == 1:
                    dve.wait_ge(sg["h_turned"], n + 1)
                    dve.wait_ge(sg["h_o"], n)
                    tt_(hAT[:, 0:TP].rearrange("p (a t) -> p a t", a=2), R[4][:, 0:TP].rearrange("p (a t) -> p a t", a=2),
                        hmask[:, :].unsqueeze(1).to_broadcast([P, 2, P]), MUL)
                    tt_(hAT[0:NS, TP:T], R[4][0:NS, TP:T], smask[:, :], MUL).then_inc(sg["h_at"], 1)
                if s == 10:
                    dve.wait_ge(sg["h_ds"], n + 1)
                    dve.wait_ge(sg["h_o"], n)
                    dve.wait_ge(sg["h_stored"], 32 * n)
                    for c in range(NHC):
                        add = R[5 + c // 4][:, (c % 4) * P:(c % 4 + 1) * P]
                        if c == 0:
                            copy(hS[:, 0, :], add).then_inc(sg["h_step"], 1)
                        else:
                            dve.wait_ge(sg["h_step"], 8 * n + c)
                            end = c * HC + HC - 1
                            stt(hS[:, c, :], hS[:, c - 1, :], hE[:, 2, end:end + 1], add, MUL, ADD).then_inc(sg["h_step"], 1)
                    dve.wait_ge(sg["h_s0"], 16 * (n + 1))
                    for b in range(NB):
                        end = TP + b * TS + TS - 1
                        stt(hSn[:, b, :], hS0[:, b, :], hE[:, 2, end:end + 1], R[2 + b // 4][:, (b % 4) * P:(b % 4 + 1) * P],
                            MUL, ADD).then_inc(sg["h_new"], 1)
                if s == 21:
                    dve.wait_ge(sg["h_rs"], n + 1)
                    stt(ht1[:, :], R[7][:, 0:T], vec[:, 0, 6 * KT:6 * KT + 1], hrs[:, :], MUL, MUL).then_inc(sg["h_t1"], 1)
                    dve.wait_ge(sg["h_t1"], n + 1)
                    dve.wait_ge(sg["h_ohi"], n)
                    dve.wait_ge(sg[f"acc_free{at.bank(1)}"], at.drained(1))
                    tt_(hof[:, :], ht1[:, :], hsg[:, :], MUL).then_inc(sg["h_out"], 1)
                if s == 24:
                    dve.wait_ge(sg["h_ohi"], n + 1)
                    o_, h_ = (olo[:, n, :], ohi[:, n, :]) if isinstance(n, int) else \
                        (olo[:, bass.ds(n, 1), :].squeeze(1), ohi[:, bass.ds(n, 1), :].squeeze(1))
                    tt_(o_, hof[:, :], h_.bitcast(F32), SUB).then_inc(sg["h_olo"], 1)

            def hgrn(at, i, n):
                for s in range(33):
                    if s % 2 == 0 and s < 32:
                        split_lo(at, s // 2)
                    if n is not None:
                        hgrn_prev(at, s, n)
                    hgrn_own(at, s, i)

            hgrn(At(S_H0), 0, None)
            loop(dve, lambda at, n: hgrn(at, n + 1, n), S_H1, 4, HH - 1, apart=1)

            for s in range(33):
                if s % 2 == 0 and s < 32:
                    split_lo(At(S_GA0), s // 2)
                hgrn_prev(At(S_GA0), s, HH - 1)

            def only_lo(at, n):
                for k in range(2):
                    slab_lo(at, k)
            loop(dve, only_lo, S_GA1, 2, (KT - 4) // 2)

            def gated(at, n):
                for k in range(2):
                    slab_lo(at, k)
                    dve.wait_ge(sg[f"t_in{k}"], 16 * n + 16)
                    dve.wait_ge(sg[f"t_stored{k}"], 16 * (M_WA // 2 + n))
                    dve.wait_ge(sg["piece_used"], at.pieces_before(4 * k + 4))
                    tt_(pb[:, k, :], acc[at.bank(k)][:, 0:T], pa[:, k, :], MUL).then_inc(sg[f"acc_free{at.bank(k)}"], 1)
            loop(dve, gated, S_WA, 2, KT // 2)

            drained(At(S_WA, KT // 2 - 1, 2), 0)
            drained(At(S_WA, KT // 2 - 1, 2), 1)
            dve.wait_ge(sg["h_olo"], HH)
            dve.wait_ge(sg["h_stored"], 32 * HH)
            nc.vector.memset(gU[:, :, 0:3], 0.0)
            for rows_ in (slice(NS, 2 * NS), slice(2 * NS, P)):
                nc.vector.memset(gvX[rows_, :, :], 0.0)
                nc.vector.memset(gkl[rows_, 2, :, :], 0.0)
            nc.vector.memset(gss[:, :, :, :], 1.0).then_inc(sg["g_zero"], 1)

            def head(t, i, size=1):
                return t[:, i:i + size] if isinstance(i, int) else t[:, bass.ds(i, size)]

            def delta_own(at, s, j):
                if s == 5:
                    for k, (first, mul, size) in enumerate(((0, 1, 1), (GJ, 1, 1), (2 * GJ, 2, 2))):
                        src = taps[:, :, first + j * mul:first + j * mul + size] if isinstance(j, int) else \
                            taps[:, :, bass.ds(first + j * mul, size)]
                        last = copy(gcw[:, k:k + size, :].rearrange("p b a -> p a b"), src)
                    last.then_inc(sg["g_cw"], 1)
                    dve.wait_ge(sg["g_halo_turned"], j + 1)
                    copy(sample_of(gU[:, :, :], 0)[:, :, :, 0:3], R[7][:, 0:96].rearrange("p (c b s) -> p c b s", c=4, b=NB)
                         ).then_inc(sg["g_halo"], 1)
                if s in (10, 18, 26, 34):
                    k = (s - 10) // 8
                    drained(at, k)
                    dve.wait_ge(sg["g_cw"], j + 1)
                    dve.wait_ge(sg["g_halo"], j + 1)
                    dve.wait_ge(sg["g_cexp"], 4 * j + k)
                    dve.wait_ge(sg["g_c"], 4 * j + k)
                    dve.wait_ge(sg["g_z"], 2 * j)
                    ts(gca[:, 0:CW], gU[:, k, 0:CW], gcw[:, k, 0:1], None, MUL).then_inc(sg["g_part"], 1)
                    for a in range(1, 4):
                        dve.wait_ge(sg["g_part"], 3 * (4 * j + k) + a)
                        stt(gca[:, 0:CW], gU[:, k, a:a + CW], gcw[:, k, a:a + 1], gca[:, 0:CW], MUL,
                            ADD).then_inc(sg["g_part" if a < 3 else "g_tap"], 1)
                if s in (13, 21, 29, 37):
                    k = (s - 13) // 8
                    m = 4 * j + k + 1
                    dve.wait_ge(sg["g_crec"], EARLIER + m)
                    dve.wait_ge(sg["g_turned"], j)
                    tt_(gC[:, k, 0:TP], gca[:, 0:TP], gce[:, 0:TP], MUL)
                    tt_(gC[:, k, TP:T].rearrange("p (b t) -> p b t", t=TS), sample_of(gca[:, :], TS)[:, :, 0:TS],
                        sample_of(gce[:, :], TS)[:, :, 0:TS], MUL).then_inc(sg["g_c"], 1)
                if s == 38:
                    dve.wait_ge(sg["g_tail_turned"], j)
                    copy(gtail[:, :, 0:3], gU[:, :, TP:TP + 3])
                    copy(gtail[:, :, 3:27].rearrange("p c (b s) -> p c b s", s=3), sample_of(gU[:, :, :], 0)[:, :, :, 4:7]
                         ).then_inc(sg["g_tail"], 1)
                if s == 41:
                    dve.wait_ge(sg["g_sdec"], 2 * j)
                    dve.wait_ge(sg["g_st"], 4 * j)
                    dve.wait_ge(sg["g_tokd"], EARLIER + j)
                    copy(gsc[:, :, :], head(tab, 2 * j, 2)).then_inc(sg["g_sc"], 1)
                if s == 44:
                    dve.wait_ge(sg["g_rs"], EARLIER + j + 1)
                    dve.wait_ge(sg["g_sc"], EARLIER + j + 1)
                    dve.wait_ge(sg["g_qk_turned"], j)
                    for a in range(3):
                        m, bank = (P if a < 2 else NS), (R[2], R[3], R[5])[a]
                        ts(gtq[0:m, a, :], bank[0:m, 0:P], gss[0:m, 2, a, 0:1], QSCALE, MUL, MUL)
                        last = ts(gtk[0:m, a, :], bank[0:m, P:2 * P], gss[0:m, 2, a, 1:2], None, MUL)
                    last.then_inc(sg["g_tokqk"], 1)
                    for a in range(3):
                        m, bank = (P if a < 2 else NS), (R[2], R[3], R[5])[a]
                        for e in range(2):
                            last = ts(gbv[0:m, a, e, :], bank[0:m, (2 + e) * P:(3 + e) * P], gsc[0:m, e, a:a + 1], None, MUL)
                    last.then_inc(sg["g_tokv"], 1)
                if s in (42, 48):
                    k = (s - 42) // 6
                    m = 2 * j + k + 1
                    dve.wait_ge(sg["g_zexp"], m)
                    dve.wait_ge(sg["g_c"], 4 * j + 4)
                    dve.wait_ge(sg["g_z"], 2 * j + k)
                    copy(gca[:, 0:T], acc[at.bank(4 + k)][:, 0:T]).then_inc(sg[f"acc_free{at.bank(4 + k)}"], 1)
                    drained(at, 4 + k)
                if s == 46:
                    dve.wait_ge(sg["g_out"], EARLIER + j)
                    silu_z(2 * j + 1, 0)

            def silu_z(m, k):
                dve.wait_ge(sg["g_zrec"], EARLIER + m)
                tt_(gz[:, k, :], gca[:, 0:T], gce[:, 0:T], MUL).then_inc(sg["g_z"], 1)

            def delta_prev(s, n, slot):
                if s == 4:
                    dve.wait_ge(sg["g_kk"], EARLIER + n + 1)
                    dve.wait_ge(sg["g_lev"], 6 * n)
                    dve.wait_ge(sg["g_attn"], n)
                    for a in range(2):
                        for e in range(2):
                            stt(gA[:, 2 * a + e, :], gGR[:, a, 0, e, :], gsc[:, e, a:a + 1], R[6][:, 2 * a * P:(2 * a + 1) * P], MUL, MUL)
                    for e in range(2):
                        last = stt(gAs[:, e, :], gGRs[:, 0, e, :], gsc[0:NS, e, 2:3], R[5][0:NS, 128:160], MUL, MUL)
                    last.then_inc(sg["g_a"], 1)
                    for a in range(2):
                        tt_(gQKm[:, a, :], R[6][:, (2 * a + 1) * P:(2 * a + 2) * P], m_incl[:, :], MUL)
                    tt_(gQKms[:, :], R[5][0:NS, 160:192], smask[:, :], MUL).then_inc(sg["g_qkm"], 1)
                if s == 5:
                    silu_z(2 * n + 2, 1)
                if s == 7:
                    dve.wait_ge(sg["g_l1"], EARLIER + n + 1)
                    tt_(gUi[:, :, :], ident[:, :].unsqueeze(1).to_broadcast([P, 4, P]), R[2][:, :].rearrange("p (q s) -> p q s", s=P), SUB)
                    tt_(gUs[:, :, :], ident[0:NS, 0:NS].unsqueeze(1).to_broadcast([NS, 2, NS]),
                        R[4][0:NS, 0:2 * NS].rearrange("p (e s) -> p e s", s=NS), SUB).then_inc(sg["g_u1"], 1)
                if s in UT:
                    l = UT.index(s) + 1
                    dve.wait_ge(sg["g_ut"], 5 * n + l)
                    dve.wait_ge(sg["g_u1"], EARLIER + n + 1)
                    dve.wait_ge(sg["g_t1"], n + 1)
                    dve.wait_ge(sg["g_unew"], 5 * n + l - 1)
                    if l == 1:
                        tt_(gUs[:, :, :], gUs[:, :, :], R[4][0:NS, 0:2 * NS].rearrange("p (e s) -> p e s", s=NS), SUB)
                    tt_(gUi[:, :, :], gUi[:, :, :], R[2][:, :].rearrange("p (q s) -> p q s", s=P), SUB).then_inc(sg["g_unew"], 1)
                    if l < 5:
                        dve.wait_ge(sg["g_tnew"], 4 * n + l - 1)
                        tt_(gT[:, :, :], gT[:, :, :], R[6][:, :].rearrange("p (q s) -> p q s", s=P), SUB).then_inc(sg["g_tnew"], 1)
                if s == 15:
                    dve.wait_ge(sg["g_qws"], n + 1)
                    tt_(guTs[:, :, :].rearrange("p e (b t) -> p e b t", t=TS), R[7][:, 64:128].rearrange("p (e b t) -> p e b t", e=2, t=TS),
                        gqws[:, :, :, 1, :], ADD).then_inc(sg["g_vt"], 1)
                if s in (21, 25):
                    e = (s - 21) // 4
                    dve.wait_ge(sg["g_dss"], 2 * n + e + 1)
                    dve.wait_ge(sg["g_sdec"], 2 * n + e + 1)
                    for a in range(2):
                        h_ = gS0[:, e, 4 * a:4 * a + 4, :]
                        last = tt_(h_, h_, R[4 + a][:, :].rearrange("p (b v) -> p b v", v=P), ADD)
                    last.then_inc(sg["g_snew"], 1)
                if s in DS:
                    c = DS.index(s)
                    dve.wait_ge(sg["g_ds"], 4 * n + c + 1)
                    dve.wait_ge(sg["g_o"], n)
                    dve.wait_ge(sg["g_stored"], 16 * n)
                    dve.wait_ge(sg["g_st"], 4 * n + c)
                    for e in range(2):
                        add = R[5][:, 2 * P * (c % 2) + e * P:2 * P * (c % 2) + (e + 1) * P]
                        if c == 0:
                            last = copy(gS[:, 0, e, :], add)
                        else:
                            last = stt(gS[:, c, e, :], gS[:, c - 1, e, :], gsc[:, e, 15 + c:16 + c], add, MUL, ADD)
                    last.then_inc(sg["g_st"], 1)
                if s == 42:
                    dve.wait_ge(sg["g_ocp"], EARLIER + n + 1)
                    for e in range(2):
                        last = tt_(go[:, e, TP:T].rearrange("p (b t) -> p b t", t=TS),
                                   (R[7], R[4])[e][:, TP:T].rearrange("p (b t) -> p b t", t=TS), gqws[:, e, :, 0, :], ADD)
                    last.then_inc(sg["g_oadd"], 1)
                if s == 46:
                    dve.wait_ge(sg["g_ors"], n + 1)
                    dve.wait_ge(sg["g_ohi"], n)
                    dve.wait_ge(sg["g_oadd"], EARLIER + n + 1)
                    dve.wait_ge(sg["g_z"], 2 * (n + 1))
                    stt(go[:, :, :], go[:, :, :], vec[:, 0, 6 * KT + 1:6 * KT + 2], gn1[:, :, :], MUL, MUL).then_inc(sg["g_ot1"], 1)
                    dve.wait_ge(sg["g_ot1"], EARLIER + n + 1)
                    tt_(gn2[:, :, :], go[:, :, :], gz[:, :, :], MUL).then_inc(sg["g_out"], 1)
                if s == 47:
                    dve.wait_ge(sg["g_ohi"], n + 1)
                    tt_(head(olo, 2 * slot, 2), gn2[:, :, :], head(ohi, 2 * slot, 2).bitcast(F32), SUB).then_inc(sg["g_olo"], 1)

            def delta(at, j, n, slot):
                for s in range(49):
                    if n is not None:
                        delta_prev(s, n, slot)
                    delta_own(at, s, j)
                    if s % 2 == 0 and s < 48:
                        split_lo(at, s // 2)

            dve.wait_ge(sg["g_zero"], 1)
            dve.wait_ge(sg["tab_made"], 1)
            delta(At(S_G0), 0, None, None)
            loop(dve, lambda at, n: delta(at, n + 1, n, n), S_G1, 6, HALF, apart=1)

            loop(dve, only_lo, S_WB1, 2, KT // 2)
            loop(dve, lambda at, n: delta(at, n + 1 + HALF, n + HALF, n), S_G2, 6, GJ - 1 - HALF)
            for s in range(49):
                if s % 2 == 0 and s < 48:
                    split_lo(At(S_GB0), s // 2)
                delta_prev(s, GJ - 1, HALF - 1)
            loop(dve, only_lo, S_GB1, 2, (KT - 6) // 2)

            def block_of(t, n, k):
                return t[:, bass.ds(2 * n + k, 1), :].squeeze(1)

            def both(at, n):
                for k in range(2):
                    slab_lo(at, k)
                    m = 2 * n + k
                    dve.wait_ge(sg[f"t_in{k}"], 8 * KT + 48 * n + 48)
                    dve.wait_ge(sg["piece_used"], at.pieces_before(4 * k + 4))
                    tt_(tu[:, k, :], acc[at.bank(k)][:, 0:T], tin[:, k, 1, :], ADD).then_inc(sg[f"acc_free{at.bank(k)}"], 1)
                    drained(at, k)
                    tt_(tu[:, k, :], tu[:, k, :], tin[:, k, 2, :], MUL).then_inc(sg["t_s2"], 1)
                    dve.wait_ge(sg["t_s2"], m + 1)
                    tt_(tt[:, k, :], tu[:, k, :], tin[:, k, 0, :], ADD).then_inc(sg["t_s3"], 1)
                    dve.wait_ge(sg["m_hi"], m + 1)
                    tt_(block_of(mlo, n, k), tt[:, k, :], block_of(mhi, n, k).bitcast(F32), SUB).then_inc(sg["m_lo"], 1)
            dve.wait_ge(sg["g_stored"], 16 * GJ)
            loop(dve, both, S_WB2, 2, KT // 2)

            def clear_sum(v):
                dve.wait_ge(sg["w_ss"], v)
                nc.vector.memset(tsum[:, :], 0.0).then_inc(sg["w_clear"], 1)

            clear_sum(0)

            def add_square(total, k):
                dve.wait_ge(sg["w_sum"], total)
                tt_(tsum[:, :], tsum[:, :], tt[:, k, :], ADD).then_inc(sg["w_sum"], 1)

            dve.wait_ge(sg["w_clear"], 1)

            def mixed(at, n):
                for k in range(2):
                    slab_lo(at, k)
                    drained(at, k)
                    add_square(2 * n + k, k)
            loop(dve, mixed, S_WO, 2, KT // 2, apart=1)
            clear_sum(1)
            dve.wait_ge(sg["w_clear"], 2)
            dve.wait_ge(sg["w_rs"], 1)
            def wide(v):
                return v[:, 1:NC].unsqueeze(2).to_broadcast([P, NB, TS])

            def mod_of(j, m):
                return mod[:, bass.ds(j * KT + m, 1), :].squeeze(1)

            def residual(n):
                for k in range(2):
                    dve.wait_ge(sg["w_h"], 2 * n)
                    tt_(tu[:, k, :], block_of(mix, n, k), trs[:, :], MUL).then_inc(sg["w_t1"], 1)
                for k in range(2):
                    m = 2 * n + k
                    dve.wait_ge(sg["w_xturned"], m + 1)
                    dve.wait_ge(sg["w_t1"], EARLIER + m + 1)
                    up, us = halves(tu[:, k, :])
                    rp, _rs = halves(block_of(res, n, k))
                    stt(rp, up, mod_of(2, m)[:, 0:1], R[3 + k][:, 0:TP], MUL, ADD)
                    tt_(us, us, wide(mod_of(2, m)), MUL).then_inc(sg["w_t2"], 1)
                for k in range(2):
                    m = 2 * n + k
                    dve.wait_ge(sg["w_t2"], m + 1)
                    us, rs_ = halves(tu[:, k, :])[1], halves(block_of(res, n, k))[1]
                    tt_(rs_, us, halves(R[3 + k][:, 0:T])[1], ADD).then_inc(sg["w_h"], 1)
                if not (isinstance(n, int) and n == 0):
                    add_pair(KT, n - 1)

            def add_pair(before, n):
                for k in range(2):
                    dve.wait_ge(sg["w_hsq"], before - KT + 2 * n + k + 1)
                    add_square(before + 2 * n + k, k)

            repeat(dve, residual, KT // 2)
            add_pair(KT, KT // 2 - 1)
            clear_sum(2)
            dve.wait_ge(sg["w_clear"], 3)
            dve.wait_ge(sg["w_rs"], 2)
            def feed_lo(n):
                for k in range(2):
                    dve.wait_ge(sg["b_hi"], 2 * n + k + 1)
                    tt_(block_of(alo, n, k), tin[:, k, 1, :], block_of(ahi, n, k).bitcast(F32), SUB).then_inc(sg["b_lo"], 1)

            def feed_input(n):
                for k in range(2):
                    dve.wait_ge(sg["b_tmp"], EARLIER + 2 * n)
                    tt_(tin[:, k, 0, :], block_of(res, n, k), trs[:, :], MUL).then_inc(sg["w_t1"], 1)
                if not (isinstance(n, int) and n == 0):
                    feed_lo(n - 1)
                    dve.wait_ge(sg["b_lo"], 2 * n)
                for k in range(2):
                    m = 2 * n + k
                    dve.wait_ge(sg["w_t1"], EARLIER + KT + m + 1)
                    ip, is_ = halves(tin[:, k, 0, :])
                    ts(halves(tin[:, k, 1, :])[0], ip, mod_of(4, m)[:, 0:1], mod_of(3, m)[:, 0:1], MUL, ADD)
                    tt_(is_, is_, wide(mod_of(4, m)), MUL).then_inc(sg["w_t2"], 1)
                for k in range(2):
                    m = 2 * n + k
                    dve.wait_ge(sg["w_t2"], KT + m + 1)
                    tt_(halves(tin[:, k, 1, :])[1], halves(tin[:, k, 0, :])[1], wide(mod_of(3, m)), ADD).then_inc(sg["b_tmp"], 1)

            repeat(dve, feed_input, KT // 2)
            feed_lo(KT // 2 - 1)
            nc.vector.memset(mix[:, :, :], 0.0).then_inc(sg["w_clear"], 1)
            dve.wait_ge(sg["w_clear"], 4)

            def up(g):
                with dve.Fori(0, KT // 2) as n:
                    at = At(S_FF, n + g * KT, 2)
                    for k in range(2):
                        slab_lo(at, k)
                        drained(at, k)
                        m = g * KT + 2 * n
                        dve.wait_ge(sg["f_lo"], EARLIER + m)
                        dve.wait_ge(sg["f_hi"], EARLIER + m)
                        tt_(tu[:, k, :], tt[:, k, :], tt[:, k, :], MUL).then_inc(sg["f_sq"], 1)
                        dve.wait_ge(sg["f_hi"], EARLIER + m + k + 1)
                        tt_(block_of(olo, n, k), tu[:, k, :], block_of(ohi, n, k).bitcast(F32), SUB).then_inc(sg["f_lo"], 1)

            def down(at, n, k):
                slab_lo(at, k)
                dve.wait_ge(sg["piece_used"], at.pieces_before(4 * k + 4))
                dve.wait_ge(sg[f"acc_free{at.bank(k)}"], at.drained(k))
                mb = block_of(mix, n, k)
                tt_(mb, mb, acc[at.bank(k)][:, 0:T], ADD).then_inc(sg[f"acc_free{at.bank(k)}"], 1)

            with dve.Fori(0, FG - 1) as g:
                up(g)
                with dve.Fori(0, KT // 2) as n:
                    for k in range(2):
                        down(At(S_FF, n + g * KT + KT // 2, 2), n, k)
            up(FG - 1)

            def last_down(n):
                if not (isinstance(n, int) and n == 0):
                    add_pair(2 * KT, n - 1)
                for k in range(2):
                    down(At(S_FF, n + FG * KT - KT // 2, 2), n, k)

            repeat(dve, last_down, KT // 2)
            add_pair(2 * KT, KT // 2 - 1)
            dve.wait_ge(sg["w_rs"], 3)

            def result_rows(n):
                for k in range(2):
                    dve.wait_ge(sg["w_h"], KT + 2 * n)
                    tt_(tin[:, k, 0, :], block_of(mix, n, k), trs[:, :], MUL).then_inc(sg["w_t1"], 1)
                for k in range(2):
                    m = 2 * n + k
                    dve.wait_ge(sg["y_turned"], 2 * n)
                    dve.wait_ge(sg["w_t1"], EARLIER + 2 * KT + m + 1)
                    ip, is_ = halves(tin[:, k, 0, :])
                    stt(halves(tu[:, k, :])[0], ip, mod_of(5, m)[:, 0:1], halves(block_of(res, n, k))[0], MUL, ADD)
                    tt_(is_, is_, wide(mod_of(5, m)), MUL).then_inc(sg["w_t2"], 1)
                for k in range(2):
                    m = 2 * n + k
                    dve.wait_ge(sg["w_t2"], 2 * KT + m + 1)
                    tt_(halves(tu[:, k, :])[1], halves(tin[:, k, 0, :])[1], halves(block_of(res, n, k))[1],
                        ADD).then_inc(sg["w_h"], 1)

            repeat(dve, result_rows, KT // 2)

        @block.gpsimd
        def _(pool):
            pt, ps = nc.gpsimd.tensor_tensor, nc.gpsimd.tensor_scalar
            MUL, SUB = ALU.mult, ALU.subtract
            steps = [0]

            def step(ins):
                steps[0] += 1
                ins.then_inc(sg["const_step"], 1)
                pool.wait_ge(sg["const_step"], steps[0])

            def keep(view, pattern, base, by_row):
                step(nc.gpsimd.affine_select(out=view, in_=view, compare_op=ALU.is_ge, fill=0.0, base=base,
                                             pattern=pattern, channel_multiplier=by_row))

            pool.dma_start(bgc[GH:2 * GH, 0:1], dt_bias.rearrange("o h -> h o")).then_inc(sg["small_in"], 16)
            pool.dma_start(bgc[GH:2 * GH, 1:2], A_log.rearrange("o h -> h o")).then_inc(sg["small_in"], 16)
            nc.gpsimd.memset(eps[:, :], EPS)
            nc.gpsimd.memset(ident[:, :], 0.0)
            for t in (ones, hmask, smask, reset, cm32, cm4, cm64, m_incl, m_str, m_str_s):
                nc.gpsimd.memset(t[:, :], 1.0)
            step(nc.gpsimd.memset(levm[:, :, :], 1.0))
            step(nc.gpsimd.affine_select(out=ident[:, :], in_=ident[:, :], compare_op=ALU.not_equal, fill=1.0, base=0,
                                         pattern=[[-1, P]], channel_multiplier=1))
            nc.gpsimd.memset(reset[:, 0:TP].rearrange("p (c t) -> p c t", t=HC)[:, :, 0:1], 0.0)
            nc.gpsimd.memset(reset[:, TP:T].rearrange("p (c t) -> p c t", t=TS)[:, :, 0:1], 0.0)

            def chunked(t, c, m):
                return t[:, :].rearrange("p (a b) -> p a b", b=m)
            for t, n_, m in ((hmask, P // HC, HC), (smask, NB, TS), (m_incl, 2, GC)):
                keep(chunked(t, n_, m), [[-m, n_], [0, m]], 0, 1)
                keep(chunked(t, n_, m), [[m, n_], [1, m]], 0, -1)
            for t, n_, m in ((m_str, 2, GC), (m_str_s, NB, TS)):
                keep(chunked(t, n_, m), [[-m, n_], [-1, m]], -1, 1)
                keep(chunked(t, n_, m), [[m, n_], [0, m]], m - 1, -1)
            for t, n_, m in ((cm32, P // HC, HC), (cm4, NB, TS), (cm64, 2, GC)):
                keep(t[:, :], [[-m, n_]], 0, 1)
                keep(t[:, :], [[m, n_]], m - 1, -1)
            for l in range(LEV):
                b = 1 << l
                n_ = P // (2 * b)
                v = levm[:, l, :].rearrange("p (k s) -> p k s", s=2 * b)
                keep(v, [[-2 * b, n_], [0, 2 * b]], -b, 1)
                keep(v, [[2 * b, n_], [0, 2 * b]], 2 * b - 1, -1)
                keep(v, [[0, n_], [-1, 2 * b]], b - 1, 0)
            nc.gpsimd.memset(eps[:, :], EPS).then_inc(sg["consts_made"], 1)

            def row(t, i):
                return t[i] if isinstance(i, int) else t[bass.ds(i, 1)].squeeze(0)

            def load_state(i):
                pool.wait_ge(sg["h_new"], 8 * i)
                pool.wait_ge(sg["h_o"], i)
                pool.dma_start(hS0[:, :, :], head_of(state_hgrn, i)).then_inc(sg["h_s0"], 16)

            def head_of(t, i):
                v = t[0].rearrange("b h d v -> d b h v")
                return v[:, :, i, :] if isinstance(i, int) else v[:, :, bass.ds(i, 1), :].squeeze(2)

            def spread(n):
                pool.wait_ge(sg["h_tok"], n + 1)
                pool.wait_ge(sg["h_ds"], n)
                for a in range(2):
                    pt(hiX[:, a], htok[:, 2 + a, :].unsqueeze(1).to_broadcast([P, P // HC, P]),
                       cm32[:, :].unsqueeze(2).to_broadcast([P, P // HC, P]), MUL)
                pt(hiXs[0:NS, :, :], htoks[0:NS, 1, :].unsqueeze(1).to_broadcast([NS, NB, P]),
                   cm4[:, :].unsqueeze(2).to_broadcast([NS, NB, P]), MUL).then_inc(sg["h_spread"], 1)

            def decayed(i):
                pool.wait_ge(sg["h_e"], i + 1)
                pool.wait_ge(sg["h_k"], i + 1)
                pool.wait_ge(sg["h_o"], i)
                pt(hX[:, 2, :], hq[:, :], hE[:, 2, :], MUL)
                pt(hX[:, 3, :], hk[:, :], hE[:, 3, :], MUL).then_inc(sg["h_decayed_p"], 1)

            def store(n):
                pool.wait_ge(sg["h_new"], 8 * (n + 1))
                out = hg_prompt[0, 0].rearrange("h d v -> d h v")
                out = out[:, n, :] if isinstance(n, int) else out[:, bass.ds(n, 1), :].squeeze(1)
                pool.dma_start(out, hS[:, NHC - 1, :]).then_inc(sg["h_stored"], 16)
                pool.dma_start(head_of(hg_sample, n), hSn[:, :, :]).then_inc(sg["h_stored"], 16)

            pool.wait_ge(sg["chunk_exp"], 1)
            pool.wait_ge(sg["tab_made"], 2)
            load_state(0)
            decayed(0)
            def hgrn(n):
                spread(n)
                store(n)
                load_state(n + 1)
                decayed(n + 1)
            repeat(pool, hgrn, HH - 1)
            spread(HH - 1)
            store(HH - 1)

            def scratch(t, j):
                return t[j] if isinstance(j, int) else t[bass.ds(j, 1)].squeeze(0)

            def save(t, j, k):
                pool.dma_start(scratch(t, j), pb[:, k, :]).then_inc(sg[f"t_stored{k}"], 16)

            def saved(blocks):
                for k in range(2):
                    pool.wait_ge(sg[f"t_stored{k}"], 8 * blocks)

            with pool.Fori(0, KT // 2) as n:
                for k in range(2):
                    pool.wait_ge(sg["t_out"], 2 * n + k + 1)
                    save(gate_d, 2 * n + k, k)
            saved(KT)
            def load_gate(j, k):
                pool.dma_start(pa[:, k, :], scratch(gate_d, j)).then_inc(sg[f"t_in{k}"], 16)

            for k in range(2):
                pool.wait_ge(sg[f"acc_free{At(S_WA).bank(k)}"], At(S_WA).drained(k))
                load_gate(k, k)
            with pool.Fori(1, KT // 2) as n:
                at = At(S_WA, n, 2)
                for k in range(2):
                    pool.wait_ge(sg[f"acc_free{at.bank(k)}"], at.drained(k))
                    save(merged_d, 2 * n - 2 + k, k)
                    load_gate(2 * n + k, k)
            for k in range(2):
                at = At(S_WA + KT - 2)
                pool.wait_ge(sg[f"acc_free{at.bank(k)}"], at.drained(k) + 1)
                save(merged_d, KT - 2 + k, k)

            cols = ((0, 1, 1), (GJ, 1, 1), (2 * GJ, 2, 2))

            def conv_cols(t, j, c):
                first, mul, size = cols[c]
                v = t.rearrange("r (c p) -> r c p", p=P)
                return v[:, first + mul * j:first + mul * j + size, :] if isinstance(j, int) else \
                    v[:, bass.ds(first + mul * j, size), :]

            places = (slice(0, 1), slice(1, 2), slice(2, 4))

            def load_cache(j):
                for c in range(3):
                    pool.dma_start(gcc[:, places[c], :], conv_cols(cache_conv[0].rearrange("b s c -> (b s) c"), j, c)
                                   ).then_inc(sg["g_cc"], 16)

            def store_tail(j):
                pool.wait_ge(sg["g_tail_out"], j + 1)
                for c in range(3):
                    pool.dma_start(conv_cols(conv_prompt[0, 0], j, c), gto[0:3, places[c], :]).then_inc(sg["g_tail_stored"], 16)
                    pool.dma_start(conv_cols(conv_sample[0].rearrange("b s c -> (b s) c"), j, c), gto[3:27, places[c], :]
                                   ).then_inc(sg["g_tail_stored"], 16)

            def pair_of(t, j):
                v = t[0].rearrange("b (j e) d v -> j e d b v", e=2)
                return v[j] if isinstance(j, int) else v[bass.ds(j, 1)].squeeze(0)

            def load_delta(j):
                for e in range(2):
                    pool.dma_start(gS0[:, e], pair_of(state_gdn, j)[e]).then_inc(sg["g_s0"], 16)

            def own(j):
                pool.wait_ge(sg["g_sc"], EARLIER + j + 1)
                pool.wait_ge(sg["g_attn"], j)
                pool.wait_ge(sg["g_a"], EARLIER + j)
                def g_of(rows_, a):
                    return gsc[0:rows_, :, 12 + a:13 + a].to_broadcast([rows_, 2, rows_])
                for a in range(2):
                    pt(gGR[:, a, 0], m_str[:, :].unsqueeze(1).to_broadcast([P, 2, P]), g_of(P, a), MUL)
                    pt(gGR[:, a, 1], m_incl[:, :].unsqueeze(1).to_broadcast([P, 2, P]), g_of(P, a), MUL)
                pt(gGRs[:, 0], m_str_s[:, :].unsqueeze(1).to_broadcast([NS, 2, NS]), g_of(NS, 2), MUL)
                last = pt(gGRs[:, 1], smask[:, :].unsqueeze(1).to_broadcast([NS, 2, NS]), g_of(NS, 2), MUL)
                last.then_inc(sg["g_gr"], 1)
                pool.wait_ge(sg["g_tokqk"], EARLIER + j + 1)
                pool.wait_ge(sg["g_o"], j)
                pool.wait_ge(sg["g_ds"], 4 * j)
                for out, src, col in ((gbek, gtk, 9), (gkl, gtk, 6)):
                    for a in range(3):
                        m = P if a < 2 else NS
                        last = pt(out[0:m, a], src[0:m, a, :].unsqueeze(1).to_broadcast([m, 2, P]),
                                  gsc[0:m, :, col + a:col + a + 1].to_broadcast([m, 2, P]), MUL)
                last.then_inc(sg["g_tokd"], 1)

            def level(n, l):
                if l == 0:
                    pool.wait_ge(sg["g_a"], EARLIER + n + 1)
                    pool.wait_ge(sg["g_pu"], 5 * n)
                if l == 2:
                    pool.wait_ge(sg["g_l1"], EARLIER + n + 1)
                    pool.wait_ge(sg["g_t1"], n + 1)
                if l > 2:
                    pool.wait_ge(sg["g_pu"], 5 * n + l - 2)
                last = pt(glev[:, l % 2], gA[:, :, :], levm[:, l, :].unsqueeze(1).to_broadcast([P, 4, P]), MUL)
                if l < 2:
                    last = pt(glevs[:, l], gAs[:, :, :], levm[0:NS, l, 0:NS].unsqueeze(1).to_broadcast([NS, 2, NS]), MUL)
                last.then_inc(sg["g_lev"], 1)

            def prev(n, between=None):
                level(n, 0)
                level(n, 1)
                pool.wait_ge(sg["g_lev"], 6 * n + 1)
                pool.wait_ge(sg["g_tnew"], 4 * n)
                pt(gT[:, :, :], ident[:, :].unsqueeze(1).to_broadcast([P, 4, P]), glev[:, 0], SUB)
                pt(gTs[:, :, :], ident[0:NS, 0:NS].unsqueeze(1).to_broadcast([NS, 2, NS]), glevs[:, 0], SUB).then_inc(sg["g_t1"], 1)
                level(n, 2)
                pool.wait_ge(sg["g_qkm"], EARLIER + n + 1)
                pool.wait_ge(sg["g_o"], n)
                for a in range(2):
                    pt(gat[:, a], gGR[:, a, 1], gQKm[:, a, :].unsqueeze(1).to_broadcast([P, 2, P]), MUL)
                pt(gats[:, :, :], gGRs[:, 1], gQKms[:, :].unsqueeze(1).to_broadcast([NS, 2, NS]), MUL).then_inc(sg["g_attn"], 1)
                level(n, 3)
                level(n, 4)
                store_tail(n)
                if not (isinstance(n, int) and n == 0):
                    store_prompt(n - 1)
                pool.wait_ge(sg["g_sw"], n + 1)
                for e in range(2):
                    pt(gS0[:, e], gS0[:, e], gsc[:, e, 19:27].unsqueeze(2).to_broadcast([P, NB, P]), MUL).then_inc(sg["g_sdec"], 1)
                level(n, 5)
                pool.wait_ge(sg["g_vns"], n + 1)
                for e in range(2):
                    pool.wait_ge(sg["g_dss"], 2 * n + e)
                    pt(gvX[0:NS, :, :], gvns[:, e, :].unsqueeze(1).to_broadcast([NS, NB, P]),
                       cm4[:, :].unsqueeze(2).to_broadcast([NS, NB, P]), MUL).then_inc(sg["g_vx"], 1)
                if between:
                    between()
                pool.wait_ge(sg["g_snew"], 2 * n + 2)
                for e in range(2):
                    pool.dma_start(pair_of(gdn_sample, n)[e], gS0[:, e]).then_inc(sg["g_stored_s"], 16)

            def store_prompt(n):
                pool.wait_ge(sg["g_st"], 4 * (n + 1))
                out = gdn_prompt[0, 0].rearrange("(j e) d v -> j d e v", e=2)
                pool.dma_start(row(out, n), gS[:, NGC - 1]).then_inc(sg["g_stored"], 16)

            pool.wait_ge(sg["g_zero"], 1)
            load_cache(0)
            load_delta(0)
            own(0)
            pool.wait_ge(sg["g_halo_turned"], 1)
            load_cache(1)

            def delta(n, cache):
                prev(n)
                pool.wait_ge(sg["g_stored_s"], 32 * (n + 1))
                load_delta(n + 1)
                own(n + 1)
                if cache:
                    pool.wait_ge(sg["g_halo_turned"], n + 2)
                    load_cache(n + 2)

            def delta_and_cache(n):
                delta(n, True)
            repeat(pool, delta_and_cache, HALF)
            with pool.Fori(0, KT // 2) as n:
                at = At(S_WB1, n, 2)
                for k in range(2):
                    pool.wait_ge(sg[f"acc_free{at.bank(k)}"], at.drained(k) + 1)
                    save(half_d, 2 * n + k, k)
            with pool.Fori(HALF, GJ - 2) as n:
                delta(n, True)
            delta(GJ - 2, False)

            def save_gates(first, count):
                for k in range(first, first + count):
                    pool.wait_ge(sg["t_out"], KT + k + 1)
                    save(gate_d, k, k % 2)
            prev(GJ - 1, lambda: save_gates(0, 2))
            save_gates(2, 2)
            store_prompt(GJ - 1)
            save_gates(4, 2)
            with pool.Fori(3, KT // 2) as n:
                for k in range(2):
                    pool.wait_ge(sg["t_out"], KT + 2 * n + k + 1)
                    save(gate_d, 2 * n + k, k)
            saved(4 * KT)
            pool.wait_ge(sg["g_stored"], 16 * GJ)
            pool.wait_ge(sg["g_stored_s"], 32 * GJ)
            pool.wait_ge(sg["g_olo"], GJ)

            def load_branches(n):
                pool.wait_ge(sg["t_s3"], 2 * n)
                for k in range(2):
                    for a, t in enumerate((merged_d, half_d, gate_d)):
                        pool.dma_start(tin[:, k, a, :], scratch(t, 2 * n + k)).then_inc(sg[f"t_in{k}"], 16)
            repeat(pool, load_branches, KT // 2)
            pool.wait_ge(sg["piece_used"], At(S_WB2).pieces_before(0))
            pool.dma_start(xin[:, 0:2, :], x_prompt[0].rearrange("(a p) d -> p a d", p=P)).then_inc(sg["w_xin"], 16)
            pool.dma_start(xin[0:NS, 2, :], x_sample.rearrange("b t d -> (b t) d")).then_inc(sg["w_xin"], 16)


INPUTS = ("x_prompt", "x_sample", "state_hgrn", "state_gdn", "cache_conv", "c_prompt", "c_sample", "lb_logits",
          "w_ada", "b_ada", "norm_g", "w_in", "conv_w", "A_log", "dt_bias", "hg_norm_g", "gdn_norm_g",
          "w_out_hg", "w_out_gdn", "w_o", "w_up", "w_down")


def kernel(**inputs):
    import numpy as np
    import concourse.bacc as bacc
    from concourse.bass_utils import run_bass_kernel_spmd

    nc = bacc.Bacc("TRN2", target_bir_lowering=False, num_devices=1)
    arrays, args = {}, []
    for name in INPUTS:
        a = np.ascontiguousarray(inputs[name])
        arrays[f"in_{name}"] = a
        args.append(nc.dram_tensor(f"in_{name}", a.shape, mybir.dt.from_np(a.dtype), kind="ExternalInput").ap())
    depth, batch = inputs["w_in"].shape[0], inputs["x_prompt"].shape[0]
    conv, hg, gdn = inputs["cache_conv"].shape, inputs["state_hgrn"].shape, inputs["state_gdn"].shape
    shapes = (inputs["x_prompt"].shape, inputs["x_sample"].shape, (depth, batch, *hg[2:]), (depth, batch, *gdn[2:]),
              (depth, batch, *conv[2:]), hg, gdn, conv)
    for i, shape in enumerate(shapes):
        args.append(nc.dram_tensor(f"out_{i}", shape, F32, kind="ExternalOutput").ap())
    hybrid_layer(nc, *args)
    r = run_bass_kernel_spmd(nc, [arrays], core_ids=[0])
    return tuple(r.results[0][f"out_{i}"] for i in range(len(shapes)))
```
